# Optimizing a Trainium2 kernel written in Bass

```python
import jax
import jax.numpy as jnp
from jax import lax
import numpy as np

D_MODEL = 1024
BATCH = 1
SEQ = 1024
DEPTH = 1

MIX_WIDTH = D_MODEL
GLA_WIDTH = MIX_WIDTH // 2
POOL_WIDTH = MIX_WIDTH - GLA_WIDTH
GLA_HEADS = 4
GLA_DV = GLA_WIDTH // GLA_HEADS
GLA_DK = GLA_DV // 2
GLA_KEY_WIDTH = GLA_HEADS * GLA_DK
GLA_GATE_RANK = 16
GLA_TAU = 16.0
GLA_CHUNK = 64
POOL_WINDOWS = (2, 4, 8, 16)
POOL_GROUPS = len(POOL_WINDOWS)
POOL_GROUP_WIDTH = POOL_WIDTH // POOL_GROUPS
PEER_HEADS = 8
PEER_NKEYS = 128
PEER_EXPERTS = PEER_NKEYS * PEER_NKEYS
PEER_QDIM = 256
PEER_HALF = PEER_QDIM // 2
PEER_TOPK = 16
PEER_TOKEN_BLOCK = 128
N_MOD = 6
EPS = 1e-6

IN_SIZES = (GLA_KEY_WIDTH, GLA_KEY_WIDTH, GLA_WIDTH, GLA_WIDTH, GLA_GATE_RANK, GLA_GATE_RANK, POOL_WIDTH)
IN_COLS = sum(IN_SIZES)
IN_SPLITS = tuple(int(s) for s in np.cumsum(IN_SIZES)[:-1])

kernel_name = "hybrid_gla_pool_peer_encoder_layer"

def rmsnorm(x, g):
    xf = x.astype(jnp.float32)
    y = xf * lax.rsqrt(jnp.mean(xf * xf, axis=-1, keepdims=True) + EPS)
    return (y * g.astype(jnp.float32)).astype(x.dtype)

def gla_chunked(q, k, v, log_a, strict):
    B, H, S, dk = q.shape
    dv = v.shape[-1]
    C = GLA_CHUNK
    n = S // C
    qc = q.reshape(B, H, n, C, dk).astype(jnp.float32)
    kc = k.reshape(B, H, n, C, dk).astype(jnp.float32)
    vc = v.reshape(B, H, n, C, dv).astype(jnp.float32)
    b = jnp.cumsum(log_a.reshape(B, H, n, C, dk), axis=3)
    b_last = b[:, :, :, -1:, :]
    q_dec = qc * jnp.exp(b)
    k_inv = kc * jnp.exp(-b)
    k_end = kc * jnp.exp(b_last - b)
    scores = jnp.einsum('bhnid,bhnjd->bhnij', q_dec, k_inv)
    mask = jnp.tril(jnp.ones((C, C), dtype=bool), k=-1 if strict else 0)
    scores = jnp.where(mask, scores, 0.0)
    o_intra = jnp.einsum('bhnij,bhnjv->bhniv', scores, vc)
    u = jnp.einsum('bhnjd,bhnjv->bhndv', k_end, vc)
    gamma = jnp.exp(b_last[:, :, :, 0, :])

    def step(state, inp):
        g_n, u_n = inp
        return g_n[..., None] * state + u_n, state

    init = jnp.zeros((B, H, dk, dv), jnp.float32)
    _, s_prev = lax.scan(step, init, (jnp.moveaxis(gamma, 2, 0), jnp.moveaxis(u, 2, 0)))
    s_prev = jnp.moveaxis(s_prev, 0, 2)
    o_inter = jnp.einsum('bhnid,bhndv->bhniv', q_dec, s_prev)
    return (o_intra + o_inter).reshape(B, H, S, dv)

def gla_group(q, k, v, r, af, ab, w_af, b_af, w_ab, b_ab, g_head):
    B, S, _ = q.shape

    def heads(t, d):
        return t.reshape(B, S, GLA_HEADS, d).transpose(0, 2, 1, 3)

    qh = heads(q, GLA_DK) * (GLA_DK ** -0.5)
    kh = heads(k, GLA_DK)
    vh = heads(v, GLA_DV)
    log_af = jax.nn.log_sigmoid((af @ w_af + b_af).astype(jnp.float32)) / GLA_TAU
    log_ab = jax.nn.log_sigmoid((ab @ w_ab + b_ab).astype(jnp.float32)) / GLA_TAU
    o_f = gla_chunked(qh, kh, vh, heads(log_af, GLA_DK), strict=False)
    o_b = jnp.flip(gla_chunked(jnp.flip(qh, 2), jnp.flip(kh, 2), jnp.flip(vh, 2),
                               jnp.flip(heads(log_ab, GLA_DK), 2), strict=True), 2)
    o = jnp.transpose(o_f + o_b, (0, 2, 1, 3)).astype(q.dtype)
    o = rmsnorm(o, g_head.reshape(GLA_HEADS, GLA_DV)).reshape(B, S, GLA_WIDTH)
    return o * jax.nn.silu(r)

def pool_group(p, w_pool, pool_scale):
    B, S, W = p.shape
    pf = p.astype(jnp.float32)
    cs = jnp.concatenate([jnp.zeros((B, 1, W), jnp.float32), jnp.cumsum(pf, axis=1)], axis=1)
    pos = jnp.arange(S)
    outs = []
    for gi, w in enumerate(POOL_WINDOWS):
        sl = slice(gi * POOL_GROUP_WIDTH, (gi + 1) * POOL_GROUP_WIDTH)
        lo = jnp.clip(pos - w // 2, 0, S)
        hi = jnp.clip(pos + w // 2, 0, S)
        seg = cs[:, :, sl]
        total = seg[:, hi] - seg[:, lo]
        count = (hi - lo).astype(jnp.float32)[None, :, None]
        outs.append(total / count - pf[:, :, sl])
    pooled = jnp.stack(outs, axis=2).astype(p.dtype)
    y = jnp.einsum('bsgc,gcd->bsgd', pooled, w_pool)
    return y.reshape(B, S, POOL_WIDTH) * pool_scale

def peer_ffn(h, w_q, sub_keys, u_tab, v_tab):
    B, S, D = h.shape
    T = B * S
    K = PEER_TOPK
    ht = h.reshape(T, D)
    q = (ht @ w_q).reshape(T, PEER_HEADS, 2, PEER_HALF)
    s = jnp.einsum('thpd,hpnd->thpn', q, sub_keys).astype(jnp.float32)
    vals, idx = lax.top_k(s, K)
    cand = vals[:, :, 0, :, None] + vals[:, :, 1, None, :]
    top_s, top_pos = lax.top_k(cand.reshape(T, PEER_HEADS, K * K), K)
    i1 = jnp.take_along_axis(idx[:, :, 0], top_pos // K, axis=-1)
    i2 = jnp.take_along_axis(idx[:, :, 1], top_pos % K, axis=-1)
    experts = (i1 * PEER_NKEYS + i2).reshape(T, PEER_HEADS * K)
    gates = jax.nn.softmax(top_s, axis=-1).reshape(T, PEER_HEADS * K)
    nb = T // PEER_TOKEN_BLOCK

    def block(args):
        xb, eb, gb = args
        a = jax.nn.gelu(jnp.einsum('td,ted->te', xb, u_tab[eb]), approximate=False)
        coeff = (gb * a.astype(jnp.float32)).astype(xb.dtype)
        return jnp.einsum('te,ted->td', coeff, v_tab[eb])

    y = lax.map(block, (ht.reshape(nb, PEER_TOKEN_BLOCK, D),
                        experts.reshape(nb, PEER_TOKEN_BLOCK, PEER_HEADS * K),
                        gates.reshape(nb, PEER_TOKEN_BLOCK, PEER_HEADS * K)))
    return y.reshape(B, S, D)

def setup_inputs(seed: int = 0) -> dict:
    key = jax.random.key(seed)
    ks = jax.random.split(key, 24)
    L, D = DEPTH, D_MODEL
    f32 = jnp.float32

    def nrm(k, shape, scale):
        return jax.random.normal(k, shape, f32) * scale

    def gain(k, shape):
        return 1.0 + 0.01 * jax.random.normal(k, shape, f32)

    return {
        "x": jax.random.normal(ks[0], (BATCH, SEQ, D), f32),
        "c": jax.random.normal(ks[1], (BATCH, D), f32),
        "w_mod": nrm(ks[2], (L, D, N_MOD * D), 0.5 * D ** -0.5),
        "b_mod": nrm(ks[3], (L, N_MOD * D), 0.01),
        "g_pre_mix": gain(ks[4], (L, D)),
        "g_post_mix": gain(ks[5], (L, D)),
        "w_in": nrm(ks[6], (L, D, IN_COLS), D ** -0.5),
        "w_alpha_f": nrm(ks[7], (L, GLA_GATE_RANK, GLA_KEY_WIDTH), GLA_GATE_RANK ** -0.5),
        "b_alpha_f": nrm(ks[8], (L, GLA_KEY_WIDTH), 0.01),
        "w_alpha_b": nrm(ks[9], (L, GLA_GATE_RANK, GLA_KEY_WIDTH), GLA_GATE_RANK ** -0.5),
        "b_alpha_b": nrm(ks[10], (L, GLA_KEY_WIDTH), 0.01),
        "g_gla_head": gain(ks[11], (L, GLA_WIDTH)),
        "w_pool": nrm(ks[12], (L, POOL_GROUPS, POOL_GROUP_WIDTH, POOL_GROUP_WIDTH), POOL_GROUP_WIDTH ** -0.5),
        "pool_scale": gain(ks[13], (L, POOL_WIDTH)),
        "w_out": nrm(ks[14], (L, MIX_WIDTH, D), MIX_WIDTH ** -0.5),
        "g_pre_ffn": gain(ks[15], (L, D)),
        "g_post_ffn": gain(ks[16], (L, D)),
        "w_peer_q": nrm(ks[17], (L, D, PEER_HEADS * PEER_QDIM), D ** -0.5),
        "peer_sub_keys": nrm(ks[18], (L, PEER_HEADS, 2, PEER_NKEYS, PEER_HALF), PEER_HALF ** -0.5),
        "peer_u": nrm(ks[19], (L, PEER_EXPERTS, D), D ** -0.5),
        "peer_v": nrm(ks[20], (L, PEER_EXPERTS, D), PEER_HEADS ** -0.5),
    }

def reference(x, c, w_mod, b_mod, g_pre_mix, g_post_mix, w_in, w_alpha_f, b_alpha_f, w_alpha_b, b_alpha_b,
              g_gla_head, w_pool, pool_scale, w_out, g_pre_ffn, g_post_ffn, w_peer_q, peer_sub_keys,
              peer_u, peer_v):
    cond = jax.nn.silu(c)
    for l in range(DEPTH):
        mod = cond @ w_mod[l] + b_mod[l]
        sh1, sc1, gt1, sh2, sc2, gt2 = [m[:, None, :] for m in jnp.split(mod, N_MOD, axis=-1)]

        h = rmsnorm(x, g_pre_mix[l]) * (1 + sc1) + sh1
        z = h @ w_in[l]
        q, k, v, r, af, ab, p = jnp.split(z, IN_SPLITS, axis=-1)
        o_gla = gla_group(q, k, v, r, af, ab, w_alpha_f[l], b_alpha_f[l], w_alpha_b[l], b_alpha_b[l],
                          g_gla_head[l])
        o_pool = pool_group(p, w_pool[l], pool_scale[l])
        mix = jnp.concatenate([o_gla.astype(x.dtype), o_pool.astype(x.dtype)], axis=-1) @ w_out[l]
        x = x + gt1 * rmsnorm(mix, g_post_mix[l])

        h2 = rmsnorm(x, g_pre_ffn[l]) * (1 + sc2) + sh2
        y = peer_ffn(h2, w_peer_q[l], peer_sub_keys[l], peer_u[l], peer_v[l])
        x = x + gt2 * rmsnorm(y, g_post_ffn[l])
    return x


_drawn_inputs = setup_inputs


def setup_inputs(seed=0):
    import zlib

    import numpy as np

    out = dict(_drawn_inputs(seed))
    spreads = {}
    factors = {'g_pre_mix': 2.835,
     'g_post_mix': 3.119,
     'b_alpha_f': 7.443,
     'b_alpha_b': 6.528,
     'g_gla_head': 4.303,
     'pool_scale': 3.539,
     'g_post_ffn': 8.0}
    for name, (base, spread) in spreads.items():
        noise = np.random.default_rng([zlib.crc32(name.encode()), seed]).standard_normal(out[name].shape)
        drawn = base * np.exp(spread * noise) if base else spread * noise
        out[name] = jnp.asarray(drawn.astype(out[name].dtype))
    for name, factor in factors.items():
        out[name] = (out[name] * factor).astype(out[name].dtype)
    return out
```

```python
from contextlib import ExitStack

import numpy as np

import concourse.bass as bass
from concourse import mybir

F32 = mybir.dt.float32
F32R = mybir.dt.float32r
U32 = mybir.dt.uint32
ALU = mybir.AluOpType
ACT = mybir.ActivationFunctionType
AX = mybir.AxisListType.X

P = 128
D = 1024
S = 1024
KC = D // P
TT = S // P
HALF = 512
N_MOD = 6
EPS = 1e-6

GLA_HEADS, GLA_DK, GLA_DV = 4, 64, 128
PAIRS = GLA_HEADS // 2
CHUNK = 64
NCHUNK = S // CHUNK
TAU = 16.0
RANK = 16
WINDOWS = (2, 4, 8, 16)
PAD = WINDOWS[-1] // 2

HEADS, NKEYS, TOPK = 8, 128, 16
QTILES = 2 * HEADS
TOK = 16
STEPS = TT * HEADS
LOWEST = -3.0e38

VECS = [("c", KC), ("b_mod", N_MOD * KC), ("g_pre_mix", KC), ("g_post_mix", KC), ("b_alpha_f", PAIRS),
        ("b_alpha_b", PAIRS), ("g_gla_head", GLA_HEADS), ("pool_scale", 4), ("g_pre_ffn", KC), ("g_post_ffn", KC)]
VCOL = {}
for _name, _n in VECS:
    VCOL[_name] = (sum(n for _, n in VCOL.values()), _n)
NVEC = sum(n for _, n in VECS)

MOD_COLS = 256
MOD_LOADS = N_MOD * D // MOD_COLS
MOD_RING = 3
QKRP = 12


def split_hi(act, hi, raw):
    return act.activation(hi, raw, ACT.Copy)


def split_lo(dve, lo, raw, hi):
    return dve.tensor_tensor(lo, raw, hi.bitcast(F32), ALU.subtract)


def tile_product(pe, acc, w_hi, w_lo, a_hi, a_lo):
    for k in range(KC):
        wh, wl = w_hi[:, k * P:(k + 1) * P], w_lo[:, k * P:(k + 1) * P]
        for w, a, first, last in ((wh, a_hi, k == 0, False), (wh, a_lo, False, False), (wl, a_hi, False, k == KC - 1)):
            for half in range(2):
                cols = slice(half * HALF, (half + 1) * HALF)
                done = pe.matmul(acc[:, cols], w, a[:, k, cols], start=first, stop=last)
    return done


class Layer:

    def __init__(self, nc, t_in, out):
        self.nc, self.i, self.out = nc, t_in, out


def layer(nc, t_in, out):
    g = Layer(nc, t_in, out)
    with ExitStack() as ctx:
        def sem(name):
            return ctx.enter_context(nc.semaphore(name))

        def small(name, shape, dt=F32):
            return ctx.enter_context(nc.sbuf_tensor(name, shape, dt))

        g.sem = sem
        g.x1_d = nc.dram_tensor("x1_d", (TT, P, D), F32, kind="Internal").ap()
        g.s_d = nc.dram_tensor("s_d", (TT, P, QTILES, NKEYS), F32, kind="Internal").ap()
        g.act_d = nc.dram_tensor("act_d", (NKEYS, P, S), F32, kind="Internal").ap()
        g.gate_d = nc.dram_tensor("gate_d", (NKEYS, P, S), F32, kind="Internal").ap()
        g.consts = small("consts", [P, 4 * P])
        g.ident, g.iota = g.consts[:, 0:P], g.consts[:, P:2 * P]
        g.mask_f, g.mask_b = g.consts[:, 2 * P:3 * P], g.consts[:, 3 * P:4 * P]
        g.vecs = small("vecs", [P, NVEC])
        g.vec = lambda name: g.vecs[:, VCOL[name][0]:VCOL[name][0] + VCOL[name][1]]
        g.mod = small("mod", [P, N_MOD * KC])
        g.scale1 = small("scale1", [P, KC])
        g.scale2 = small("scale2", [P, KC])
        g.gate_cols = small("gate_cols", [P, 2 * KC])
        g.gate_rows = small("gate_rows", [P, 2, D])
        g.ssq = small("ssq", [P, 4 * TT])
        g.rstd = small("rstd", [P, 4 * TT])
        g.eps = small("eps", [P, 1])
        base = nc.sbuf_base
        base = (base() if callable(base) else base)
        base = (base + 1023) // 1024 * 1024
        g.at = lambda name, kb, shape, dt=F32: nc.alloc_sbuf_tensor_at(name, shape, dt, offset=base + int(kb * 1024))
        g.a_hi = g.at("a_hi", 128, [P, KC, S], F32R)
        g.a_lo = g.at("a_lo", 160, [P, KC, S], F32R)

        modulation(g)
        projections(g)
        decays(g)
        attention(g)
        mix_out(g)
        second_norm(g)
        retrieval_scores(g)
        expert_sweep_1(g)
        expert_sweep_2(g)


def modulate_transposed(g, tag, xn, hf, tp, scale, shift, sems, act, dve, pe):
    s_tp, s_hf, s_hi, s_lo = sems
    if pe is not None:
        for k in range(KC):
            if k >= 2:
                pe.wait_ge(s_hf, k - 1)
            for t in range(TT):
                last = pe.transpose(tp[k % 2][:, t * P:(t + 1) * P], xn[:, t, k * P:(k + 1) * P], g.ident)
            last.then_inc(s_tp, 1)
    if act is not None:
        for k in range(KC):
            act.wait_ge(s_tp, k + 1)
            if k >= 2:
                act.wait_ge(s_lo, k - 1)
            act.activation(hf[k % 2][:], tp[k % 2][:], ACT.Identity, bias=shift[:, k:k + 1],
                           scale=scale[:, k:k + 1]).then_inc(s_hf, 1)
    if dve is not None:
        for k in range(KC):
            dve.wait_ge(s_hf, k + 1)
            dve.tensor_copy(g.a_hi[:, k, :], hf[k % 2][:]).then_inc(s_hi, 1)
            dve.wait_ge(s_hi, k + 1)
            split_lo(dve, g.a_lo[:, k, :], hf[k % 2][:], g.a_hi[:, k, :]).then_inc(s_lo, 1)


def modulation(g):
    nc, i, sem = g.nc, g.i, g.sem
    x = g.at("x", 0, [P, TT, D])
    w_mod = [g.at(f"w_mod{s}", 32 + 8 * s, [P, KC, MOD_COLS]) for s in range(MOD_RING)]
    hf = [g.at(f"hf{s}", 56 + 4 * s, [P, S]) for s in range(2)]
    junk = g.at("junk_a", 64, [P, D])
    spread = g.at("spread", 68, [P, 2 * KC, P])
    silu_c = g.at("silu_c", 76, [P, KC])
    consts_in, vecs_in = sem("consts_in"), sem("vecs_in")
    x_in = [sem(f"x_in{t}") for t in range(TT)]
    w_mod_in = [sem(f"w_mod_in{s}") for s in range(MOD_RING)]
    silu_ready, eps_ready, ssq_ready, root_ready, xn_ready = (sem(n) for n in (
        "silu_ready", "eps_ready", "ssq_ready", "root_ready", "xn_ready"))
    mod_done, cols_ready, spread_ready, rows_ps, rows_ready = (sem(n) for n in (
        "mod_done", "cols_ready", "spread_ready", "rows_ps", "rows_ready"))
    sems = tuple(sem(n) for n in ("tp_a", "hf_a", "hi_a", "lo_a"))
    with nc.psum_tensor("mod_ps", [P, HALF], F32) as mod_ps, \
            nc.psum_tensor("tp_a0", [P, S], F32) as tp0, nc.psum_tensor("tp_a1", [P, S], F32) as tp1, \
            nc.psum_tensor("rows", [P, S], F32) as rows, nc.Block() as block:
        tp = [tp0, tp1]
        per_load = MOD_COLS // P

        @block.sync
        def _(sp):
            sp.dma_start(g.vecs[:], i["vecs"]).then_inc(vecs_in, 16)
            sp.dma_start(g.consts[:], i["consts"]).then_inc(consts_in, 16)
            for s in range(MOD_RING):
                sp.dma_start(w_mod[s][:], i["w_mod"][s]).then_inc(w_mod_in[s], 16)
            for t in range(TT):
                sp.dma_start(x[:, t, :], i["x"][t * P:(t + 1) * P, :]).then_inc(x_in[t], 16)
            with sp.Fori(1, MOD_LOADS // MOD_RING) as r:
                for s in range(MOD_RING):
                    sp.wait_ge(mod_done, (r - 1) * MOD_RING + s + 1)
                    sp.dma_start(w_mod[s][:], i["w_mod"][r * MOD_RING + s]).then_inc(w_mod_in[s], 16)

        @block.scalar
        def _(act):
            act.wait_ge(vecs_in, 16)
            act.activation(silu_c[:], g.vec("c"), ACT.Silu).then_inc(silu_ready, 1)
            for t in range(TT):
                act.wait_ge(x_in[t], 16)
                if t:
                    act.wait_ge(ssq_ready, t)
                act.activation(junk[:], x[:, t, :], ACT.Square, accum_out=g.ssq[:, t:t + 1]).then_inc(ssq_ready, 1)
            act.wait_ge(ssq_ready, TT)
            act.wait_ge(eps_ready, 1)
            act.activation(g.rstd[:, 0:TT], g.ssq[:, 0:TT], ACT.Sqrt, scale=1.0 / D, bias=g.eps[:]).then_inc(root_ready, 1)
            act.wait_ge(cols_ready, 1)
            modulate_transposed(g, "a", x, hf, tp, g.scale1, g.mod[:, 0:KC], sems, act, None, None)

        @block.vector
        def _(dve):
            dve.memset(g.eps[:], EPS).then_inc(eps_ready, 1)
            dve.wait_ge(root_ready, 1)
            dve.reciprocal(g.rstd[:, 0:TT], g.rstd[:, 0:TT])
            dve.drain()
            for t in range(TT):
                last = dve.tensor_scalar(x[:, t, :], x[:, t, :], g.rstd[:, t:t + 1], None, ALU.mult)
            last.then_inc(xn_ready, 1)
            dve.wait_ge(vecs_in, 16)
            dve.wait_ge(mod_done, MOD_LOADS)
            dve.tensor_tensor(g.mod[:], mod_ps[:, 0:N_MOD * KC], g.vec("b_mod"), ALU.add)
            dve.drain()
            one = lambda out, m, gain: dve.scalar_tensor_tensor(out, g.mod[:, m * KC:(m + 1) * KC], 1.0, g.vec(gain),
                                                                 ALU.add, ALU.mult)
            one(g.scale1[:], 1, "g_pre_mix")
            one(g.scale2[:], 4, "g_pre_ffn").then_inc(cols_ready, 1)
            dve.tensor_tensor(g.gate_cols[:, 0:KC], g.mod[:, 2 * KC:3 * KC], g.vec("g_post_mix"), ALU.mult)
            dve.tensor_tensor(g.gate_cols[:, KC:], g.mod[:, 5 * KC:6 * KC], g.vec("g_post_ffn"), ALU.mult)
            dve.drain()
            dve.tensor_copy(spread[:], g.gate_cols[:].unsqueeze(2).to_broadcast([P, 2 * KC, P])).then_inc(spread_ready, 1)
            modulate_transposed(g, "a", x, hf, tp, None, None, sems, None, dve, None)
            for n in range(2):
                dve.wait_ge(rows_ps, n + 1)
                dve.tensor_copy(g.gate_rows[:, n, :], rows[:]).then_inc(rows_ready, 1)

        @block.tensor
        def _(pe):
            pe.wait_ge(silu_ready, 1)
            with pe.Fori(0, MOD_LOADS // MOD_RING) as r:
                for s in range(MOD_RING):
                    pe.wait_ge(w_mod_in[s], (r + 1) * 16)
                    for m in range(per_load):
                        col = (r * MOD_RING + s) * per_load + m
                        for k in range(KC):
                            last = pe.matmul(mod_ps[:, bass.ds(col, 1)], w_mod[s][:, k, m * P:(m + 1) * P],
                                             silu_c[:, k:k + 1], start=k == 0, stop=k == KC - 1)
                    last.then_inc(mod_done, 1)
            pe.wait_ge(consts_in, 16)
            pe.wait_ge(xn_ready, 1)
            modulate_transposed(g, "a", x, hf, tp, None, None, sems, None, None, pe)
            pe.wait_ge(spread_ready, 1)
            for n in range(2):
                if n:
                    pe.wait_ge(rows_ready, n)
                for k in range(KC):
                    last = pe.matmul(rows[:, k * P:(k + 1) * P], spread[:, n * KC + k, :], g.ident, start=True, stop=True)
                last.then_inc(rows_ps, 1)


def projections(g):
    nc, i, sem = g.nc, g.i, g.sem
    g.z = g.at("z", 0, [P, QKRP, S])
    g.za = g.at("za", 48, [P, S])
    g.v = g.at("v", 52, [P, TT, GLA_HEADS * GLA_DV])
    raw = [g.at(f"w_raw{s}", 68 + 4 * s, [P, D]) for s in range(2)]
    w_hi = [g.at(f"w_hi{s}", 76 + 4 * s, [P, D], F32R) for s in range(2)]
    w_lo = [g.at(f"w_lo{s}", 84 + 4 * s, [P, D], F32R) for s in range(2)]
    wv_hi = g.at("wv_hi", 92, [P, KC, HALF], F32R)
    wv_lo = g.at("wv_lo", 108, [P, KC, HALF], F32R)
    raw_in = [sem(f"w_raw_in{s}") for s in range(2)]
    hi_ready, lo_ready, tile_done, tile_out = (sem(n) for n in ("w_hi_ready", "w_lo_ready", "z_done", "z_out"))
    v_done, v_out = sem("v_done"), sem("v_out")
    VP = KC * HALF // D
    LOADS = QKRP + 2 * 1 + VP
    with nc.psum_tensor("acc_b0", [P, S], F32) as acc0, nc.psum_tensor("acc_b1", [P, S], F32) as acc1, nc.Block() as block:
        acc = [acc0, acc1]
        piece = lambda t, n: t[:, 2 * n:2 * n + 2, :].rearrange("p a b -> p (a b)")

        @block.sync
        def _(sp):
            for n in range(2):
                sp.dma_start(raw[n][:], i["w_qkrp"][n]).then_inc(raw_in[n], 16)
            with sp.Fori(1, QKRP // 2) as r:
                for s in range(2):
                    sp.wait_ge(lo_ready, (r - 1) * 2 + s + 1)
                    sp.dma_start(raw[s][:], i["w_qkrp"][r * 2 + s]).then_inc(raw_in[s], 16)
            for n in range(QKRP, QKRP + 1 + VP):
                sp.wait_ge(lo_ready, n - 1)
                src = i["w_rank"] if n == QKRP else i["w_v"][n - QKRP - 1]
                sp.dma_start(raw[n % 2][:], src).then_inc(raw_in[n % 2], 16)

        @block.scalar
        def _(act):
            def split(s, count):
                act.wait_ge(raw_in[s], count)
                split_hi(act, w_hi[s][:], raw[s][:]).then_inc(hi_ready, 1)

            def evacuate(n, s, dst):
                act.wait_ge(tile_done, n + 1)
                act.activation(dst, acc[s][:], ACT.Copy).then_inc(tile_out, 1)

            split(0, 16)
            split(1, 16)
            with act.Fori(0, QKRP // 2 - 1) as r:
                for s in range(2):
                    evacuate(2 * r + s, s, g.z[:, bass.ds(2 * r + s, 1), :])
                    split(s, (r + 2) * 16)
            evacuate(QKRP - 2, 0, g.z[:, QKRP - 2, :])
            split(0, (QKRP // 2 + 1) * 16)
            for n in range(VP):
                m = QKRP + 1 + n
                act.wait_ge(raw_in[m % 2], (m // 2 + 1) * 16)
                split_hi(act, piece(wv_hi, n), raw[m % 2][:]).then_inc(hi_ready, 1)
            evacuate(QKRP - 1, 1, g.z[:, QKRP - 1, :])
            evacuate(QKRP, 0, g.za[:])
            for t in range(TT):
                act.wait_ge(v_done, t + 1)
                act.activation(g.v[:, t, :], acc[1][:, (t % 2) * HALF:(t % 2 + 1) * HALF], ACT.Copy).then_inc(v_out, 1)

        @block.vector
        def _(dve):
            def split(n, s):
                dve.wait_ge(hi_ready, n + 1)
                split_lo(dve, w_lo[s][:], raw[s][:], w_hi[s][:]).then_inc(lo_ready, 1)

            with dve.Fori(0, QKRP // 2) as r:
                for s in range(2):
                    split(2 * r + s, s)
            split(QKRP, 0)
            for n in range(VP):
                m = QKRP + 1 + n
                dve.wait_ge(hi_ready, m + 1)
                split_lo(dve, piece(wv_lo, n), raw[m % 2][:], piece(wv_hi, n)).then_inc(lo_ready, 1)

        @block.tensor
        def _(pe):
            with pe.Fori(0, QKRP // 2) as r:
                for s in range(2):
                    pe.wait_ge(lo_ready, 2 * r + s + 1)
                    tile_product(pe, acc[s], w_hi[s], w_lo[s], g.a_hi, g.a_lo).then_inc(tile_done, 1)
            pe.wait_ge(lo_ready, QKRP + 1)
            tile_product(pe, acc[0], w_hi[0], w_lo[0], g.a_hi, g.a_lo).then_inc(tile_done, 1)
            pe.wait_ge(lo_ready, QKRP + 1 + VP)
            pe.wait_ge(tile_out, QKRP)
            for t in range(TT):
                if t >= 2:
                    pe.wait_ge(v_out, t - 1)
                dst = acc[1][:, (t % 2) * HALF:(t % 2 + 1) * HALF]
                for k in range(KC):
                    ah, al = g.a_hi[:, k, t * P:(t + 1) * P], g.a_lo[:, k, t * P:(t + 1) * P]
                    pe.matmul(dst, ah, wv_hi[:, k, :], start=k == 0, stop=False)
                    pe.matmul(dst, ah, wv_lo[:, k, :], start=False, stop=False)
                    last = pe.matmul(dst, al, wv_hi[:, k, :], start=False, stop=k == KC - 1)
                last.then_inc(v_done, 1)


def decays(g):
    nc, i, sem = g.nc, g.i, g.sem
    reset = g.at("reset", 68, [P, S])
    la = g.at("la", 72, [P, PAIRS, S])
    prefix = g.at("prefix", 80, [P, PAIRS, S])
    tail = g.at("tail", 88, [P, PAIRS, S])
    e_q = g.at("e_q", 96, [P, PAIRS, S])
    e_inv = g.at("e_inv", 104, [P, PAIRS, S])
    e_end = g.at("e_end", 112, [P, PAIRS, S])
    g.q_dec = [g.at(f"q_dec{d}", 120 + 24 * d, [P, PAIRS, S]) for d in range(2)]
    g.k_inv = [g.at(f"k_inv{d}", 128 + 24 * d, [P, PAIRS, S]) for d in range(2)]
    g.k_end = [g.at(f"k_end{d}", 136 + 24 * d, [P, PAIRS, S]) for d in range(2)]
    g.gamma = g.at("gamma", 168, [P, 2, PAIRS, NCHUNK])
    width = S + 2 * PAD
    win = [g.at(f"win{n}", 169 + 4.125 * n, [P, width]) for n in range(2)]
    pooled = g.at("pooled", 178, [P, S])
    w_alpha = g.at("w_alpha", 182, [P, GLA_HEADS * GLA_DK])
    w_pool = g.at("w_pool", 183, [P, 4, P])
    edges = g.at("edges", 185, [P, 4, 2 * PAD])
    edge_tmp = g.at("edge_tmp", 186, [P, 2 * PAD])
    consts_in, weights_in = sem("reset_in"), sem("small_w_in")
    logits, logit_out, ln_ready, scan_ready, tail_ready, exps_ready, dir_done = (sem(n) for n in (
        "logits", "logit_out", "ln_ready", "scan_ready", "tail_ready", "exps_ready", "dir_done"))
    act_self = sem("act_self_c")
    silu_done, pooled_ready, pool_mm, pool_out = (sem(n) for n in ("silu_r", "pooled_ready", "pool_mm", "pool_out"))
    with ExitStack() as banks:
        lps = [banks.enter_context(nc.psum_tensor(f"logit{n}", [P, S], F32)) for n in range(PAIRS)]
        pps = [banks.enter_context(nc.psum_tensor(f"pool_ps{n}", [P, S], F32)) for n in range(2)]
        block = banks.enter_context(nc.Block())
        flat = lambda a: a[:].rearrange("p a b -> p (a b)")
        chunks = lambda a, pair: a[:, pair, :].rearrange("p (n c) -> p n c", c=CHUNK)
        last_of = lambda a, pair: chunks(a, pair)[:, :, CHUNK - 1:CHUNK]

        @block.sync
        def _(sp):
            sp.dma_start(w_alpha[:], i["w_alpha"]).then_inc(weights_in, 16)
            sp.dma_start(w_pool[:], i["w_pool"]).then_inc(weights_in, 16)
            sp.dma_start(reset[:], i["reset"]).then_inc(consts_in, 16)
            sp.dma_start(edges[:], i["edges"]).then_inc(consts_in, 16)

        @block.tensor
        def _(pe):
            pe.wait_ge(weights_in, 32)
            for d in range(2):
                if d:
                    pe.wait_ge(logit_out, 1)
                rows = slice(64 * d, 64 * d + RANK)
                for pair in range(PAIRS):
                    for half in range(2):
                        cols = slice(half * HALF, (half + 1) * HALF)
                        last = pe.matmul(lps[pair][:, cols], w_alpha[rows, pair * P:(pair + 1) * P], g.za[rows, cols],
                                         start=True, stop=True)
                last.then_inc(logits, 1)
            for n in range(4):
                pe.wait_ge(pooled_ready, n + 1)
                if n >= 2:
                    pe.wait_ge(pool_out, n - 1)
                for half in range(2):
                    cols = slice(half * HALF, (half + 1) * HALF)
                    last = pe.matmul(pps[n % 2][:, cols], w_pool[:, n, :], pooled[:, cols], start=True, stop=True)
                last.then_inc(pool_mm, 1)

        @block.scalar
        def _(act):
            act.activation(g.z[:, 4:8, :], g.z[:, 4:8, :], ACT.Silu).then_inc(silu_done, 1)
            for d in range(2):
                if d:
                    act.wait_ge(dir_done, d)
                act.wait_ge(logit_out, d + 1)
                act.activation(flat(e_q), flat(la), ACT.Abs)
                act.drain()
                act.activation(flat(e_q), flat(e_q), ACT.Exp, scale=-1.0)
                act.drain()
                act.activation(flat(e_end), flat(e_q), ACT.Ln, bias=1.0).then_inc(ln_ready, 1)
                act.wait_ge(scan_ready, d + 1)
                b = prefix if d == 0 else e_end
                for pair in range(PAIRS):
                    act.activation(g.gamma[:, d, pair, :], last_of(prefix, pair).squeeze(2), ACT.Exp, scale=1.0 / TAU)
                act.wait_ge(tail_ready, d + 1)
                act.activation(flat(e_q), flat(b), ACT.Exp, scale=1.0 / TAU)
                act.activation(flat(e_inv), flat(b), ACT.Exp, scale=-1.0 / TAU)
                act.drain()
                act.activation(flat(e_end), flat(tail), ACT.Exp, scale=1.0 / TAU).then_inc(exps_ready, 1)
            for n in range(4):
                act.wait_ge(pool_mm, n + 1)
                act.activation(g.z[:, 8 + n, :], pps[n % 2][:], ACT.Copy, scale=g.vec("pool_scale")[:, n:n + 1])\
                   .then_inc(pool_out, 1)

        @block.vector
        def _(dve):
            dve.wait_ge(consts_in, 32)
            for d in range(2):
                bias = g.vec("b_alpha_f" if d == 0 else "b_alpha_b")
                dve.wait_ge(logits, d + 1)
                for pair in range(PAIRS):
                    last = dve.tensor_scalar(la[:, pair, :], lps[pair][:], bias[:, pair:pair + 1], None, ALU.add)
                last.then_inc(logit_out, 1)
                dve.wait_ge(logit_out, d + 1)
                dve.wait_ge(ln_ready, d + 1)
                dve.scalar_tensor_tensor(flat(la), flat(la), 0.0, flat(e_end), ALU.min, ALU.subtract)
                dve.drain()
                for pair in range(PAIRS):
                    last = dve.tensor_tensor_scan(prefix[:, pair, :], reset[:], la[:, pair, :], 0.0, ALU.mult, ALU.add)
                last.then_inc(scan_ready, 1)
                dve.drain()
                for pair in range(PAIRS):
                    total = last_of(prefix, pair).to_broadcast([P, NCHUNK, CHUNK])
                    if d == 0:
                        last = dve.tensor_tensor(chunks(tail, pair), total, chunks(prefix, pair), ALU.subtract)
                    else:
                        dve.tensor_tensor(tail[:, pair, :], prefix[:, pair, :], la[:, pair, :], ALU.subtract)
                        dve.drain()
                        last = dve.tensor_tensor(chunks(e_end, pair), total, chunks(tail, pair), ALU.subtract)
                last.then_inc(tail_ready, 1)
                dve.wait_ge(exps_ready, d + 1)
                q, k = g.z[:, 0:2, :].rearrange("p a b -> p (a b)"), g.z[:, 2:4, :].rearrange("p a b -> p (a b)")
                dve.scalar_tensor_tensor(flat(g.q_dec[d]), q, GLA_DK ** -0.5, flat(e_q), ALU.mult, ALU.mult)
                dve.tensor_tensor(flat(g.k_inv[d]), k, flat(e_inv), ALU.mult)
                dve.tensor_tensor(flat(g.k_end[d]), k, flat(e_end), ALU.mult).then_inc(dir_done, 1)
            dve.memset(win[0][:], 0.0)
            dve.memset(win[1][:], 0.0)
            for n, w in enumerate(WINDOWS):
                p = g.z[:, 8 + n, :]
                dve.drain()
                dve.tensor_copy(win[0][:, PAD:PAD + S], p)
                src, dst, m, lo, hi = win[0], win[1], 1, 0, width
                while m < w:
                    left, right = (1, 0) if m == 1 else (m // 2, m // 2)
                    lo, hi = lo + left, hi - right
                    dve.drain()
                    dve.tensor_tensor(dst[:, lo:hi], src[:, lo - left:hi - left], src[:, lo + right:hi + right], ALU.add)
                    src, dst, m = dst, src, 2 * m
                if n:
                    dve.wait_ge(pool_mm, n)
                dve.drain()
                body = src[:, PAD:PAD + S]
                dve.scalar_tensor_tensor(pooled[:], body, 1.0 / w, p, ALU.mult, ALU.subtract)
                ends = lambda a: a[:, 0:S].rearrange("p (a b) -> p a b", b=S // 2)
                for e in range(2):
                    cols = slice(0, PAD) if e == 0 else slice(S - PAD, S)
                    dve.tensor_tensor(edge_tmp[:, e * PAD:(e + 1) * PAD], src[:, PAD + cols.start:PAD + cols.stop],
                                      edges[:, n, e * PAD:(e + 1) * PAD], ALU.mult)
                dve.drain()
                for e in range(2):
                    cols = slice(0, PAD) if e == 0 else slice(S - PAD, S)
                    last = dve.tensor_tensor(pooled[:, cols], edge_tmp[:, e * PAD:(e + 1) * PAD], p[:, cols], ALU.subtract)
                last.then_inc(pooled_ready, 1)
                if n < 3:
                    dve.drain()
                    dve.memset(win[0][:, 0:PAD], 0.0)
                    dve.memset(win[0][:, PAD + S:width], 0.0)


def attention(g):
    nc, i, sem = g.nc, g.i, g.sem
    g.o = g.at("o", 0, [P, TT, GLA_HEADS * GLA_DV])
    k_tok = [g.at(f"k_tok{d}", 72 + 8 * d, [P, TT, PAIRS * P]) for d in range(2)]
    state = g.at("state", 88, [P, 2, PAIRS, NCHUNK, GLA_DV])
    scores = [g.at(f"scores{n}", 169 + 0.5 * n, [P, P]) for n in range(4)]
    kt_ps, kt_out, upd_ps, upd_done, sc_ps, sc_out, o_ps_done, o_out = (sem(n) for n in (
        "kt_ps", "kt_out", "upd_ps", "upd_done", "sc_ps", "sc_out", "o_done", "o_out"))
    steps = NCHUNK - 1
    with ExitStack() as banks:
        bank = lambda name: banks.enter_context(nc.psum_tensor(name, [P, 4, P], F32))
        tr = [bank(f"tr{n}") for n in range(2)]
        upd = [[bank(f"upd{d}{n}") for n in range(2)] for d in range(2)]
        ops = upd
        sps = [bank(f"sps{n}") for n in range(2)]
        block = banks.enter_context(nc.Block())
        groups = [(d, pair, q) for d in range(2) for pair in range(PAIRS) for q in range(TT // 4)]
        chunk_at = lambda d, n: n if d == 0 else NCHUNK - 1 - n

        @block.tensor
        def _(pe):
            for n, (d, pair, q) in enumerate(groups):
                if n >= 2:
                    pe.wait_ge(kt_out, n - 1)
                for t in range(4):
                    cols = slice((4 * q + t) * P, (4 * q + t + 1) * P)
                    last = pe.transpose(tr[n % 2][:, t, :], g.k_end[d][:, pair, cols], g.ident)
                last.then_inc(kt_ps, 1)
            pe.wait_ge(kt_out, len(groups))
            for n in range(steps):
                if n >= 2:
                    pe.wait_ge(upd_done, n - 1)
                for d in range(2):
                    c = chunk_at(d, n)
                    rows = slice(CHUNK * (c % 2), CHUNK * (c % 2) + CHUNK)
                    for pair in range(PAIRS):
                        for h in range(2):
                            head = 2 * pair + h
                            last = pe.matmul(upd[d][n % 2][h * GLA_DK:(h + 1) * GLA_DK, pair, :],
                                             k_tok[d][rows, c // 2, pair * P + h * GLA_DK:pair * P + (h + 1) * GLA_DK],
                                             g.v[rows, c // 2, head * GLA_DV:(head + 1) * GLA_DV], start=True, stop=True)
                last.then_inc(upd_ps, 1)

            def score(n):
                t, head = n // GLA_HEADS, n % GLA_HEADS
                pair, keys = head // 2, slice(GLA_DK * (head % 2), GLA_DK * (head % 2 + 1))
                cols = slice(t * P, (t + 1) * P)
                if n >= 2:
                    pe.wait_ge(sc_out, n - 1)
                for d in range(2):
                    last = pe.matmul(sps[n % 2][:, d, :], g.k_inv[d][keys, pair, cols], g.q_dec[d][keys, pair, cols],
                                     start=True, stop=True)
                last.then_inc(sc_ps, 1)

            score(0)
            for n in range(TT * GLA_HEADS):
                t, head = n // GLA_HEADS, n % GLA_HEADS
                pair, keys = head // 2, slice(GLA_DK * (head % 2), GLA_DK * (head % 2 + 1))
                if n + 1 < TT * GLA_HEADS:
                    score(n + 1)
                pe.wait_ge(sc_out, n + 1)
                if head == 0 and t >= 2:
                    pe.wait_ge(o_out, t - 1)
                if n == 0:
                    pe.wait_ge(upd_done, steps)
                cols = slice(head * GLA_DV, (head + 1) * GLA_DV)
                dst = ops[t % 2][head % 2][:, pair, :]
                pe.matmul(dst, scores[n % 4][:], g.v[:, t, cols], start=True, stop=False)
                for half in range(2):
                    c = 2 * t + half
                    rows = slice(CHUNK * half, CHUNK * (half + 1))
                    for d in range(2):
                        last = pe.matmul(dst[rows, :], g.q_dec[d][keys, pair, c * CHUNK:(c + 1) * CHUNK],
                                         state[keys, d, pair, c, :], start=False, stop=d == 1)
                if head == GLA_HEADS - 1:
                    last.then_inc(o_ps_done, 1)

        @block.vector
        def _(dve):
            for n, (d, pair, q) in enumerate(groups):
                dve.wait_ge(kt_ps, n + 1)
                dve.tensor_copy(k_tok[d][:, 4 * q:4 * q + 4, pair * P:(pair + 1) * P], tr[n % 2][:]).then_inc(kt_out, 1)
            for n in range(4):
                dve.memset(scores[n][:], 0.0)
            for d in range(2):
                dve.memset(state[:, d, :, chunk_at(d, 0), :], 0.0)
            dve.drain()
            for n in range(steps):
                dve.wait_ge(upd_ps, n + 1)
                for d in range(2):
                    c, nxt = chunk_at(d, n), chunk_at(d, n + 1)
                    for pair in range(PAIRS):
                        last = dve.scalar_tensor_tensor(state[:, d, pair, nxt, :], state[:, d, pair, c, :],
                                                        g.gamma[:, d, pair, c:c + 1], upd[d][n % 2][:, pair, :],
                                                        ALU.mult, ALU.add)
                last.then_inc(upd_done, 1)
                dve.drain()
            for n in range(TT * GLA_HEADS):
                dve.wait_ge(sc_ps, n + 1)
                dve.copy_predicated(scores[n % 4][:], g.mask_f.bitcast(U32), sps[n % 2][:, 0, :])
                dve.drain()
                dve.copy_predicated(scores[n % 4][:], g.mask_b.bitcast(U32), sps[n % 2][:, 1, :]).then_inc(sc_out, 1)

        @block.scalar
        def _(act):
            for t in range(TT):
                act.wait_ge(o_ps_done, t + 1)
                heads = g.o[:, t, :].rearrange("p (a b v) -> p b a v", b=2, v=GLA_DV)
                for h in range(2):
                    last = act.activation(heads[:, h], ops[t % 2][h][:, 0:PAIRS, :], ACT.Copy)
                last.then_inc(o_out, 1)


def mix_out(g):
    nc, i, sem = g.nc, g.i, g.sem
    m_hi = g.at("m_hi", 52, [P, KC, S], F32R)
    m_lo = g.at("m_lo", 84, [P, KC, S], F32R)
    wo_hi = g.at("wo_hi", 116, [P, KC, D], F32R)
    wo_lo = g.at("wo_lo", 148, [P, KC, D], F32R)
    raw = [g.at(f"wo_raw{s}", 180 + 4 * s, [P, D]) for s in range(2)]
    mf = g.at("mf", 188, [P, S])
    g.xn = g.at("xn", 0, [P, TT, D])
    xt = [g.at(f"xt{s}", 32 + 4 * s, [P, D]) for s in range(2)]
    junk = g.at("junk_e", 40, [P, D])
    junk_v = g.at("junk_v", 44, [P, D])
    wo_in = [sem(f"wo_in{s}") for s in range(2)]
    xt_in = [sem(f"xt_in{s}") for s in range(2)]
    x1_stored = [sem(f"x1_stored{s}") for s in range(2)]
    o_ssq, o_root, o_scaled, wo_hi_ready, wo_lo_ready, ot_ps, mf_ready, m_hi_ready, m_lo_ready, mixed = (
        sem(n) for n in ("o_ssq", "o_root", "o_scaled", "wo_hi_r", "wo_lo_r", "ot_ps", "mf_ready", "m_hi_r", "m_lo_r", "mixed"))
    mix_root, x1_ready, x1_root, xn_done = (sem(n) for n in ("mix_root", "x1_ready", "x1_root", "xn_done"))
    act_self = sem("act_self_e")
    HT = GLA_HEADS * TT
    with ExitStack() as banks:
        otp = [banks.enter_context(nc.psum_tensor(f"otp{n}", [P, S], F32)) for n in range(2)]
        mps = [banks.enter_context(nc.psum_tensor(f"mps{n}", [P, D], F32)) for n in range(2)]
        block = banks.enter_context(nc.Block())
        heads_view = g.o[:].rearrange("p t (h v) -> p (t h) v", v=GLA_DV)

        @block.sync
        def _(sp):
            for k in range(KC):
                if k >= 2:
                    sp.wait_ge(wo_lo_ready, k - 1)
                sp.dma_start(raw[k % 2][:], i["w_out"][:, k, :]).then_inc(wo_in[k % 2], 16)
            sp.wait_ge(m_lo_ready, KC)
            for t in range(TT):
                if t >= 2:
                    sp.wait_ge(xn_done, t - 1)
                    sp.wait_ge(x1_stored[t % 2], 16 * (t // 2))
                sp.dma_start(xt[t % 2][:], i["x"][t * P:(t + 1) * P, :]).then_inc(xt_in[t % 2], 16)
                if t >= 1:
                    sp.wait_ge(x1_ready, t)
                    sp.dma_start(g.x1_d[t - 1], xt[(t - 1) % 2][:]).then_inc(x1_stored[(t - 1) % 2], 16)
            sp.wait_ge(x1_ready, TT)
            sp.dma_start(g.x1_d[TT - 1], xt[(TT - 1) % 2][:]).then_inc(x1_stored[(TT - 1) % 2], 16)
            for s in range(2):
                sp.wait_ge(x1_stored[s], 16 * TT // 2)

        @block.scalar
        def _(act):
            for n in range(HT):
                if n >= KC:
                    act.wait_ge(o_ssq, n - KC + 1)
                act.activation(mf[:, n % KC * P:(n % KC + 1) * P], heads_view[:, n, :], ACT.Square,
                               accum_out=g.ssq[:, n:n + 1]).then_inc(o_ssq, 1)
            act.wait_ge(o_ssq, HT)
            act.activation(g.rstd[:, 0:HT], g.ssq[:, 0:HT], ACT.Sqrt, scale=1.0 / GLA_DV, bias=g.eps[:]).then_inc(o_root, 1)
            for k in range(KC):
                act.wait_ge(wo_in[k % 2], 16 * (k // 2 + 1))
                split_hi(act, wo_hi[:, k, :], raw[k % 2][:]).then_inc(wo_hi_ready, 1)
            for t in range(TT):
                act.wait_ge(mixed, t + 1)
                act.activation(junk[:], mps[t % 2][:], ACT.Square, accum_out=g.ssq[:, 2 * t:2 * t + 1]).then_inc(act_self, 1)
                act.wait_ge(act_self, 2 * t + 1)
                act.activation(g.rstd[:, 2 * t:2 * t + 1], g.ssq[:, 2 * t:2 * t + 1], ACT.Sqrt, scale=1.0 / D,
                               bias=g.eps[:]).then_inc(mix_root, 1)
                act.wait_ge(x1_ready, t + 1)
                act.activation(junk[:], xt[t % 2][:], ACT.Square, accum_out=g.ssq[:, 2 * t + 1:2 * t + 2]).then_inc(act_self, 1)
                act.wait_ge(act_self, 2 * t + 2)
                act.activation(g.rstd[:, 2 * t + 1:2 * t + 2], g.ssq[:, 2 * t + 1:2 * t + 2], ACT.Sqrt, scale=1.0 / D,
                               bias=g.eps[:]).then_inc(x1_root, 1)

        @block.vector
        def _(dve):
            dve.wait_ge(o_root, 1)
            dve.reciprocal(g.rstd[:, 0:HT], g.rstd[:, 0:HT])
            dve.drain()
            dve.tensor_tensor(heads_view, heads_view, g.rstd[:, 0:HT].unsqueeze(2).to_broadcast([P, HT, GLA_DV]),
                              ALU.mult).then_inc(o_scaled, 1)
            for k in range(KC):
                dve.wait_ge(wo_hi_ready, k + 1)
                split_lo(dve, wo_lo[:, k, :], raw[k % 2][:], wo_hi[:, k, :]).then_inc(wo_lo_ready, 1)
            for k in range(KC):
                if k < GLA_HEADS:
                    dve.wait_ge(ot_ps, k + 1)
                    if k:
                        dve.drain()
                    dve.scalar_tensor_tensor(mf[:], otp[k % 2][:], g.vec("g_gla_head")[:, k:k + 1], g.z[:, 4 + k, :],
                                             ALU.mult, ALU.mult).then_inc(mf_ready, 1)
                    dve.drain()
                    src = mf[:]
                else:
                    src = g.z[:, 4 + k, :]
                dve.tensor_copy(m_hi[:, k, :], src)
                dve.drain()
                split_lo(dve, m_lo[:, k, :], src, m_hi[:, k, :]).then_inc(m_lo_ready, 1)
            for t in range(TT):
                dve.wait_ge(mix_root, t + 1)
                dve.reciprocal(g.rstd[:, 2 * t:2 * t + 1], g.rstd[:, 2 * t:2 * t + 1])
                dve.drain()
                dve.scalar_tensor_tensor(junk_v[:], mps[t % 2][:], g.rstd[:, 2 * t:2 * t + 1], g.gate_rows[:, 0, :],
                                         ALU.mult, ALU.mult)
                dve.drain()
                dve.wait_ge(xt_in[t % 2], 16 * (t // 2 + 1))
                dve.tensor_tensor(xt[t % 2][:], xt[t % 2][:], junk_v[:], ALU.add).then_inc(x1_ready, 1)
                dve.wait_ge(x1_root, t + 1)
                dve.reciprocal(g.rstd[:, 2 * t + 1:2 * t + 2], g.rstd[:, 2 * t + 1:2 * t + 2])
                dve.drain()
                dve.tensor_scalar(g.xn[:, t, :], xt[t % 2][:], g.rstd[:, 2 * t + 1:2 * t + 2], None, ALU.mult)\
                   .then_inc(xn_done, 1)

        @block.tensor
        def _(pe):
            pe.wait_ge(o_scaled, 1)
            for h in range(GLA_HEADS):
                if h >= 2:
                    pe.wait_ge(mf_ready, h - 1)
                for t in range(TT):
                    last = pe.transpose(otp[h % 2][:, t * P:(t + 1) * P], g.o[:, t, h * GLA_DV:(h + 1) * GLA_DV], g.ident)
                last.then_inc(ot_ps, 1)
            pe.wait_ge(wo_lo_ready, KC)
            pe.wait_ge(m_lo_ready, KC)
            for t in range(TT):
                if t >= 2:
                    pe.wait_ge(x1_ready, t - 1)
                for k in range(KC):
                    mh, ml = m_hi[:, k, t * P:(t + 1) * P], m_lo[:, k, t * P:(t + 1) * P]
                    for m, w, first, final in ((mh, wo_hi, k == 0, False), (mh, wo_lo, False, False),
                                               (ml, wo_hi, False, k == KC - 1)):
                        for half in range(2):
                            cols = slice(half * HALF, (half + 1) * HALF)
                            last = pe.matmul(mps[t % 2][:, cols], m, w[:, k, cols], start=first, stop=final)
                last.then_inc(mixed, 1)


def second_norm(g):
    nc, sem = g.nc, g.sem
    hf = [g.at(f"hf_e{s}", 52 + 4 * s, [P, S]) for s in range(2)]
    sems = tuple(sem(n) for n in ("tp_e", "hf_e", "hi_e", "lo_e"))
    with nc.psum_tensor("tp_e0", [P, S], F32) as tp0, nc.psum_tensor("tp_e1", [P, S], F32) as tp1, nc.Block() as block:
        tp = [tp0, tp1]

        @block.tensor
        def _(pe):
            modulate_transposed(g, "e", g.xn, hf, tp, None, None, sems, None, None, pe)

        @block.scalar
        def _(act):
            modulate_transposed(g, "e", g.xn, hf, tp, g.scale2, g.mod[:, 3 * KC:4 * KC], sems, act, None, None)

        @block.vector
        def _(dve):
            modulate_transposed(g, "e", g.xn, hf, tp, None, None, sems, None, dve, None)


def topk_buffers(g):
    g.s_work = g.at("s_work", 104, [P, 2, NKEYS])
    g.s_rest = g.at("s_rest", 105, [P, 2, NKEYS])
    g.cand = g.at("cand", 106, [P, TOPK, TOPK])
    g.cand_rest = g.at("cand_rest", 107, [P, TOPK, TOPK])
    g.match = g.at("match", 108, [P, 2, TOPK, TOPK])
    g.chosen = g.at("chosen", 110, [P, 2, HEADS, TOPK])
    g.top_all = g.at("top_all", 111, [P, HEADS, TOPK])
    g.vals = g.at("vals", 111.5, [P, 2, TOPK])
    g.tops = g.at("tops", 111.625, [P, TOPK])
    g.idx = g.at("idx", 111.6875, [P, 2, TOPK], U32)
    g.pos = g.at("pos", 111.8125, [P, TOPK], U32)
    g.hilo = g.at("hilo", 111.875, [P, 2, TOPK], U32)
    g.gates = g.at("gates", 192, [P, HEADS, TOPK])
    g.norm = g.at("norm", 192.5, [P, HEADS])
    g.slots = g.at("slots", 193, [P, 3, P])
    g.zero = g.at("zero", 192.75, [P, 1])


def topk_head(g, dve, h, topk_done):
    flat = lambda a: a.rearrange("p a b -> p (a b)")
    for p in range(2):
        dve.max(g.vals[:, p, 0:8], g.s_work[:, p, :])
    dve.drain()
    for p in range(2):
        dve.max_index(g.idx[:, p, 0:8], g.vals[:, p, 0:8], g.s_work[:, p, :])
        dve.match_replace(g.s_rest[:, p, :], g.vals[:, p, 0:8], g.s_work[:, p, :], LOWEST)
    dve.drain()
    for p in range(2):
        dve.max(g.vals[:, p, 8:16], g.s_rest[:, p, :])
    dve.drain()
    for p in range(2):
        dve.max_index(g.idx[:, p, 8:16], g.vals[:, p, 8:16], g.s_rest[:, p, :])
    dve.tensor_tensor(g.cand[:], g.vals[:, 0, :].unsqueeze(2).to_broadcast([P, TOPK, TOPK]),
                      g.vals[:, 1, :].unsqueeze(1).to_broadcast([P, TOPK, TOPK]), ALU.add)
    dve.drain()
    cand, rest = flat(g.cand[:]), flat(g.cand_rest[:])
    dve.max(g.tops[:, 0:8], cand)
    dve.drain()
    dve.max_index(g.pos[:, 0:8], g.tops[:, 0:8], cand)
    dve.match_replace(rest, g.tops[:, 0:8], cand, LOWEST)
    dve.drain()
    dve.max(g.tops[:, 8:16], rest)
    dve.drain()
    dve.max_index(g.pos[:, 8:16], g.tops[:, 8:16], rest)
    dve.tensor_copy(g.top_all[:, bass.ds(h, 1), :], g.tops[:].unsqueeze(1))
    dve.drain()
    dve.tensor_scalar(g.hilo[:, 0, :], g.pos[:], 4, None, ALU.logical_shift_right)
    dve.tensor_scalar(g.hilo[:, 1, :], g.pos[:], TOPK - 1, None, ALU.bitwise_and)
    dve.drain()
    full = [P, 2, TOPK, TOPK]
    dve.tensor_tensor(g.match[:], g.hilo[:].unsqueeze(3).to_broadcast(full),
                      g.iota[:, 0:TOPK].unsqueeze(1).unsqueeze(1).to_broadcast(full), ALU.is_equal)
    dve.drain()
    dve.tensor_tensor(g.match[:], g.match[:], g.idx[:].unsqueeze(2).to_broadcast(full), ALU.mult)
    dve.drain()
    dve.tensor_reduce(g.chosen[:, :, bass.ds(h, 1), :].rearrange("p a b c -> p a (b c)") if isinstance(h, int) else
                      g.chosen[:, :, bass.ds(h, 1), :], g.match[:], AX, ALU.add).then_inc(topk_done, 1)


def finish_topk(g, dve, n, shifted, exps, slots_ready):
    dve.drain()
    dve.tensor_tensor(g.gates[:], g.top_all[:], g.top_all[:, :, 0:1].to_broadcast([P, HEADS, TOPK]), ALU.subtract)\
       .then_inc(shifted, 1)
    dve.wait_ge(exps, n + 1)
    dve.tensor_reduce(g.norm[:], g.gates[:], AX, ALU.add)
    dve.drain()
    dve.reciprocal(g.norm[:], g.norm[:])
    dve.drain()
    dve.tensor_tensor(g.gates[:], g.gates[:], g.norm[:].unsqueeze(2).to_broadcast([P, HEADS, TOPK]), ALU.mult)\
       .then_inc(slots_ready, 1)


def retrieval_scores(g):
    nc, i, sem = g.nc, g.i, g.sem
    raw = [g.at(f"wq_raw{s}", 4 * s, [P, D]) for s in range(2)]
    w_hi = [g.at(f"wq_hi{s}", 8 + 4 * s, [P, D], F32R) for s in range(2)]
    w_lo = [g.at(f"wq_lo{s}", 16 + 4 * s, [P, D], F32R) for s in range(2)]
    q = [g.at(f"q{s}", 24 + 4 * s, [P, S]) for s in range(2)]
    keys = g.at("keys", 32, [P, QTILES, NKEYS])
    stage = [g.at(f"stage{s}", 40 + 4 * s, [P, TT, NKEYS]) for s in range(2)]
    topk_buffers(g)
    raw_in = [sem(f"wq_raw_in{s}") for s in range(2)]
    keys_in = sem("keys_in")
    s_stored = [sem(f"s_stored{s}") for s in range(2)]
    hi_ready, lo_ready, q_done, q_out, s_done, s_out, stage_free = (sem(n) for n in (
        "wq_hi_r", "wq_lo_r", "q_done", "q_out", "s_done", "s_out", "stage_free"))
    topk_done = sem("topk_first")
    g.shifted, g.exps, g.slots_ready = sem("shifted"), sem("exps"), sem("slots_ready")
    s_view = g.s_d.rearrange("t p m n -> p t m n")
    with ExitStack() as banks:
        acc = [banks.enter_context(nc.psum_tensor(f"acc_q{n}", [P, S], F32)) for n in range(2)]
        sps = [banks.enter_context(nc.psum_tensor(f"s_ps{n}", [P, TT, NKEYS], F32)) for n in range(2)]
        block = banks.enter_context(nc.Block())

        @block.sync
        def _(sp):
            sp.dma_start(keys[:], i["keys"]).then_inc(keys_in, 16)
            for s in range(2):
                sp.dma_start(raw[s][:], i["w_q"][s]).then_inc(raw_in[s], 16)
            sp.sem_inc(stage_free, 2)

            def store(r):
                for s in range(2):
                    sp.wait_ge(s_out, 2 * r + s + 1)
                    sp.dma_start(s_view[:, :, bass.ds(2 * r + s, 1), :], stage[s][:].unsqueeze(2)).then_inc(s_stored[s], 16)
                for s in range(2):
                    sp.wait_ge(s_stored[s], (r + 1) * 16)
                    sp.sem_inc(stage_free, 1)

            with sp.Fori(0, HEADS - 1) as r:
                for s in range(2):
                    sp.wait_ge(lo_ready, 2 * r + s + 1)
                    sp.dma_start(raw[s][:], i["w_q"][2 * (r + 1) + s]).then_inc(raw_in[s], 16)
                store(r)
            store(HEADS - 1)

        @block.scalar
        def _(act):
            def split(s, count):
                act.wait_ge(raw_in[s], count)
                split_hi(act, w_hi[s][:], raw[s][:]).then_inc(hi_ready, 1)

            def evacuate(n, s):
                act.wait_ge(q_done, n + 1)
                act.activation(q[s][:], acc[s][:], ACT.Copy).then_inc(q_out, 1)

            split(0, 16)
            split(1, 16)
            with act.Fori(0, HEADS - 1) as r:
                for s in range(2):
                    evacuate(2 * r + s, s)
                    split(s, (r + 2) * 16)
            evacuate(QTILES - 2, 0)
            evacuate(QTILES - 1, 1)
            act.wait_ge(g.shifted, 1)
            act.activation(g.gates[:], g.gates[:], ACT.Exp).then_inc(g.exps, 1)

        @block.vector
        def _(dve):
            def split(n, s):
                dve.wait_ge(hi_ready, n + 1)
                split_lo(dve, w_lo[s][:], raw[s][:], w_hi[s][:]).then_inc(lo_ready, 1)

            def scores_out(n, s):
                dve.wait_ge(s_done, n + 1)
                dve.wait_ge(stage_free, n + 1)
                dve.tensor_copy(stage[s][:], sps[s][:]).then_inc(s_out, 1)
                dve.tensor_copy(g.s_work[:, s, :], sps[s][:, 0, :])

            split(0, 0)
            split(1, 1)
            with dve.Fori(0, HEADS - 1) as r:
                for s in range(2):
                    scores_out(2 * r + s, s)
                    split(2 * (r + 1) + s, s)
                dve.drain()
                topk_head(g, dve, r, topk_done)
            for s in range(2):
                scores_out(QTILES - 2 + s, s)
            dve.drain()
            topk_head(g, dve, HEADS - 1, topk_done)
            finish_topk(g, dve, 0, g.shifted, g.exps, g.slots_ready)

        @block.tensor
        def _(pe):
            pe.wait_ge(keys_in, 16)
            with pe.Fori(0, HEADS) as r:
                for s in range(2):
                    n = 2 * r + s
                    pe.wait_ge(lo_ready, n + 1)
                    tile_product(pe, acc[s], w_hi[s], w_lo[s], g.a_hi, g.a_lo).then_inc(q_done, 1)
                    pe.wait_ge(q_out, n + 1)
                    for t in range(TT):
                        last = pe.matmul(sps[s][:, t, :], q[s][:, t * P:(t + 1) * P], keys[:, bass.ds(n, 1), :],
                                         start=True, stop=True)
                    last.then_inc(s_done, 1)


def expert_sweep_1(g):
    nc, i, sem = g.nc, g.i, g.sem
    raw = [g.at(f"u_raw{s}", 4 * s, [P, D]) for s in range(2)]
    w_hi = [g.at(f"u_hi{s}", 8 + 4 * s, [P, D], F32R) for s in range(2)]
    w_lo = [g.at(f"u_lo{s}", 16 + 4 * s, [P, D], F32R) for s in range(2)]
    gelu = [g.at(f"gelu{s}", 24 + 4 * s, [P, S]) for s in range(2)]
    gate_tile = g.at("gate_tile", 32, [P, NKEYS, P])
    s_tile = g.at("s_tile", 96, [P, QTILES, NKEYS])
    onehot = [g.at(f"onehot{s}", 112 + 8 * s, [P, TOK, NKEYS]) for s in range(2)]
    raw_in = [sem(f"u_raw_in{s}") for s in range(2)]
    act_stored = [sem(f"act_stored{s}") for s in range(2)]
    s_in, gate_stored = sem("s_in"), sem("gate_stored")
    hi_ready, lo_ready, tile_done, gelu_done, gelu_free = (sem(n) for n in (
        "u_hi_r", "u_lo_r", "u_done", "gelu_done", "gelu_free"))
    topk_done, slots_ps, slots_out, eq_ready, onehot_ready, onehot_free, gate_ps, gate_ps_free, gate_out, gate_tile_free = (
        sem(n) for n in ("topk_done", "slots_ps", "slots_out", "eq_ready", "onehot_ready", "onehot_free", "gate_ps",
                         "gate_ps_free", "gate_out", "gate_tile_free"))
    BANKS = 4
    PER = TOK // BANKS
    with ExitStack() as banks:
        acc = [banks.enter_context(nc.psum_tensor(f"acc_u{n}", [P, S], F32)) for n in range(2)]
        gps = [banks.enter_context(nc.psum_tensor(f"gate_ps{n}", [P, PER, NKEYS], F32)) for n in range(BANKS)]
        block = banks.enter_context(nc.Block())

        def run(eng, before_tile, step, after_tile):
            with eng.Fori(0, TT - 1) as j:
                before_tile(j, True)
                with eng.Fori(0, HEADS) as h:
                    step(j, h, j * HEADS + h, True, True)
                after_tile(j, True)
            j = TT - 1
            before_tile(j, False)
            with eng.Fori(0, HEADS - 1) as h:
                step(j, h, j * HEADS + h, False, True)
            step(j, HEADS - 1, STEPS - 1, False, False)
            after_tile(j, False)

        @block.sync
        def _(sp):
            for s in range(2):
                sp.dma_start(raw[s][:], i["u"][s]).then_inc(raw_in[s], 16)
            sp.sem_inc(gelu_free, 2)

            def before_tile(j, more):
                if more:
                    sp.wait_ge(topk_done, j * HEADS + 1)
                    sp.dma_start(s_tile[:], g.s_d[j + 1]).then_inc(s_in, 16)

            def step(j, h, b, topk, more):
                if more:
                    for s in range(2):
                        sp.wait_ge(lo_ready, 2 * b + s + 1)
                        sp.dma_start(raw[s][:], i["u"][2 * (b + 1) + s]).then_inc(raw_in[s], 16)
                for s in range(2):
                    sp.wait_ge(gelu_done, 2 * b + s + 1)
                    sp.dma_start(g.act_d[2 * b + s], gelu[s][:]).then_inc(act_stored[s], 16)
                for s in range(2):
                    sp.wait_ge(act_stored[s], (b + 1) * 16)
                    sp.sem_inc(gelu_free, 1)

            def after_tile(j, more):
                sp.wait_ge(gate_out, (j + 1) * HEADS)
                dst = g.gate_d.rearrange("n p t -> p n t")[:, :, bass.ts(j, P)]
                sp.dma_start(dst, gate_tile[:]).then_inc(gate_stored, 16)

            run(sp, before_tile, step, after_tile)
            sp.wait_ge(gate_stored, TT * 16)

        @block.gpsimd
        def _(pool):
            pool.sem_inc(gate_tile_free, 1)

            def step(j, h, b, topk, more):
                pool.wait_ge(eq_ready, b + 1)
                pool.tensor_tensor(onehot[1][:], onehot[1][:],
                                   g.slots[:, 2, bass.ts(h, TOK)].unsqueeze(2).to_broadcast([P, TOK, NKEYS]),
                                   ALU.mult).then_inc(onehot_ready, 1)

            def after_tile(j, more):
                pool.wait_ge(gate_stored, (j + 1) * 16)
                pool.sem_inc(gate_tile_free, 1)

            run(pool, lambda j, more: None, step, after_tile)

        @block.scalar
        def _(act):
            def split(s, count):
                act.wait_ge(raw_in[s], count)
                split_hi(act, w_hi[s][:], raw[s][:]).then_inc(hi_ready, 1)

            split(0, 16)
            split(1, 16)
            act.sem_inc(gate_ps_free, 1)

            def step(j, h, b, topk, more):
                for s in range(2):
                    act.wait_ge(tile_done, 2 * b + s + 1)
                    act.wait_ge(gelu_free, 2 * b + s + 1)
                    act.activation(gelu[s][:], acc[s][:], ACT.Gelu).then_inc(gelu_done, 1)
                    if more:
                        split(s, (b + 2) * 16)
                act.wait_ge(gate_tile_free, j + 1)
                for n in range(BANKS):
                    act.wait_ge(gate_ps, BANKS * b + n + 1)
                    dst = gate_tile[:, :, bass.ds(h * TOK + n * PER, PER)]
                    last = act.activation(dst.rearrange("p n t -> p t n"), gps[n][:], ACT.Copy)
                last.then_inc(gate_out, 1)
                act.wait_ge(gate_out, b + 1)
                act.sem_inc(gate_ps_free, 1)

            def after_tile(j, more):
                if more:
                    act.wait_ge(g.shifted, j + 2)
                    act.activation(g.gates[:], g.gates[:], ACT.Exp).then_inc(g.exps, 1)

            run(act, lambda j, more: None, step, after_tile)

        @block.vector
        def _(dve):
            def split(n, s):
                dve.wait_ge(hi_ready, n + 1)
                split_lo(dve, w_lo[s][:], raw[s][:], w_hi[s][:]).then_inc(lo_ready, 1)

            dve.sem_inc(topk_done, 1)
            split(0, 0)
            split(1, 1)

            def before_tile(j, more):
                dve.wait_ge(slots_ps, j + 1)
                dve.tensor_copy(g.slots[:], gps[0][:, 0:3, :])
                dve.drain()

            def step(j, h, b, topk, more):
                dve.wait_ge(onehot_free, b + 1)
                for n in range(2):
                    last = dve.tensor_tensor(onehot[n][:], g.iota.unsqueeze(1).to_broadcast([P, TOK, NKEYS]),
                                             g.slots[:, n, bass.ts(h, TOK)].unsqueeze(2).to_broadcast([P, TOK, NKEYS]),
                                             ALU.is_equal)
                last.then_inc(eq_ready, 1)
                if more:
                    split(2 * (b + 1), 0)
                if topk:
                    dve.wait_ge(s_in, (j + 1) * 16)
                    dve.tensor_copy(g.s_work[:], s_tile[:, bass.ds(2 * h, 2), :])
                    dve.drain()
                    topk_head(g, dve, h, topk_done)
                if more:
                    split(2 * (b + 1) + 1, 1)

            def after_tile(j, more):
                if more:
                    finish_topk(g, dve, j + 1, g.shifted, g.exps, g.slots_ready)

            run(dve, before_tile, step, after_tile)

        @block.tensor
        def _(pe):
            pe.sem_inc(onehot_free, 1)

            def before_tile(j, more):
                pe.wait_ge(g.slots_ready, j + 1)
                pe.wait_ge(gate_ps_free, j * HEADS + 1)
                flat = lambda a: a.rearrange("p a b -> p (a b)")
                for n, src in enumerate((flat(g.chosen[:, 0]), flat(g.chosen[:, 1]), flat(g.gates[:]))):
                    last = pe.transpose(gps[0][:, n, :], src, g.ident)
                last.then_inc(slots_ps, 1)

            def step(j, h, b, topk, more):
                for s in range(2):
                    pe.wait_ge(lo_ready, 2 * b + s + 1)
                    tile_product(pe, acc[s], w_hi[s], w_lo[s], g.a_hi, g.a_lo).then_inc(tile_done, 1)
                pe.wait_ge(onehot_ready, b + 1)
                pe.wait_ge(gate_ps_free, b + 1)
                for n in range(BANKS):
                    for t in range(PER):
                        last = pe.matmul(gps[n][:, t, :], onehot[0][:, n * PER + t, :], onehot[1][:, n * PER + t, :],
                                         start=True, stop=True)
                    last.then_inc(gate_ps, 1)
                pe.wait_ge(gate_ps, BANKS * (b + 1))
                pe.sem_inc(onehot_free, 1)

            run(pe, before_tile, step, lambda j, more: None)


def expert_sweep_2(g):
    nc, i, sem = g.nc, g.i, g.sem
    RING = 2
    v_raw = [g.at(f"v_raw{s}", 4 * s, [P, D]) for s in range(RING)]
    v_hi = [g.at(f"v_hi{s}", 8 + 4 * s, [P, D], F32R) for s in range(2)]
    v_lo = [g.at(f"v_lo{s}", 16 + 4 * s, [P, D], F32R) for s in range(2)]
    gt = [g.at(f"gt{s}", 24 + 2 * s, [P, HALF]) for s in range(RING)]
    at = [g.at(f"at{s}", 28 + 2 * s, [P, HALF]) for s in range(RING)]
    cf = [g.at(f"cf{s}", 32 + 2 * s, [P, HALF]) for s in range(2)]
    c_hi = [g.at(f"c_hi{s}", 36 + 2 * s, [P, HALF], F32R) for s in range(2)]
    c_lo = [g.at(f"c_lo{s}", 40 + 2 * s, [P, HALF], F32R) for s in range(2)]
    y = g.at("y", 64, [P, TT, D])
    x1 = g.at("x1", 96, [P, TT, D])
    junk = g.at("junk_y", 128, [P, D])
    v_in, gt_in, at_in = ([sem(f"{n}{s}") for s in range(RING)] for n in ("v_in", "gt_in", "at_in"))
    vhi_r, vlo_r, cf_r, chi_r, clo_r, used, y_out_act, y_out_dve = (sem(n) for n in (
        "vhi_r", "vlo_r", "cf_r", "chi_r", "clo_r", "used", "y_out_act", "y_out_dve"))
    x1_in, y_ssq, y_root, out_ready, stored = (sem(n) for n in ("x1_in", "y_ssq", "y_root", "out_ready", "out_stored"))
    ROUNDS = S // HALF
    RT = TT // ROUNDS
    N = NKEYS
    with ExitStack() as banks:
        yps = [banks.enter_context(nc.psum_tensor(f"y_ps{n}", [P, D], F32)) for n in range(RT)]
        block = banks.enter_context(nc.Block())

        @block.sync
        def _(sp):
            def load(r, n, s):
                cols = slice(r * HALF, (r + 1) * HALF)
                sp.dma_start(v_raw[s][:], i["v"][n]).then_inc(v_in[s], 16)
                sp.dma_start(gt[s][:], g.gate_d[n][:, cols]).then_inc(gt_in[s], 16)
                sp.dma_start(at[s][:], g.act_d[n][:, cols]).then_inc(at_in[s], 16)

            for s in range(2):
                load(0, s, s)
            sp.dma_start(x1[:], g.x1_d.rearrange("t p d -> p t d")).then_inc(x1_in, 16)
            for r in range(ROUNDS):
                with sp.Fori(1 if r == 0 else 0, N // 2) as q:
                    for s in range(2):
                        n = 2 * q + s
                        sp.wait_ge(vlo_r, r * N + n - 1)
                        sp.wait_ge(cf_r, r * N + n - 1)
                        load(r, n, s)
            for t in range(TT):
                sp.wait_ge(out_ready, t + 1)
                sp.dma_start(g.out[t * P:(t + 1) * P, :], y[:, t, :]).then_inc(stored, 16)
            sp.wait_ge(stored, TT * 16)

        @block.scalar
        def _(act):
            def prepare(m, s, turn, free):
                act.wait_ge(v_in[s], turn * 16)
                if free:
                    act.wait_ge(used, m - 1)
                split_hi(act, v_hi[s][:], v_raw[s][:]).then_inc(vhi_r, 1)
                act.wait_ge(cf_r, m + 1)
                split_hi(act, c_hi[s][:], cf[s][:]).then_inc(chi_r, 1)

            def empty(r):
                act.wait_ge(used, (r + 1) * N)
                for t in range(0, RT, 2):
                    act.activation(y[:, r * RT + t, :], yps[t][:], ACT.Copy).then_inc(y_out_act, 1)

            for r in range(ROUNDS):
                prepare(r * N, 0, r * N // 2 + 1, r > 0)
                if r:
                    empty(r - 1)
                prepare(r * N + 1, 1, r * N // 2 + 1, r > 0)
                with act.Fori(1, N // 2) as q:
                    for s in range(2):
                        prepare(r * N + 2 * q + s, s, r * N // 2 + q + 1, True)
            empty(ROUNDS - 1)
            act.wait_ge(y_out_act, TT // 2)
            act.wait_ge(y_out_dve, TT // 2)
            for t in range(TT):
                if t:
                    act.wait_ge(y_ssq, t)
                act.activation(junk[:], y[:, t, :], ACT.Square, accum_out=g.ssq[:, t:t + 1]).then_inc(y_ssq, 1)
            act.wait_ge(y_ssq, TT)
            act.activation(g.rstd[:, 0:TT], g.ssq[:, 0:TT], ACT.Sqrt, scale=1.0 / D, bias=g.eps[:]).then_inc(y_root, 1)

        @block.vector
        def _(dve):
            def prepare(m, s, turn):
                dve.wait_ge(gt_in[s], turn * 16)
                dve.wait_ge(at_in[s], turn * 16)
                dve.tensor_tensor(cf[s][:], gt[s][:], at[s][:], ALU.mult).then_inc(cf_r, 1)
                dve.wait_ge(vhi_r, m + 1)
                split_lo(dve, v_lo[s][:], v_raw[s][:], v_hi[s][:]).then_inc(vlo_r, 1)
                dve.wait_ge(chi_r, m + 1)
                split_lo(dve, c_lo[s][:], cf[s][:], c_hi[s][:]).then_inc(clo_r, 1)

            def empty(r):
                dve.wait_ge(used, (r + 1) * N)
                for t in range(1, RT, 2):
                    dve.tensor_copy(y[:, r * RT + t, :], yps[t][:]).then_inc(y_out_dve, 1)

            for r in range(ROUNDS):
                prepare(r * N, 0, r * N // 2 + 1)
                if r:
                    empty(r - 1)
                prepare(r * N + 1, 1, r * N // 2 + 1)
                with dve.Fori(1, N // 2) as q:
                    for s in range(2):
                        prepare(r * N + 2 * q + s, s, r * N // 2 + q + 1)
            empty(ROUNDS - 1)
            dve.wait_ge(x1_in, 16)
            dve.wait_ge(y_root, 1)
            dve.reciprocal(g.rstd[:, 0:TT], g.rstd[:, 0:TT])
            dve.drain()
            for t in range(TT):
                dve.scalar_tensor_tensor(y[:, t, :], y[:, t, :], g.rstd[:, t:t + 1], g.gate_rows[:, 1, :],
                                         ALU.mult, ALU.mult)
                dve.drain()
                dve.tensor_tensor(y[:, t, :], y[:, t, :], x1[:, t, :], ALU.add).then_inc(out_ready, 1)

        @block.tensor
        def _(pe):
            def product(r, n, s, first=False, last=False):
                m = r * N + n
                pe.wait_ge(vlo_r, m + 1)
                pe.wait_ge(clo_r, m + 1)
                for t in range(RT):
                    if first and r:
                        pe.wait_ge(y_out_dve if t % 2 else y_out_act, (r - 1) * RT // 2 + t // 2 + 1)
                    ch, cl = c_hi[s][:, t * P:(t + 1) * P], c_lo[s][:, t * P:(t + 1) * P]
                    for k, (c, v) in enumerate(((ch, v_hi), (ch, v_lo), (cl, v_hi))):
                        for half in range(2):
                            cols = slice(half * HALF, (half + 1) * HALF)
                            done = pe.matmul(yps[t][:, cols], c, v[s][:, cols], start=first and k == 0, stop=last and k == 2)
                done.then_inc(used, 1)

            for r in range(ROUNDS):
                product(r, 0, 0, first=True)
                product(r, 1, 1)
                with pe.Fori(1, N // 2 - 1) as q:
                    for s in range(2):
                        product(r, 2 * q + s, s)
                product(r, N - 2, 0)
                product(r, N - 1, 1, last=True)


def lay_out(a):
    f = np.ascontiguousarray
    one = {k: np.asarray(v)[0] for k, v in a.items() if k not in ("x", "c")}
    cols = lambda v: np.asarray(v).reshape(-1, P).T
    tiles = lambda w, n: f(w.reshape(KC, P, n, P).transpose(2, 1, 0, 3).reshape(n, P, KC * P))
    rows = lambda w: f(w.reshape(-1, P, w.shape[1]).transpose(1, 0, 2))
    vecs = dict(one, c=np.asarray(a["c"])[0])
    w_in = one["w_in"]
    kw, vw = GLA_HEADS * GLA_DK, GLA_HEADS * GLA_DV
    at = np.cumsum([0, kw, kw, vw, vw, RANK, RANK, D - vw])
    q, k, v, r, af, ab, p = (w_in[:, at[n]:at[n + 1]] for n in range(7))
    rank = np.zeros((D, P), np.float32)
    rank[:, 0:RANK], rank[:, 64:64 + RANK] = af, ab
    w_alpha = np.zeros((P, kw), np.float32)
    w_alpha[0:RANK], w_alpha[64:64 + RANK] = one["w_alpha_f"], one["w_alpha_b"]
    j, t = np.meshgrid(np.arange(P), np.arange(P), indexing="ij")
    same = j // CHUNK == t // CHUNK
    consts = np.concatenate([np.eye(P), np.broadcast_to(np.arange(P), (P, P)), same & (j <= t), same & (j > t)], 1)
    reset = np.broadcast_to((np.arange(S) % CHUNK != 0), (P, S))
    pos = np.r_[0:PAD, S - PAD:S]
    edges = np.stack([1.0 / (np.clip(pos + w // 2, 0, S) - np.clip(pos - w // 2, 0, S)) for w in WINDOWS])
    return {
        "x": f(np.asarray(a["x"])[0]),
        "vecs": f(np.concatenate([cols(vecs[n]) for n, _ in VECS], 1)),
        "consts": f(consts.astype(np.float32)),
        "reset": f(reset.astype(np.float32)),
        "edges": f(np.broadcast_to(edges.astype(np.float32), (P, len(WINDOWS), 2 * PAD))),
        "w_mod": f(one["w_mod"].reshape(KC, P, MOD_LOADS, MOD_COLS).transpose(2, 1, 0, 3)),
        "w_qkrp": tiles(np.concatenate([q, k, r, p], 1), QKRP),
        "w_rank": tiles(rank, 1)[0],
        "w_v": f(v.reshape(4, 2, P, vw).transpose(0, 2, 1, 3).reshape(4, P, 2 * vw)),
        "w_alpha": w_alpha,
        "w_pool": f(one["w_pool"].transpose(1, 0, 2)),
        "w_out": rows(one["w_out"]),
        "w_q": tiles(one["w_peer_q"], QTILES),
        "keys": f(one["peer_sub_keys"].reshape(QTILES, NKEYS, P).transpose(2, 0, 1)),
        "u": f(one["peer_u"].reshape(NKEYS, NKEYS, KC, P).transpose(1, 3, 2, 0).reshape(NKEYS, P, KC * P)),
        "v": f(one["peer_v"].reshape(NKEYS, NKEYS, D).transpose(1, 0, 2)),
    }


def kernel(**inputs):
    import concourse.bacc as bacc
    from concourse.bass_utils import run_bass_kernel_spmd

    nc = bacc.Bacc("TRN2", target_bir_lowering=False, num_devices=1)
    arrays = {f"in_{n}": a for n, a in lay_out(inputs).items()}
    t_in = {n[3:]: nc.dram_tensor(n, a.shape, F32, kind="ExternalInput").ap() for n, a in arrays.items()}
    out = nc.dram_tensor("out", (S, D), F32, kind="ExternalOutput").ap()
    layer(nc, t_in, out)
    r = run_bass_kernel_spmd(nc, [arrays], core_ids=[0])
    return r.results[0]["out"].reshape(1, S, D)
```

```python
from contextlib import ExitStack

import numpy as np

import concourse.bass as bass
from concourse import mybir

F32 = mybir.dt.float32
F32R = mybir.dt.float32r
U32 = mybir.dt.uint32
ALU = mybir.AluOpType
ACT = mybir.ActivationFunctionType
AX = mybir.AxisListType.X

P = 128
D = 1024
S = 1024
KC = D // P
TT = S // P
HALF = 512
N_MOD = 6
EPS = 1e-6

GLA_HEADS, GLA_DK, GLA_DV = 4, 64, 128
PAIRS = GLA_HEADS // 2
CHUNK = 64
NCHUNK = S // CHUNK
TAU = 16.0
RANK = 16
WINDOWS = (2, 4, 8, 16)
PAD = WINDOWS[-1] // 2

HEADS, NKEYS, TOPK = 8, 128, 16
QTILES = 2 * HEADS
TOK = 16
GTOK = P // 2
BLOCK_STEPS = GTOK // TOK
STEPS = TT * HEADS
LOWEST = -3.0e38

VECS = [("b_mod", N_MOD * KC), ("g_pre_mix", KC), ("g_post_mix", KC), ("b_alpha_f", PAIRS),
        ("b_alpha_b", PAIRS), ("g_gla_head", GLA_HEADS), ("pool_scale", 4), ("g_pre_ffn", KC), ("g_post_ffn", KC)]
VCOL = {}
for _name, _n in VECS:
    VCOL[_name] = (sum(n for _, n in VCOL.values()), _n)
NVEC = sum(n for _, n in VECS)

MOD_TILES = N_MOD * KC
MOD_FIRST = 2 * KC
MOD_LOAD = 3
MOD_PER_PAIR = 5
QKRP = 12


def split_hi(act, hi, raw):
    return act.activation(hi, raw, ACT.Copy)


def split_lo(dve, lo, raw, hi):
    return dve.tensor_tensor(lo, raw, hi.bitcast(F32), ALU.subtract)


def tile_product(pe, acc, w_hi, w_lo, a_hi, a_lo):
    for k in range(KC):
        wh, wl = w_hi[:, k * P:(k + 1) * P], w_lo[:, k * P:(k + 1) * P]
        for w, a, first, last in ((wh, a_hi, k == 0, False), (wh, a_lo, False, False), (wl, a_hi, False, k == KC - 1)):
            for half in range(2):
                cols = slice(half * HALF, (half + 1) * HALF)
                done = pe.matmul(acc[:, cols], w, a[:, k, cols], start=first, stop=last)
    return done


class Layer:

    def __init__(self, nc, t_in, out):
        self.nc, self.i, self.out = nc, t_in, out


def layer(nc, t_in, out):
    g = Layer(nc, t_in, out)
    with ExitStack() as ctx:
        def sem(name):
            return ctx.enter_context(nc.semaphore(name))

        def small(name, shape, dt=F32):
            return ctx.enter_context(nc.sbuf_tensor(name, shape, dt))

        g.sem = sem
        g.x1_d = nc.dram_tensor("x1_d", (TT, P, D), F32, kind="Internal").ap()
        g.s_d = nc.dram_tensor("s_d", (TT * HEADS, P, 2, NKEYS), F32, kind="Internal").ap()
        g.act_d = nc.dram_tensor("act_d", (NKEYS, P, S), F32, kind="Internal").ap()
        g.gate_d = nc.dram_tensor("gate_d", (S // GTOK, P, NKEYS, GTOK), F32, kind="Internal").ap()
        g.consts = small("consts", [P, 4 * P])
        g.ident, g.iota = g.consts[:, 0:P], g.consts[:, P:2 * P]
        g.mask_f, g.mask_b = g.consts[:, 2 * P:3 * P], g.consts[:, 3 * P:4 * P]
        g.vecs = small("vecs", [P, NVEC])
        g.vec = lambda name: g.vecs[:, VCOL[name][0]:VCOL[name][0] + VCOL[name][1]]
        g.mod = small("mod", [P, N_MOD * KC])
        g.scale1 = small("scale1", [P, KC])
        g.scale2 = small("scale2", [P, KC])
        g.gate_cols = small("gate_cols", [P, 2 * KC])
        g.gate_rows = small("gate_rows", [P, 2, D])
        g.ssq = small("ssq", [P, 4 * TT])
        g.rstd = small("rstd", [P, 4 * TT])
        g.eps = small("eps", [P, 1])
        base = nc.sbuf_base
        base = (base() if callable(base) else base)
        base = (base + 1023) // 1024 * 1024
        g.at = lambda name, kb, shape, dt=F32: nc.alloc_sbuf_tensor_at(name, shape, dt, offset=base + int(kb * 1024))
        g.a_hi = g.at("a_hi", 128, [P, KC, S], F32R)
        g.a_lo = g.at("a_lo", 160, [P, KC, S], F32R)

        modulation(g)
        projections(g)
        decays(g)
        attention(g)
        mix_out(g)
        retrieval_scores(g)
        expert_sweep_1(g)
        expert_sweep_2(g)


def modulate_transposed(g, tag, xn, hf, tp, scale, shift, sems, act, dve, pe):
    s_tp, s_hf, s_hi, s_lo = sems
    if pe is not None:
        for k in range(KC):
            if k >= 2:
                pe.wait_ge(s_hf, k - 1)
            for t in range(TT):
                last = pe.transpose(tp[k % 2][:, t * P:(t + 1) * P], xn[:, t, k * P:(k + 1) * P], g.ident)
            last.then_inc(s_tp, 1)
    if act is not None:
        for k in range(KC):
            act.wait_ge(s_tp, k + 1)
            if k >= 2:
                act.wait_ge(s_lo, k - 1)
            act.activation(hf[k % 2][:], tp[k % 2][:], ACT.Identity, bias=shift[:, k:k + 1],
                           scale=scale[:, k:k + 1]).then_inc(s_hf, 1)
    if dve is not None:
        for k in range(KC):
            dve.wait_ge(s_hf, k + 1)
            dve.tensor_copy(g.a_hi[:, k, :], hf[k % 2][:]).then_inc(s_hi, 1)
            dve.wait_ge(s_hi, k + 1)
            split_lo(dve, g.a_lo[:, k, :], hf[k % 2][:], g.a_hi[:, k, :]).then_inc(s_lo, 1)


def mod_column(g, dve, col, w):
    return dve.scalar_tensor_tensor(w, w, 1.0, g.silu_row[:], ALU.mult, ALU.mult, accum_out=g.mod[:, bass.ds(col, 1)])


def modulation(g):
    nc, i, sem = g.nc, g.i, g.sem
    early = MOD_TILES - MOD_PER_PAIR * QKRP // 2
    x = g.at("x", 0, [P, TT, D])
    w_mod = g.at("w_mod", 32, [P, early, D])
    hf = [g.at(f"hf{s}", 104 + 4 * s, [P, S]) for s in range(2)]
    junk = g.at("junk_a", 112, [P, D])
    g.silu_row = g.at("silu_row", 124, [P, D])
    consts_in, vecs_in, c_in = sem("consts_in"), sem("vecs_in"), sem("c_in")
    x_in = [sem(f"x_in{t}") for t in range(TT)]
    w_mod_in = [sem(f"w_mod_in{s}") for s in range(early // MOD_LOAD)]
    silu_ready, eps_ready, ssq_ready, root_ready, xn_ready = (sem(n) for n in (
        "silu_ready", "eps_ready", "ssq_ready", "root_ready", "xn_ready"))
    cols_ready = sem("cols_ready")
    sems = tuple(sem(n) for n in ("tp_a", "hf_a", "hi_a", "lo_a"))
    with nc.psum_tensor("tp_a0", [P, S], F32) as tp0, nc.psum_tensor("tp_a1", [P, S], F32) as tp1, nc.Block() as block:
        tp = [tp0, tp1]

        @block.sync
        def _(sp):
            sp.dma_start(g.silu_row[:], i["c"].to_broadcast([P, D])).then_inc(c_in, 16)
            for t in range(TT):
                sp.dma_start(x[:, t, :], i["x"][t * P:(t + 1) * P, :]).then_inc(x_in[t], 16)
            sp.dma_start(g.vecs[:], i["vecs"]).then_inc(vecs_in, 16)
            sp.dma_start(g.consts[:], i["consts"]).then_inc(consts_in, 16)
            for s in range(early // MOD_LOAD):
                tiles = slice(s * MOD_LOAD, (s + 1) * MOD_LOAD)
                sp.dma_start(w_mod[:, tiles, :], i["w_mod"][tiles].rearrange("n p d -> p n d")).then_inc(w_mod_in[s], 16)

        @block.scalar
        def _(act):
            act.wait_ge(c_in, 16)
            act.activation(g.silu_row[:], g.silu_row[:], ACT.Silu).then_inc(silu_ready, 1)
            for t in range(TT):
                act.wait_ge(x_in[t], 16)
                if t:
                    act.wait_ge(ssq_ready, t)
                act.activation(junk[:], x[:, t, :], ACT.Square, accum_out=g.ssq[:, t:t + 1]).then_inc(ssq_ready, 1)
            act.wait_ge(ssq_ready, TT)
            act.wait_ge(eps_ready, 1)
            act.activation(g.rstd[:, 0:TT], g.ssq[:, 0:TT], ACT.Sqrt, scale=1.0 / D, bias=g.eps[:]).then_inc(root_ready, 1)
            act.wait_ge(cols_ready, 1)
            modulate_transposed(g, "a", x, hf, tp, g.scale1, g.mod[:, 0:KC], sems, act, None, None)

        @block.vector
        def _(dve):
            dve.memset(g.eps[:], EPS).then_inc(eps_ready, 1)
            dve.wait_ge(root_ready, 1)
            dve.reciprocal(g.rstd[:, 0:TT], g.rstd[:, 0:TT])
            dve.drain()
            for t in range(TT):
                last = dve.tensor_scalar(x[:, t, :], x[:, t, :], g.rstd[:, t:t + 1], None, ALU.mult)
            last.then_inc(xn_ready, 1)
            dve.wait_ge(silu_ready, 1)
            for n in range(MOD_FIRST):
                dve.wait_ge(w_mod_in[n // MOD_LOAD], 16)
                mod_column(g, dve, n, w_mod[:, n, :])
            dve.wait_ge(vecs_in, 16)
            dve.drain()
            dve.tensor_tensor(g.mod[:, 0:MOD_FIRST], g.mod[:, 0:MOD_FIRST], g.vec("b_mod")[:, 0:MOD_FIRST], ALU.add)
            dve.drain()
            dve.scalar_tensor_tensor(g.scale1[:], g.mod[:, KC:2 * KC], 1.0, g.vec("g_pre_mix"), ALU.add, ALU.mult)\
               .then_inc(cols_ready, 1)
            for n in range(MOD_FIRST, early):
                dve.wait_ge(w_mod_in[n // MOD_LOAD], 16)
                mod_column(g, dve, n, w_mod[:, n, :])
            modulate_transposed(g, "a", x, hf, tp, None, None, sems, None, dve, None)

        @block.tensor
        def _(pe):
            pe.wait_ge(consts_in, 16)
            pe.wait_ge(xn_ready, 1)
            modulate_transposed(g, "a", x, hf, tp, None, None, sems, None, None, pe)


def projections(g):
    nc, i, sem = g.nc, g.i, g.sem
    g.z = g.at("z", 0, [P, QKRP, S])
    g.za = g.at("za", 48, [P, S])
    g.v = g.at("v", 52, [P, TT, GLA_HEADS * GLA_DV])
    raw = [g.at(f"w_raw{s}", 68 + 4 * s, [P, D]) for s in range(2)]
    w_hi = [g.at(f"w_hi{s}", 76 + 4 * s, [P, D], F32R) for s in range(2)]
    w_lo = [g.at(f"w_lo{s}", 84 + 4 * s, [P, D], F32R) for s in range(2)]
    wv_hi = g.at("wv_hi", 92, [P, KC, HALF], F32R)
    wv_lo = g.at("wv_lo", 108, [P, KC, HALF], F32R)
    w_mod = g.at("w_mod_b", 104, [P, MOD_PER_PAIR, D])
    spread = g.at("spread", 192, [P, KC // 2, P])
    w_mod_in = sem("w_mod_b_in")
    mod_done, cols_ready, spread_ready, rows_ps, rows_ready = (sem(n) for n in (
        "mod_b_done", "cols_b_ready", "spread_ready", "rows_ps", "rows_ready"))
    early = MOD_TILES - MOD_PER_PAIR * QKRP // 2
    raw_in = [sem(f"w_raw_in{s}") for s in range(2)]
    hi_ready, lo_ready, tile_done, tile_out = (sem(n) for n in ("w_hi_ready", "w_lo_ready", "z_done", "z_out"))
    v_done, v_out = sem("v_done"), sem("v_out")
    VP = KC * HALF // D
    LOADS = QKRP + 2 * 1 + VP
    with nc.psum_tensor("acc_b0", [P, S], F32) as acc0, nc.psum_tensor("acc_b1", [P, S], F32) as acc1, \
            nc.psum_tensor("rows", [P, HALF], F32) as rows, \
            nc.Block() as block:
        acc = [acc0, acc1]
        piece = lambda t, n: t[:, 2 * n:2 * n + 2, :].rearrange("p a b -> p (a b)")

        @block.sync
        def _(sp):
            for n in range(2):
                sp.dma_start(raw[n][:], i["w_qkrp"][n]).then_inc(raw_in[n], 16)
            late = i["w_mod"].rearrange("n p d -> p n d")
            sp.dma_start(w_mod[:], late[:, early:early + MOD_PER_PAIR, :]).then_inc(w_mod_in, 16)
            with sp.Fori(1, QKRP // 2) as r:
                for s in range(2):
                    sp.wait_ge(lo_ready, (r - 1) * 2 + s + 1)
                    sp.dma_start(raw[s][:], i["w_qkrp"][r * 2 + s]).then_inc(raw_in[s], 16)
                sp.wait_ge(mod_done, r)
                sp.dma_start(w_mod[:], late[:, bass.ds(early + r * MOD_PER_PAIR, MOD_PER_PAIR), :]).then_inc(w_mod_in, 16)
            for n in range(QKRP, QKRP + 1 + VP):
                sp.wait_ge(lo_ready, n - 1)
                src = i["w_rank"] if n == QKRP else i["w_v"][n - QKRP - 1]
                sp.dma_start(raw[n % 2][:], src).then_inc(raw_in[n % 2], 16)

        @block.scalar
        def _(act):
            def split(s, count):
                act.wait_ge(raw_in[s], count)
                split_hi(act, w_hi[s][:], raw[s][:]).then_inc(hi_ready, 1)

            def evacuate(n, s, dst):
                act.wait_ge(tile_done, n + 1)
                act.activation(dst, acc[s][:], ACT.Copy).then_inc(tile_out, 1)

            split(0, 16)
            split(1, 16)
            with act.Fori(0, QKRP // 2 - 1) as r:
                for s in range(2):
                    evacuate(2 * r + s, s, g.z[:, bass.ds(2 * r + s, 1), :])
                    split(s, (r + 2) * 16)
            evacuate(QKRP - 2, 0, g.z[:, QKRP - 2, :])
            split(0, (QKRP // 2 + 1) * 16)
            for n in range(VP):
                m = QKRP + 1 + n
                act.wait_ge(raw_in[m % 2], (m // 2 + 1) * 16)
                split_hi(act, piece(wv_hi, n), raw[m % 2][:]).then_inc(hi_ready, 1)
            evacuate(QKRP - 1, 1, g.z[:, QKRP - 1, :])
            evacuate(QKRP, 0, g.za[:])
            for t in range(TT):
                act.wait_ge(v_done, t + 1)
                act.activation(g.v[:, t, :], acc[1][:, (t % 2) * HALF:(t % 2 + 1) * HALF], ACT.Copy).then_inc(v_out, 1)

        @block.vector
        def _(dve):
            def split(n, s):
                dve.wait_ge(hi_ready, n + 1)
                split_lo(dve, w_lo[s][:], raw[s][:], w_hi[s][:]).then_inc(lo_ready, 1)

            with dve.Fori(0, QKRP // 2) as r:
                for s in range(2):
                    split(2 * r + s, s)
                dve.wait_ge(w_mod_in, (r + 1) * 16)
                for s in range(MOD_PER_PAIR):
                    last = mod_column(g, dve, early + r * MOD_PER_PAIR + s, w_mod[:, s, :])
                last.then_inc(mod_done, 1)
            split(QKRP, 0)
            dve.drain()
            for n in range(VP):
                m = QKRP + 1 + n
                dve.wait_ge(hi_ready, m + 1)
                split_lo(dve, piece(wv_lo, n), raw[m % 2][:], piece(wv_hi, n)).then_inc(lo_ready, 1)
            rest = slice(MOD_FIRST, MOD_TILES)
            dve.tensor_tensor(g.mod[:, rest], g.mod[:, rest], g.vec("b_mod")[:, rest], ALU.add)
            dve.drain()
            dve.scalar_tensor_tensor(g.scale2[:], g.mod[:, 4 * KC:5 * KC], 1.0, g.vec("g_pre_ffn"), ALU.add, ALU.mult)
            dve.tensor_tensor(g.gate_cols[:, 0:KC], g.mod[:, 2 * KC:3 * KC], g.vec("g_post_mix"), ALU.mult)
            dve.tensor_tensor(g.gate_cols[:, KC:], g.mod[:, 5 * KC:6 * KC], g.vec("g_post_ffn"), ALU.mult)
            dve.drain()
            half = KC // 2
            for n in range(4):
                gate = g.gate_cols[:, n * half:(n + 1) * half]
                dve.tensor_copy(spread[:], gate.unsqueeze(2).to_broadcast([P, half, P])).then_inc(spread_ready, 1)
                dve.wait_ge(rows_ps, n + 1)
                dve.tensor_copy(g.gate_rows[:, n // 2, n % 2 * HALF:(n % 2 + 1) * HALF], rows[:]).then_inc(rows_ready, 1)

        @block.tensor
        def _(pe):
            def make_rows(n):
                pe.wait_ge(spread_ready, n + 1)
                if n:
                    pe.wait_ge(rows_ready, n)
                for k in range(KC // 2):
                    last = pe.matmul(rows[:, k * P:(k + 1) * P], spread[:, k, :], g.ident, start=True, stop=True)
                last.then_inc(rows_ps, 1)

            with pe.Fori(0, QKRP // 2) as r:
                for s in range(2):
                    pe.wait_ge(lo_ready, 2 * r + s + 1)
                    tile_product(pe, acc[s], w_hi[s], w_lo[s], g.a_hi, g.a_lo).then_inc(tile_done, 1)
            pe.wait_ge(lo_ready, QKRP + 1)
            tile_product(pe, acc[0], w_hi[0], w_lo[0], g.a_hi, g.a_lo).then_inc(tile_done, 1)
            pe.wait_ge(lo_ready, QKRP + 1 + VP)
            pe.wait_ge(tile_out, QKRP)
            for t in range(TT):
                if t >= 2:
                    pe.wait_ge(v_out, t - 1)
                if t >= TT - 4:
                    make_rows(t - (TT - 4))
                dst = acc[1][:, (t % 2) * HALF:(t % 2 + 1) * HALF]
                for k in range(KC):
                    ah, al = g.a_hi[:, k, t * P:(t + 1) * P], g.a_lo[:, k, t * P:(t + 1) * P]
                    pe.matmul(dst, ah, wv_hi[:, k, :], start=k == 0, stop=False)
                    pe.matmul(dst, ah, wv_lo[:, k, :], start=False, stop=False)
                    last = pe.matmul(dst, al, wv_hi[:, k, :], start=False, stop=k == KC - 1)
                last.then_inc(v_done, 1)


def decays(g):
    nc, i, sem = g.nc, g.i, g.sem
    reset = g.at("reset", 68, [P, S])
    la = g.at("la", 72, [P, PAIRS, S])
    prefix = g.at("prefix", 80, [P, PAIRS, S])
    tail = g.at("tail", 88, [P, PAIRS, S])
    e_q = g.at("e_q", 96, [P, PAIRS, S])
    e_inv = g.at("e_inv", 104, [P, PAIRS, S])
    e_end = g.at("e_end", 112, [P, PAIRS, S])
    g.q_dec = [g.at(f"q_dec{d}", (187, 144)[d], [P, PAIRS, S]) for d in range(2)]
    g.k_inv = [g.at(f"k_inv{d}", 128 + 24 * d, [P, PAIRS, S]) for d in range(2)]
    g.k_end = [g.at(f"k_end{d}", 136 + 24 * d, [P, PAIRS, S]) for d in range(2)]
    g.gamma = g.at("gamma", 168, [P, 2, PAIRS, NCHUNK])
    width = S + 2 * PAD
    win = [g.at(f"win{n}", 169 + 4.125 * n, [P, width]) for n in range(2)]
    pooled = g.at("pooled", 178, [P, S])
    w_alpha = g.at("w_alpha", 182, [P, GLA_HEADS * GLA_DK])
    w_pool = g.at("w_pool", 183, [P, 4, P])
    edges = g.at("edges", 185, [P, 4, 2 * PAD])
    edge_tmp = g.at("edge_tmp", 186, [P, 2 * PAD])
    consts_in, weights_in = sem("reset_in"), sem("small_w_in")
    logits, logit_out, ln_ready, scan_ready, tail_ready, exps_ready, dir_done = (sem(n) for n in (
        "logits", "logit_out", "ln_ready", "scan_ready", "tail_ready", "exps_ready", "dir_done"))
    act_self = sem("act_self_c")
    silu_done, pooled_ready, pool_mm, pool_out = (sem(n) for n in ("silu_r", "pooled_ready", "pool_mm", "pool_out"))
    with ExitStack() as banks:
        lps = [banks.enter_context(nc.psum_tensor(f"logit{n}", [P, S], F32)) for n in range(PAIRS)]
        pps = [banks.enter_context(nc.psum_tensor(f"pool_ps{n}", [P, S], F32)) for n in range(2)]
        block = banks.enter_context(nc.Block())
        flat = lambda a: a[:].rearrange("p a b -> p (a b)")
        chunks = lambda a, pair: a[:, pair, :].rearrange("p (n c) -> p n c", c=CHUNK)
        last_of = lambda a, pair: chunks(a, pair)[:, :, CHUNK - 1:CHUNK]

        @block.sync
        def _(sp):
            sp.dma_start(w_alpha[:], i["w_alpha"]).then_inc(weights_in, 16)
            sp.dma_start(w_pool[:], i["w_pool"]).then_inc(weights_in, 16)
            sp.dma_start(reset[:], i["reset"]).then_inc(consts_in, 16)
            sp.dma_start(edges[:], i["edges"]).then_inc(consts_in, 16)

        @block.tensor
        def _(pe):
            pe.wait_ge(weights_in, 32)
            for d in range(2):
                if d:
                    pe.wait_ge(logit_out, 1)
                rows = slice(64 * d, 64 * d + RANK)
                for pair in range(PAIRS):
                    for half in range(2):
                        cols = slice(half * HALF, (half + 1) * HALF)
                        last = pe.matmul(lps[pair][:, cols], w_alpha[rows, pair * P:(pair + 1) * P], g.za[rows, cols],
                                         start=True, stop=True)
                last.then_inc(logits, 1)
            for n in range(4):
                pe.wait_ge(pooled_ready, n + 1)
                if n >= 2:
                    pe.wait_ge(pool_out, n - 1)
                for half in range(2):
                    cols = slice(half * HALF, (half + 1) * HALF)
                    last = pe.matmul(pps[n % 2][:, cols], w_pool[:, n, :], pooled[:, cols], start=True, stop=True)
                last.then_inc(pool_mm, 1)

        @block.scalar
        def _(act):
            act.activation(g.z[:, 4:8, :], g.z[:, 4:8, :], ACT.Silu).then_inc(silu_done, 1)
            for d in range(2):
                if d:
                    act.wait_ge(dir_done, d)
                act.wait_ge(logit_out, d + 1)
                act.activation(flat(e_q), flat(la), ACT.Abs)
                act.drain()
                act.activation(flat(e_q), flat(e_q), ACT.Exp, scale=-1.0)
                act.drain()
                act.activation(flat(e_end), flat(e_q), ACT.Ln, bias=1.0).then_inc(ln_ready, 1)
                act.wait_ge(scan_ready, d + 1)
                b = prefix if d == 0 else e_end
                for pair in range(PAIRS):
                    act.activation(g.gamma[:, d, pair, :], last_of(prefix, pair).squeeze(2), ACT.Exp, scale=1.0 / TAU)
                act.wait_ge(tail_ready, d + 1)
                act.activation(flat(e_q), flat(b), ACT.Exp, scale=1.0 / TAU)
                act.activation(flat(e_inv), flat(b), ACT.Exp, scale=-1.0 / TAU)
                act.drain()
                act.activation(flat(e_end), flat(tail), ACT.Exp, scale=1.0 / TAU).then_inc(exps_ready, 1)
            for n in range(4):
                act.wait_ge(pool_mm, n + 1)
                act.activation(g.z[:, 8 + n, :], pps[n % 2][:], ACT.Copy, scale=g.vec("pool_scale")[:, n:n + 1])\
                   .then_inc(pool_out, 1)

        @block.vector
        def _(dve):
            dve.wait_ge(consts_in, 32)
            for d in range(2):
                bias = g.vec("b_alpha_f" if d == 0 else "b_alpha_b")
                dve.wait_ge(logits, d + 1)
                for pair in range(PAIRS):
                    last = dve.tensor_scalar(la[:, pair, :], lps[pair][:], bias[:, pair:pair + 1], None, ALU.add)
                last.then_inc(logit_out, 1)
                dve.wait_ge(logit_out, d + 1)
                dve.wait_ge(ln_ready, d + 1)
                dve.scalar_tensor_tensor(flat(la), flat(la), 0.0, flat(e_end), ALU.min, ALU.subtract)
                dve.drain()
                for pair in range(PAIRS):
                    last = dve.tensor_tensor_scan(prefix[:, pair, :], reset[:], la[:, pair, :], 0.0, ALU.mult, ALU.add)
                last.then_inc(scan_ready, 1)
                dve.drain()
                for pair in range(PAIRS):
                    total = last_of(prefix, pair).to_broadcast([P, NCHUNK, CHUNK])
                    if d == 0:
                        last = dve.tensor_tensor(chunks(tail, pair), total, chunks(prefix, pair), ALU.subtract)
                    else:
                        dve.tensor_tensor(tail[:, pair, :], prefix[:, pair, :], la[:, pair, :], ALU.subtract)
                        dve.drain()
                        last = dve.tensor_tensor(chunks(e_end, pair), total, chunks(tail, pair), ALU.subtract)
                last.then_inc(tail_ready, 1)
                dve.wait_ge(exps_ready, d + 1)
                q, k = g.z[:, 0:2, :].rearrange("p a b -> p (a b)"), g.z[:, 2:4, :].rearrange("p a b -> p (a b)")
                dve.scalar_tensor_tensor(flat(g.q_dec[d]), q, GLA_DK ** -0.5, flat(e_q), ALU.mult, ALU.mult)
                dve.tensor_tensor(flat(g.k_inv[d]), k, flat(e_inv), ALU.mult)
                dve.tensor_tensor(flat(g.k_end[d]), k, flat(e_end), ALU.mult).then_inc(dir_done, 1)
            dve.memset(win[0][:], 0.0)
            dve.memset(win[1][:], 0.0)
            for n, w in enumerate(WINDOWS):
                p = g.z[:, 8 + n, :]
                dve.drain()
                dve.tensor_copy(win[0][:, PAD:PAD + S], p)
                src, dst, m, lo, hi = win[0], win[1], 1, 0, width
                while m < w:
                    left, right = (1, 0) if m == 1 else (m // 2, m // 2)
                    lo, hi = lo + left, hi - right
                    dve.drain()
                    dve.tensor_tensor(dst[:, lo:hi], src[:, lo - left:hi - left], src[:, lo + right:hi + right], ALU.add)
                    src, dst, m = dst, src, 2 * m
                if n:
                    dve.wait_ge(pool_mm, n)
                dve.drain()
                body = src[:, PAD:PAD + S]
                dve.scalar_tensor_tensor(pooled[:], body, 1.0 / w, p, ALU.mult, ALU.subtract)
                ends = lambda a: a[:, 0:S].rearrange("p (a b) -> p a b", b=S // 2)
                for e in range(2):
                    cols = slice(0, PAD) if e == 0 else slice(S - PAD, S)
                    dve.tensor_tensor(edge_tmp[:, e * PAD:(e + 1) * PAD], src[:, PAD + cols.start:PAD + cols.stop],
                                      edges[:, n, e * PAD:(e + 1) * PAD], ALU.mult)
                dve.drain()
                for e in range(2):
                    cols = slice(0, PAD) if e == 0 else slice(S - PAD, S)
                    last = dve.tensor_tensor(pooled[:, cols], edge_tmp[:, e * PAD:(e + 1) * PAD], p[:, cols], ALU.subtract)
                last.then_inc(pooled_ready, 1)
                if n < 3:
                    dve.drain()
                    dve.memset(win[0][:, 0:PAD], 0.0)
                    dve.memset(win[0][:, PAD + S:width], 0.0)


def attention(g):
    nc, i, sem = g.nc, g.i, g.sem
    g.o = g.at("o", 0, [P, TT, GLA_HEADS * GLA_DV])
    k_tok = [g.at(f"k_tok{d}", 68 + 8 * d, [P, TT, PAIRS * P]) for d in range(2)]
    state = g.at("state", 84, [P, 2, PAIRS, NCHUNK, GLA_DV])
    scores = [g.at(f"scores{n}", 169 + 0.5 * n, [P, P]) for n in range(4)]
    kt_ps, kt_out, upd_ps, upd_done, sc_ps, sc_out, o_ps_done, o_out = (sem(n) for n in (
        "kt_ps", "kt_out", "upd_ps", "upd_done", "sc_ps", "sc_out", "o_done", "o_out"))
    o_ssq, o_root, o_rstd = sem("o_ssq"), sem("o_root"), sem("o_rstd")
    junk = g.at("junk_o", 172, [P, GLA_DV])
    g.wo_raw = [g.at(f"wo_raw{s}", kb, [P, D]) for s, kb in enumerate((48, 116, 120, 124))]
    g.wo_in = [sem(f"wo_in{s}") for s in range(WO_RING)]
    steps = NCHUNK - 1
    with ExitStack() as banks:
        bank = lambda name: banks.enter_context(nc.psum_tensor(name, [P, 4, P], F32))
        tr = [bank(f"tr{n}") for n in range(2)]
        upd = [[bank(f"upd{d}{n}") for n in range(2)] for d in range(2)]
        ops = upd
        sps = [bank(f"sps{n}") for n in range(2)]
        block = banks.enter_context(nc.Block())
        groups = [(d, pair, q) for d in range(2) for pair in range(PAIRS) for q in range(TT // 4)]
        chunk_at = lambda d, n: n if d == 0 else NCHUNK - 1 - n

        @block.sync
        def _(sp):
            for n in range(WO_RING):
                sp.dma_start(g.wo_raw[n][:], i["w_out"][:, MIX_ORDER[n], :]).then_inc(g.wo_in[n], 16)

        @block.tensor
        def _(pe):
            for n, (d, pair, q) in enumerate(groups):
                if n >= 2:
                    pe.wait_ge(kt_out, n - 1)
                for t in range(4):
                    cols = slice((4 * q + t) * P, (4 * q + t + 1) * P)
                    last = pe.transpose(tr[n % 2][:, t, :], g.k_end[d][:, pair, cols], g.ident)
                last.then_inc(kt_ps, 1)
            pe.wait_ge(kt_out, len(groups))
            for n in range(steps):
                if n >= 2:
                    pe.wait_ge(upd_done, n - 1)
                for d in range(2):
                    c = chunk_at(d, n)
                    rows = slice(CHUNK * (c % 2), CHUNK * (c % 2) + CHUNK)
                    for pair in range(PAIRS):
                        for h in range(2):
                            head = 2 * pair + h
                            last = pe.matmul(upd[d][n % 2][h * GLA_DK:(h + 1) * GLA_DK, pair, :],
                                             k_tok[d][rows, c // 2, pair * P + h * GLA_DK:pair * P + (h + 1) * GLA_DK],
                                             g.v[rows, c // 2, head * GLA_DV:(head + 1) * GLA_DV], start=True, stop=True)
                last.then_inc(upd_ps, 1)

            def score(n):
                t, head = n // GLA_HEADS, n % GLA_HEADS
                pair, keys = head // 2, slice(GLA_DK * (head % 2), GLA_DK * (head % 2 + 1))
                cols = slice(t * P, (t + 1) * P)
                if n >= 2:
                    pe.wait_ge(sc_out, n - 1)
                for d in range(2):
                    last = pe.matmul(sps[n % 2][:, d, :], g.k_inv[d][keys, pair, cols], g.q_dec[d][keys, pair, cols],
                                     start=True, stop=True)
                last.then_inc(sc_ps, 1)

            score(0)
            for n in range(TT * GLA_HEADS):
                t, head = n // GLA_HEADS, n % GLA_HEADS
                pair, keys = head // 2, slice(GLA_DK * (head % 2), GLA_DK * (head % 2 + 1))
                if n + 1 < TT * GLA_HEADS:
                    score(n + 1)
                pe.wait_ge(sc_out, n + 1)
                if head == 0 and t >= 2:
                    pe.wait_ge(o_out, t - 1)
                if n == 0:
                    pe.wait_ge(upd_done, steps)
                cols = slice(head * GLA_DV, (head + 1) * GLA_DV)
                dst = ops[t % 2][head % 2][:, pair, :]
                pe.matmul(dst, scores[n % 4][:], g.v[:, t, cols], start=True, stop=False)
                for half in range(2):
                    c = 2 * t + half
                    rows = slice(CHUNK * half, CHUNK * (half + 1))
                    for d in range(2):
                        last = pe.matmul(dst[rows, :], g.q_dec[d][keys, pair, c * CHUNK:(c + 1) * CHUNK],
                                         state[keys, d, pair, c, :], start=False, stop=d == 1)
                if head == GLA_HEADS - 1:
                    last.then_inc(o_ps_done, 1)

        @block.vector
        def _(dve):
            for n, (d, pair, q) in enumerate(groups):
                dve.wait_ge(kt_ps, n + 1)
                dve.tensor_copy(k_tok[d][:, 4 * q:4 * q + 4, pair * P:(pair + 1) * P], tr[n % 2][:]).then_inc(kt_out, 1)
            for n in range(4):
                dve.memset(scores[n][:], 0.0)
            for d in range(2):
                dve.memset(state[:, d, :, chunk_at(d, 0), :], 0.0)
            dve.drain()
            for n in range(steps):
                dve.wait_ge(upd_ps, n + 1)
                for d in range(2):
                    c, nxt = chunk_at(d, n), chunk_at(d, n + 1)
                    for pair in range(PAIRS):
                        last = dve.scalar_tensor_tensor(state[:, d, pair, nxt, :], state[:, d, pair, c, :],
                                                        g.gamma[:, d, pair, c:c + 1], upd[d][n % 2][:, pair, :],
                                                        ALU.mult, ALU.add)
                last.then_inc(upd_done, 1)
                dve.drain()
            def invert(t):
                dve.wait_ge(o_root, t + 1)
                cols = slice(t * GLA_HEADS, (t + 1) * GLA_HEADS)
                dve.reciprocal(g.rstd[:, cols], g.rstd[:, cols]).then_inc(o_rstd, 1)

            for n in range(TT * GLA_HEADS):
                if n > 4 and n % 4 == 3:
                    invert(n // 4 - 1)
                dve.wait_ge(sc_ps, n + 1)
                dve.copy_predicated(scores[n % 4][:], g.mask_f.bitcast(U32), sps[n % 2][:, 0, :])
                dve.drain()
                dve.copy_predicated(scores[n % 4][:], g.mask_b.bitcast(U32), sps[n % 2][:, 1, :]).then_inc(sc_out, 1)
            invert(TT - 1)

        @block.scalar
        def _(act):
            for t in range(TT):
                act.wait_ge(o_ps_done, t + 1)
                for head in range(GLA_HEADS):
                    n = t * GLA_HEADS + head
                    if n:
                        act.wait_ge(o_ssq, n)
                    act.activation(junk[:], ops[t % 2][head % 2][:, head // 2, :], ACT.Square,
                                   accum_out=g.ssq[:, n:n + 1]).then_inc(o_ssq, 1)
                act.wait_ge(o_ssq, (t + 1) * GLA_HEADS)
                cols = slice(t * GLA_HEADS, (t + 1) * GLA_HEADS)
                act.activation(g.rstd[:, cols], g.ssq[:, cols], ACT.Sqrt, scale=1.0 / GLA_DV, bias=g.eps[:]).then_inc(o_root, 1)
                act.wait_ge(o_rstd, t + 1)
                for head in range(GLA_HEADS):
                    n = t * GLA_HEADS + head
                    last = act.activation(g.o[:, t, head * GLA_DV:(head + 1) * GLA_DV], ops[t % 2][head % 2][:, head // 2, :],
                                          ACT.Copy, scale=g.rstd[:, n:n + 1])
                last.then_inc(o_out, 1)


MIX_ORDER = (4, 5, 6, 7, 0, 1, 2, 3)
WO_RING = 4


def mix_out(g):
    nc, i, sem = g.nc, g.i, g.sem
    m_hi, m_lo = g.a_hi, g.a_lo
    mf = [g.at(f"mf{k}", 160 + 4 * k, [P, S]) for k in range(GLA_HEADS)]
    wo_hi = g.at("wo_hi", 52, [P, KC, D], F32R)
    wo_lo = g.at("wo_lo", 84, [P, KC, D], F32R)
    raw, wo_in = g.wo_raw, g.wo_in
    xn = [g.at(f"xn{s}", 4 * s, [P, D]) for s in range(2)]
    xt = [g.at(f"xt{s}", 8 + 4 * s, [P, D]) for s in range(2)]
    junk = g.at("junk_e", 16, [P, D])
    junk_v = g.at("junk_v", 20, [P, D])
    hf = [g.at(f"hf_e{s}", 24 + 4 * s, [P, KC, P]) for s in range(2)]
    retrieval_weights(g)
    xt_in = [sem(f"xt_in{s}") for s in range(2)]
    x1_stored = [sem(f"x1_stored{s}") for s in range(2)]
    wo_hi_ready, wo_lo_ready, ot_ps, mf_ready, m_hi_ready, pooled_lo, heads_lo, mixed = (
        sem(n) for n in ("wo_hi_r", "wo_lo_r", "ot_ps", "mf_ready", "m_hi_r", "pooled_lo", "heads_lo", "mixed"))
    mix_root, x1_ready, x1_root, xn_done, xt_ps, hf_ready, a_hi_ready, a_ready = (sem(n) for n in (
        "mix_root", "x1_ready", "x1_root", "xn_done", "xt_ps", "hf_ready", "a_hi_ready", "a_ready"))
    act_self = sem("act_self_e")
    with ExitStack() as banks:
        otp = [banks.enter_context(nc.psum_tensor(f"otp{n}", [P, KC, P], F32)) for n in range(2)]
        mps = [banks.enter_context(nc.psum_tensor(f"mps{n}", [P, D], F32)) for n in range(2)]
        block = banks.enter_context(nc.Block())
        flat = lambda a: a[:].rearrange("p a b -> p (a b)")

        @block.sync
        def _(sp):
            for n in range(WO_RING, KC):
                sp.wait_ge(wo_lo_ready, n - WO_RING + 1)
                sp.dma_start(raw[n % WO_RING][:], i["w_out"][:, MIX_ORDER[n], :]).then_inc(wo_in[n % WO_RING], 16)
            sp.wait_ge(ot_ps, GLA_HEADS)
            for t in range(TT):
                if t >= 2:
                    sp.wait_ge(xn_done, t - 1)
                    sp.wait_ge(x1_stored[t % 2], 16 * (t // 2))
                sp.dma_start(xt[t % 2][:], i["x"][t * P:(t + 1) * P, :]).then_inc(xt_in[t % 2], 16)
                if t == 2:
                    sp.wait_ge(wo_lo_ready, KC)
                    for s in range(2):
                        sp.dma_start(g.wq_raw[s][:], i["w_q"][s]).then_inc(g.wq_in[s], 16)
                if t >= 1:
                    sp.wait_ge(x1_ready, t)
                    sp.dma_start(g.x1_d[t - 1], xt[(t - 1) % 2][:]).then_inc(x1_stored[(t - 1) % 2], 16)
            sp.wait_ge(x1_ready, TT)
            sp.dma_start(g.x1_d[TT - 1], xt[(TT - 1) % 2][:]).then_inc(x1_stored[(TT - 1) % 2], 16)
            for s in range(2):
                sp.wait_ge(x1_stored[s], 16 * TT // 2)

        @block.gpsimd
        def _(pool):
            for n in range(KC - GLA_HEADS):
                k = MIX_ORDER[n]
                pool.wait_ge(m_hi_ready, n + 1)
                split_lo(pool, m_lo[:, k, :], g.z[:, 4 + k, :], m_hi[:, k, :]).then_inc(pooled_lo, 1)

        @block.scalar
        def _(act):
            for n, k in enumerate(MIX_ORDER):
                act.wait_ge(wo_in[n % WO_RING], 16 * (n // WO_RING + 1))
                split_hi(act, wo_hi[:, k, :], raw[n % WO_RING][:]).then_inc(wo_hi_ready, 1)
                if k < GLA_HEADS:
                    act.wait_ge(mf_ready, k + 1)
                split_hi(act, m_hi[:, k, :], mf[k][:] if k < GLA_HEADS else g.z[:, 4 + k, :]).then_inc(m_hi_ready, 1)

            def modulate(t):
                act.wait_ge(xt_ps, t + 1)
                if t >= 2:
                    act.wait_ge(a_ready, t - 1)
                for k in range(KC):
                    last = act.activation(hf[t % 2][:, k, :], otp[t % 2][:, k, :], ACT.Identity,
                                          bias=g.mod[:, 3 * KC + k:3 * KC + k + 1], scale=g.scale2[:, k:k + 1])
                last.then_inc(hf_ready, 1)
                act.wait_ge(hf_ready, t + 1)
                split_hi(act, g.a_hi[:, :, t * P:(t + 1) * P], hf[t % 2][:]).then_inc(a_hi_ready, 1)

            for t in range(TT):
                act.wait_ge(mixed, t + 1)
                act.activation(junk[:], mps[t % 2][:], ACT.Square, accum_out=g.ssq[:, 2 * t:2 * t + 1]).then_inc(act_self, 1)
                act.wait_ge(act_self, 2 * t + 1)
                act.activation(g.rstd[:, 2 * t:2 * t + 1], g.ssq[:, 2 * t:2 * t + 1], ACT.Sqrt, scale=1.0 / D,
                               bias=g.eps[:]).then_inc(mix_root, 1)
                act.wait_ge(x1_ready, t + 1)
                act.activation(junk[:], xt[t % 2][:], ACT.Square, accum_out=g.ssq[:, 2 * t + 1:2 * t + 2]).then_inc(act_self, 1)
                act.wait_ge(act_self, 2 * t + 2)
                act.activation(g.rstd[:, 2 * t + 1:2 * t + 2], g.ssq[:, 2 * t + 1:2 * t + 2], ACT.Sqrt, scale=1.0 / D,
                               bias=g.eps[:]).then_inc(x1_root, 1)
                if t:
                    modulate(t - 1)
                if t in (3, 4):
                    split_query(g, act, t - 3)
            modulate(TT - 1)

        @block.vector
        def _(dve):
            for k in range(GLA_HEADS):
                dve.wait_ge(ot_ps, k + 1)
                dve.scalar_tensor_tensor(mf[k][:], flat(otp[k % 2]), g.vec("g_gla_head")[:, k:k + 1], g.z[:, 4 + k, :],
                                         ALU.mult, ALU.mult).then_inc(mf_ready, 1)
            for n, k in enumerate(MIX_ORDER):
                dve.wait_ge(wo_hi_ready, n + 1)
                split_lo(dve, wo_lo[:, k, :], raw[n % WO_RING][:], wo_hi[:, k, :]).then_inc(wo_lo_ready, 1)
                if k < GLA_HEADS:
                    dve.wait_ge(m_hi_ready, n + 1)
                    split_lo(dve, m_lo[:, k, :], mf[k][:], m_hi[:, k, :]).then_inc(heads_lo, 1)

            def modulated(t):
                dve.wait_ge(a_hi_ready, t + 1)
                cols = slice(t * P, (t + 1) * P)
                split_lo(dve, g.a_lo[:, :, cols], hf[t % 2][:], g.a_hi[:, :, cols]).then_inc(a_ready, 1)

            for t in range(TT):
                dve.wait_ge(mix_root, t + 1)
                dve.reciprocal(g.rstd[:, 2 * t:2 * t + 1], g.rstd[:, 2 * t:2 * t + 1])
                dve.drain()
                dve.scalar_tensor_tensor(junk_v[:], mps[t % 2][:], g.rstd[:, 2 * t:2 * t + 1], g.gate_rows[:, 0, :],
                                         ALU.mult, ALU.mult)
                dve.drain()
                dve.wait_ge(xt_in[t % 2], 16 * (t // 2 + 1))
                dve.tensor_tensor(xt[t % 2][:], xt[t % 2][:], junk_v[:], ALU.add).then_inc(x1_ready, 1)
                dve.wait_ge(x1_root, t + 1)
                dve.reciprocal(g.rstd[:, 2 * t + 1:2 * t + 2], g.rstd[:, 2 * t + 1:2 * t + 2])
                dve.drain()
                if t >= 2:
                    dve.wait_ge(xt_ps, t - 1)
                dve.tensor_scalar(xn[t % 2][:], xt[t % 2][:], g.rstd[:, 2 * t + 1:2 * t + 2], None, ALU.mult)\
                   .then_inc(xn_done, 1)
                if t:
                    modulated(t - 1)
                if t in (3, 4):
                    split_query_lo(g, dve, t - 3)
            modulated(TT - 1)

        @block.tensor
        def _(pe):
            for h in range(GLA_HEADS):
                if h >= 2:
                    pe.wait_ge(mf_ready, h - 1)
                for t in range(TT):
                    last = pe.transpose(otp[h % 2][:, t, :], g.o[:, t, h * GLA_DV:(h + 1) * GLA_DV], g.ident)
                last.then_inc(ot_ps, 1)

            def part(t, k, first, final):
                cols = slice(t * P, (t + 1) * P)
                for m, w, start, stop in ((m_hi, wo_hi, first, False), (m_hi, wo_lo, False, False), (m_lo, wo_hi, False, final)):
                    for half in range(2):
                        out = slice(half * HALF, (half + 1) * HALF)
                        last = pe.matmul(mps[t % 2][:, out], m[:, k, cols], w[:, k, out], start=start, stop=stop)
                return last

            def transpose_xn(t):
                pe.wait_ge(xn_done, t + 1)
                if t >= 2:
                    pe.wait_ge(hf_ready, t - 1)
                else:
                    pe.wait_ge(mf_ready, GLA_HEADS)
                for k in range(KC):
                    last = pe.transpose(otp[t % 2][:, k, :], xn[t % 2][:, k * P:(k + 1) * P], g.ident)
                last.then_inc(xt_ps, 1)

            for n, k in enumerate(MIX_ORDER):
                pe.wait_ge(wo_lo_ready, n + 1)
                if k < GLA_HEADS:
                    pe.wait_ge(heads_lo, k + 1)
                else:
                    pe.wait_ge(pooled_lo, n + 1)
                for t in range(2):
                    last = part(t, k, n == 0, n == KC - 1)
                    if n == KC - 1:
                        last.then_inc(mixed, 1)
            for t in range(2, TT):
                pe.wait_ge(x1_ready, t - 1)
                for n, k in enumerate(MIX_ORDER):
                    last = part(t, k, n == 0, n == KC - 1)
                last.then_inc(mixed, 1)
                transpose_xn(t - 2)
            transpose_xn(TT - 2)
            transpose_xn(TT - 1)


def retrieval_weights(g):
    g.wq_raw = [g.at(f"wq_raw{s}", 116 + 4 * s, [P, D]) for s in range(2)]
    g.wq_hi = [g.at(f"wq_hi{s}", 32 + 4 * s, [P, D], F32R) for s in range(2)]
    g.wq_lo = [g.at(f"wq_lo{s}", 40 + 4 * s, [P, D], F32R) for s in range(2)]
    g.wq_in = [g.sem(f"wq_in{s}") for s in range(2)]
    g.wq_hi_ready, g.wq_lo_ready = g.sem("wq_hi_r"), g.sem("wq_lo_r")


def split_query(g, act, s):
    act.wait_ge(g.wq_in[s], 16)
    split_hi(act, g.wq_hi[s][:], g.wq_raw[s][:]).then_inc(g.wq_hi_ready, 1)


def split_query_lo(g, dve, s):
    dve.wait_ge(g.wq_hi_ready, s + 1)
    split_lo(dve, g.wq_lo[s][:], g.wq_raw[s][:], g.wq_hi[s][:]).then_inc(g.wq_lo_ready, 1)


def topk_buffers(g):
    g.s_work = g.at("s_work", 96, [P, 2, NKEYS])
    g.s_rest = g.at("s_rest", 97, [P, 2, NKEYS])
    g.cand = g.at("cand", 98, [P, TOPK, TOPK])
    g.cand_rest = g.at("cand_rest", 99, [P, TOPK, TOPK])
    g.match = g.at("match", 100, [P, 2, TOPK, TOPK])
    g.chosen = g.at("chosen", 102, [P, 2, HEADS, TOPK])
    g.top_all = g.at("top_all", 103, [P, HEADS, TOPK])
    g.vals = g.at("vals", 103.5, [P, 2, TOPK])
    g.tops = g.at("tops", 103.625, [P, TOPK])
    g.idx = g.at("idx", 103.6875, [P, 2, TOPK], U32)
    g.pos = g.at("pos", 103.8125, [P, TOPK], U32)
    g.hilo = g.at("hilo", 103.875, [P, 2, TOPK], U32)
    g.gates = g.at("gates", 192, [P, HEADS, TOPK])
    g.norm = g.at("norm", 192.5, [P, HEADS])
    g.gate_hi = g.at("gate_hi", 194.75, [P, P], F32R)
    g.slots = g.at("slots", 192.75, [P, 4, P])


def topk_head(g, dve, h, topk_done):
    flat = lambda a: a.rearrange("p a b -> p (a b)")
    for p in range(2):
        dve.max(g.vals[:, p, 0:8], g.s_work[:, p, :])
    dve.drain()
    for p in range(2):
        dve.max_index(g.idx[:, p, 0:8], g.vals[:, p, 0:8], g.s_work[:, p, :])
        dve.match_replace(g.s_rest[:, p, :], g.vals[:, p, 0:8], g.s_work[:, p, :], LOWEST)
    dve.drain()
    for p in range(2):
        dve.max(g.vals[:, p, 8:16], g.s_rest[:, p, :])
    dve.drain()
    for p in range(2):
        dve.max_index(g.idx[:, p, 8:16], g.vals[:, p, 8:16], g.s_rest[:, p, :])
    dve.tensor_tensor(g.cand[:], g.vals[:, 0, :].unsqueeze(2).to_broadcast([P, TOPK, TOPK]),
                      g.vals[:, 1, :].unsqueeze(1).to_broadcast([P, TOPK, TOPK]), ALU.add)
    dve.drain()
    cand, rest = flat(g.cand[:]), flat(g.cand_rest[:])
    dve.max(g.tops[:, 0:8], cand)
    dve.drain()
    dve.max_index(g.pos[:, 0:8], g.tops[:, 0:8], cand)
    dve.match_replace(rest, g.tops[:, 0:8], cand, LOWEST)
    dve.drain()
    dve.max(g.tops[:, 8:16], rest)
    dve.drain()
    dve.max_index(g.pos[:, 8:16], g.tops[:, 8:16], rest)
    dve.tensor_copy(g.top_all[:, bass.ds(h, 1), :], g.tops[:].unsqueeze(1))
    dve.drain()
    dve.tensor_scalar(g.hilo[:, 0, :], g.pos[:], 4, None, ALU.logical_shift_right)
    dve.tensor_scalar(g.hilo[:, 1, :], g.pos[:], TOPK - 1, None, ALU.bitwise_and)
    dve.drain()
    full = [P, 2, TOPK, TOPK]
    dve.tensor_tensor(g.match[:], g.hilo[:].unsqueeze(3).to_broadcast(full),
                      g.iota[:, 0:TOPK].unsqueeze(1).unsqueeze(1).to_broadcast(full), ALU.is_equal)
    dve.drain()
    dve.tensor_tensor(g.match[:], g.match[:], g.idx[:].unsqueeze(2).to_broadcast(full), ALU.mult)
    dve.drain()
    dve.tensor_reduce(g.chosen[:, :, bass.ds(h, 1), :].rearrange("p a b c -> p a (b c)") if isinstance(h, int) else
                      g.chosen[:, :, bass.ds(h, 1), :], g.match[:], AX, ALU.add).then_inc(topk_done, 1)


def finish_topk(g, dve, n, shifted, exps, slots_ready):
    dve.drain()
    dve.tensor_tensor(g.gates[:], g.top_all[:], g.top_all[:, :, 0:1].to_broadcast([P, HEADS, TOPK]), ALU.subtract)\
       .then_inc(shifted, 1)
    dve.wait_ge(exps, n + 1)
    dve.tensor_reduce(g.norm[:], g.gates[:], AX, ALU.add)
    dve.drain()
    dve.reciprocal(g.norm[:], g.norm[:])
    dve.drain()
    dve.tensor_tensor(g.gates[:], g.gates[:], g.norm[:].unsqueeze(2).to_broadcast([P, HEADS, TOPK]), ALU.mult)\
       .then_inc(slots_ready, 1)


def retrieval_scores(g):
    nc, i, sem = g.nc, g.i, g.sem
    raw, w_hi, w_lo, raw_in, hi_ready, lo_ready = g.wq_raw, g.wq_hi, g.wq_lo, g.wq_in, g.wq_hi_ready, g.wq_lo_ready
    q = [g.at(f"q{s}", 4 * s, [P, S]) for s in range(2)]
    keys = g.at("keys", 8, [P, QTILES, NKEYS])
    stage = [g.at(f"stage{s}", 16 + 4 * s, [P, TT, NKEYS]) for s in range(2)]
    topk_buffers(g)
    keys_in = sem("keys_in")
    s_stored = [sem(f"s_stored{s}") for s in range(2)]
    q_done, q_out, s_done, s_out, stage_free = (sem(n) for n in (
        "q_done", "q_out", "s_done", "s_out", "stage_free"))
    topk_done = sem("topk_first")
    g.shifted, g.exps, g.slots_ready = sem("shifted"), sem("exps"), sem("slots_ready")
    s_view = g.s_d.rearrange("(t h) p m n -> p t h m n", h=HEADS)
    with ExitStack() as banks:
        acc = [banks.enter_context(nc.psum_tensor(f"acc_q{n}", [P, S], F32)) for n in range(2)]
        sps = [banks.enter_context(nc.psum_tensor(f"s_ps{n}", [P, TT, NKEYS], F32)) for n in range(2)]
        block = banks.enter_context(nc.Block())

        @block.sync
        def _(sp):
            sp.dma_start(keys[:], i["keys"]).then_inc(keys_in, 16)
            sp.sem_inc(stage_free, 2)

            def store(r):
                for s in range(2):
                    sp.wait_ge(s_out, 2 * r + s + 1)
                    sp.dma_start(s_view[:, :, bass.ds(r, 1), s, :], stage[s][:].unsqueeze(2)).then_inc(s_stored[s], 16)
                for s in range(2):
                    sp.wait_ge(s_stored[s], (r + 1) * 16)
                    sp.sem_inc(stage_free, 1)

            with sp.Fori(0, HEADS - 1) as r:
                for s in range(2):
                    sp.wait_ge(lo_ready, 2 * r + s + 1)
                    sp.dma_start(raw[s][:], i["w_q"][2 * (r + 1) + s]).then_inc(raw_in[s], 16)
                store(r)
            store(HEADS - 1)

        @block.scalar
        def _(act):
            def split(s, count):
                act.wait_ge(raw_in[s], count)
                split_hi(act, w_hi[s][:], raw[s][:]).then_inc(hi_ready, 1)

            def evacuate(n, s):
                act.wait_ge(q_done, n + 1)
                act.activation(q[s][:], acc[s][:], ACT.Copy).then_inc(q_out, 1)

            with act.Fori(0, HEADS - 1) as r:
                for s in range(2):
                    evacuate(2 * r + s, s)
                    split(s, (r + 2) * 16)
            evacuate(QTILES - 2, 0)
            evacuate(QTILES - 1, 1)
            act.wait_ge(g.shifted, 1)
            act.activation(g.gates[:], g.gates[:], ACT.Exp).then_inc(g.exps, 1)

        @block.vector
        def _(dve):
            def split(n, s):
                dve.wait_ge(hi_ready, n + 1)
                split_lo(dve, w_lo[s][:], raw[s][:], w_hi[s][:]).then_inc(lo_ready, 1)

            def scores_out(n, s):
                dve.wait_ge(s_done, n + 1)
                dve.wait_ge(stage_free, n + 1)
                dve.tensor_copy(stage[s][:], sps[s][:]).then_inc(s_out, 1)
                dve.tensor_copy(g.s_work[:, s, :], sps[s][:, 0, :])

            with dve.Fori(0, HEADS - 1) as r:
                for s in range(2):
                    scores_out(2 * r + s, s)
                    split(2 * (r + 1) + s, s)
                dve.drain()
                topk_head(g, dve, r, topk_done)
            for s in range(2):
                scores_out(QTILES - 2 + s, s)
            dve.drain()
            topk_head(g, dve, HEADS - 1, topk_done)
            finish_topk(g, dve, 0, g.shifted, g.exps, g.slots_ready)

        @block.tensor
        def _(pe):
            pe.wait_ge(keys_in, 16)
            with pe.Fori(0, HEADS) as r:
                for s in range(2):
                    n = 2 * r + s
                    pe.wait_ge(lo_ready, n + 1)
                    tile_product(pe, acc[s], w_hi[s], w_lo[s], g.a_hi, g.a_lo).then_inc(q_done, 1)
                    pe.wait_ge(q_out, n + 1)
                    for t in range(TT):
                        last = pe.matmul(sps[s][:, t, :], q[s][:, t * P:(t + 1) * P], keys[:, bass.ds(n, 1), :],
                                         start=True, stop=True)
                    last.then_inc(s_done, 1)


ROUNDS = S // HALF
RT = TT // ROUNDS
RING = 4
GROUP = 4
UNROLL = 2 * GROUP


def sweep_2_loads(g):
    g.gt = [g.at(f"gt{s}", 32 + 8 * s, [P, HALF // GTOK, GROUP, GTOK]) for s in range(2)]
    g.act_in = [g.at(f"at{s}", 48 + 2 * s, [P, HALF]) for s in range(RING)]
    g.v_raw = [g.at(f"v_raw{s}", (56, 60, 96, 100)[s], [P, D]) for s in range(RING)]
    g.v_in, g.act_in_sem = ([g.sem(f"{n}{s}") for s in range(RING)] for n in ("v_in", "at_in"))
    g.gt_in = [g.sem(f"gt_in{s}") for s in range(2)]


def load_expert(g, sp, r, n, s):
    if s % GROUP == 0:
        per = HALF // GTOK
        gates = g.gate_d[r * per:(r + 1) * per, :, bass.ds(n, GROUP), :]
        sp.dma_start(g.gt[s // GROUP][:], gates.rearrange("j p n t -> p j n t")).then_inc(g.gt_in[s // GROUP], 16)
    sp.dma_start(g.act_in[s % RING][:], g.act_d[n][:, r * HALF:(r + 1) * HALF]).then_inc(g.act_in_sem[s % RING], 16)
    sp.dma_start(g.v_raw[s % RING][:], g.i["v"][n]).then_inc(g.v_in[s % RING], 16)


def expert_sweep_1(g):
    nc, i, sem = g.nc, g.i, g.sem
    raw = [g.at(f"u_raw{s}", 4 * s, [P, D]) for s in range(2)]
    w_hi = [g.at(f"u_hi{s}", 8 + 4 * s, [P, D], F32R) for s in range(2)]
    w_lo = [g.at(f"u_lo{s}", 16 + 4 * s, [P, D], F32R) for s in range(2)]
    gelu = [g.at(f"gelu{s}", 24 + 4 * s, [P, S]) for s in range(2)]
    gate_block = [g.at(f"gate_block{s}", 32 + 32 * s, [P, NKEYS, GTOK]) for s in range(2)]
    onehot_1 = [g.at(f"onehot_1{u}", 104 + 12 * u, [P, TOK // 2, NKEYS], F32R) for u in range(2)]
    onehot_2 = [g.at(f"onehot_2{u}", 108 + 12 * u, [P, TOK // 2, 2, NKEYS], F32R) for u in range(2)]
    raw_in = [sem(f"u_raw_in{s}") for s in range(2)]
    act_stored = [sem(f"act_stored{s}") for s in range(2)]
    g.gate_block_last = gate_block[1]
    sweep_2_loads(g)
    s_in = sem("s_in")
    gate_stored = g.gate_stored = [sem(f"gate_stored{s}") for s in range(2)]
    hi_ready, lo_ready, tile_done, gelu_done, gelu_free = (sem(n) for n in (
        "u_hi_r", "u_lo_r", "u_done", "gelu_done", "gelu_free"))
    high_out = sem("high_out")
    topk_done, slots_ps, slots_out, eq_ready, onehot_ready, gate_ps, gate_out = (
        sem(n) for n in ("topk_done", "slots_ps", "slots_out", "eq_ready", "onehot_ready", "gate_ps", "gate_out"))
    BANKS = 4
    PER = TOK // 2 // BANKS
    BANK_ORDER = [*range(1, BANKS), 0]
    with ExitStack() as banks:
        acc = [banks.enter_context(nc.psum_tensor(f"acc_u{n}", [P, S], F32)) for n in range(2)]
        gps_all = banks.enter_context(nc.psum_tensor("gate_ps", [P, TOK // 2, 2, NKEYS], F32))
        gps = [gps_all[:, n * PER:(n + 1) * PER] for n in range(BANKS)]
        block = banks.enter_context(nc.Block())

        def gate_columns(h, half, u):
            first = (h - half * BLOCK_STEPS) * TOK + u * TOK // 2
            return gate_block[half][:, :, bass.ds(first, TOK // 2)].rearrange("p n t -> p t n")

        def run(eng, step, after_block=lambda j, half: None, peel=1):
            def tile(j, topk, load_last):
                for half in range(2):
                    peeled = half
                    with eng.Fori(half * BLOCK_STEPS, (half + 1) * BLOCK_STEPS - peeled) as h:
                        step(j, h, half, j * HEADS + h, topk, True, False)
                    if peeled:
                        step(j, HEADS - 1, half, j * HEADS + HEADS - 1, topk, load_last, topk)
                    after_block(j, half)

            with eng.Fori(0, TT - peel) as j:
                tile(j, True, True)
            for j in range(TT - peel, TT):
                tile(j, j < TT - 1, j < TT - 1)

        @block.sync
        def _(sp):
            for s in range(2):
                sp.dma_start(raw[s][:], i["u"][s]).then_inc(raw_in[s], 16)
            sp.sem_inc(gelu_free, 2)
            for s in range(2):
                sp.sem_inc(gate_stored[s], 16)

            sp.dma_start(g.s_work[:], g.s_d[HEADS]).then_inc(s_in, 16)

            def step(j, h, half, b, topk, more, switch):
                if more:
                    for s in range(2):
                        sp.wait_ge(lo_ready, 2 * b + s + 1)
                        sp.dma_start(raw[s][:], i["u"][2 * (b + 1) + s]).then_inc(raw_in[s], 16)
                else:
                    sp.wait_ge(gate_stored[0], (TT + 1) * 16)
                    for n in range(RING):
                        load_expert(g, sp, 0, n, n)
                for s in range(2):
                    sp.wait_ge(gelu_done, 2 * b + s + 1)
                    sp.dma_start(g.act_d[2 * b + s], gelu[s][:]).then_inc(act_stored[s], 16)
                if topk and not (switch and isinstance(j, int)):
                    sp.wait_ge(topk_done, b + 1)
                    sp.dma_start(g.s_work[:], g.s_d[b + HEADS + 1]).then_inc(s_in, 16)
                for s in range(2):
                    sp.wait_ge(act_stored[s], (b + 1) * 16)
                    sp.sem_inc(gelu_free, 1)

            def after_block(j, half):
                if not (isinstance(j, int) and j == TT - 1 and half):
                    sp.wait_ge(gate_out, 2 * (j * HEADS + (half + 1) * BLOCK_STEPS) + 1)
                    sp.dma_start(g.gate_d[2 * j + half], gate_block[half][:]).then_inc(gate_stored[half], 16)

            run(sp, step, after_block, peel=2)

        @block.gpsimd
        def _(pool):
            def step(j, h, half, b, topk, more, switch):
                for u in range(2):
                    pool.wait_ge(eq_ready, 2 * b + u + 1)
                    for part in (1, 0):
                        gate = g.slots[:, 2 + part, bass.ds(h * TOK + u * TOK // 2, TOK // 2)]
                        last = pool.tensor_tensor(onehot_2[u][:, :, part, :], onehot_2[u][:, :, 0, :].bitcast(F32),
                                                  gate.unsqueeze(2).to_broadcast([P, TOK // 2, NKEYS]), ALU.mult)
                    last.then_inc(onehot_ready, 1)

            run(pool, step)

        @block.scalar
        def _(act):
            def split(s, count):
                act.wait_ge(raw_in[s], count)
                split_hi(act, w_hi[s][:], raw[s][:]).then_inc(hi_ready, 1)

            split(0, 16)
            split(1, 16)

            def step(j, h, half, b, topk, more, switch):
                for s in range(2):
                    act.wait_ge(tile_done, 2 * b + s + 1)
                    act.wait_ge(gelu_free, 2 * b + s + 1)
                    act.activation(gelu[s][:], acc[s][:], ACT.Gelu).then_inc(gelu_done, 1)
                    if s == 0:
                        act.wait_ge(gate_stored[half], (j + 1) * 16)
                    act.wait_ge(gate_ps, 2 * BANKS * (b + 1) + (s + 1) * BANKS)
                    act.activation(gate_columns(h, half, s), gps_all[:, :, 0, :], ACT.Copy).then_inc(high_out, 1)
                    if more:
                        split(s, (b + 2) * 16)
                    if switch and s == 0:
                        act.wait_ge(g.shifted, j + 2)
                        act.activation(g.gates[:], g.gates[:], ACT.Exp).then_inc(g.exps, 1)

            run(act, step)

        @block.vector
        def _(dve):
            def split(n, s):
                dve.wait_ge(hi_ready, n + 1)
                split_lo(dve, w_lo[s][:], raw[s][:], w_hi[s][:]).then_inc(lo_ready, 1)

            def take_slots(turn):
                dve.wait_ge(slots_ps, turn)
                dve.tensor_copy(g.slots[:, 0:2, :], gps[0][:, 0, :, :])
                dve.tensor_copy(g.slots[:, 3, :], gps[0][:, 1, 0, :]).then_inc(slots_out, 1)
                dve.drain()
                dve.tensor_copy(g.gate_hi[:], g.slots[:, 3, :])
                dve.drain()
                dve.tensor_tensor(g.slots[:, 3, :], g.slots[:, 3, :], g.gate_hi[:].bitcast(F32), ALU.subtract)
                dve.tensor_copy(g.slots[:, 2, :], g.gate_hi[:].bitcast(F32))
                dve.drain()

            dve.sem_inc(gate_out, 1)
            split(0, 0)
            split(1, 1)
            take_slots(1)

            def step(j, h, half, b, topk, more, switch):
                def compare(u):
                    dve.wait_ge(gate_ps, 2 * BANKS * b + (u + 1) * BANKS)
                    for n, rows in enumerate((onehot_1[u][:], onehot_2[u][:, :, 0, :])):
                        chosen = g.slots[:, n, bass.ds(h * TOK + u * TOK // 2, TOK // 2)]
                        last = dve.tensor_tensor(rows, g.iota.unsqueeze(1).to_broadcast([P, TOK // 2, NKEYS]),
                                                 chosen.unsqueeze(2).to_broadcast([P, TOK // 2, NKEYS]), ALU.is_equal)
                    last.then_inc(eq_ready, 1)

                def gates_out(u):
                    dve.wait_ge(high_out, 2 * b + u + 1)
                    dst = gate_columns(h, half, u)
                    dve.tensor_tensor(dst, dst, gps_all[:, :, 1, :], ALU.add).then_inc(gate_out, 1)

                if topk:
                    dve.wait_ge(s_in, (b + 1) * 16)
                compare(0)
                if topk:
                    topk_head(g, dve, h, topk_done)
                if switch:
                    finish_topk(g, dve, j + 1, g.shifted, g.exps, g.slots_ready)
                gates_out(0)
                compare(1)
                if more:
                    split(2 * (b + 1), 0)
                if switch:
                    dve.wait_ge(onehot_ready, 2 * b + 2)
                    take_slots(j + 2)
                gates_out(1)
                if more:
                    split(2 * (b + 1) + 1, 1)

            run(dve, step)

        @block.tensor
        def _(pe):
            flat = lambda a: a.rearrange("p a b -> p (a b)")

            def transpose_slots():
                for n, src in enumerate((flat(g.chosen[:, 0]), flat(g.chosen[:, 1]), flat(g.gates[:]))):
                    last = pe.transpose(gps[0][:, n // 2, n % 2, :], src, g.ident)
                last.then_inc(slots_ps, 1)

            pe.sem_inc(gate_ps, 2 * BANKS)
            pe.wait_ge(g.slots_ready, 1)
            transpose_slots()

            def step(j, h, half, b, topk, more, switch):
                for s in range(2):
                    pe.wait_ge(lo_ready, 2 * b + s + 1)
                    tile_product(pe, acc[s], w_hi[s], w_lo[s], g.a_hi, g.a_lo).then_inc(tile_done, 1)
                    pe.wait_ge(gate_out, 2 * b + s + 1)
                    if switch and s:
                        pe.wait_ge(g.slots_ready, j + 2)
                        transpose_slots()
                    pe.wait_ge(onehot_ready, 2 * b + s + 1)
                    for n in BANK_ORDER:
                        if n == 0:
                            pe.wait_ge(slots_out, j + (2 if switch and s else 1))
                        for t in range(n * PER, (n + 1) * PER):
                            last = pe.matmul(gps[n][:, t % PER], onehot_1[s][:, t, :], onehot_2[s][:, t], start=True, stop=True)
                        last.then_inc(gate_ps, 1)

            run(pe, step)


def expert_sweep_2(g):
    nc, i, sem = g.nc, g.i, g.sem
    N = NKEYS
    v_raw, gt, at, v_in, gt_in, at_in = g.v_raw, g.gt, g.act_in, g.v_in, g.gt_in, g.act_in_sem
    v_hi = [g.at(f"v_hi{s}", 4 * s, [P, D], F32R) for s in range(2)]
    v_lo = [g.at(f"v_lo{s}", 8 + 4 * s, [P, D], F32R) for s in range(2)]
    c_lo = [g.at(f"c_lo{s}", 16 + 2 * s, [P, HALF], F32R) for s in range(2)]
    junk = g.at("junk_y", 20, [P, D])
    cf = [g.at(f"cf{s}", 104 + 2 * s, [P, HALF]) for s in range(2)]
    c_hi = [g.at(f"c_hi{s}", 108 + 2 * s, [P, HALF], F32R) for s in range(2)]
    gate_block = g.gate_block_last
    y = g.at("y", 64, [P, RT, D])
    x1 = g.at("x1", 128, [P, TT, D])
    vhi_r, vlo_r, cf_r, chi_r, clo_r, used, tile_summed, y_out = (sem(n) for n in (
        "vhi_r", "vlo_r", "cf_r", "chi_r", "clo_r", "used", "tile_summed", "y_out"))
    x1_in, y_ssq, y_root, y_scaled, out_ready = (sem(n) for n in ("x1_in", "y_ssq", "y_root", "y_scaled", "out_ready"))
    out_stored = sem("out_stored")
    with ExitStack() as banks:
        yps = [banks.enter_context(nc.psum_tensor(f"y_ps{n}", [P, D], F32)) for n in range(RT)]
        block = banks.enter_context(nc.Block())

        @block.sync
        def _(sp):
            def refill(r, n, s):
                m = r * N + n
                sp.wait_ge(cf_r, m - RING + 1)
                sp.wait_ge(vlo_r, m - RING + 1)
                load_expert(g, sp, r, n, s)

            for n in range(RING, UNROLL):
                sp.wait_ge(vlo_r, n - RING + 1)
                load_expert(g, sp, 0, n, n)
            sp.dma_start(g.gate_d[S // GTOK - 1], gate_block[:]).then_inc(g.gate_stored[1], 16)
            for r in range(ROUNDS):
                for part in range(2):
                    with sp.Fori(part * N // UNROLL // 2 if r or part else 1, (part + 1) * N // UNROLL // 2) as q:
                        for s in range(UNROLL):
                            refill(r, UNROLL * q + s, s)
                    if r == 0 and part == 0:
                        sp.dma_start(x1[:], g.x1_d.rearrange("t p d -> p t d")).then_inc(x1_in, 16)
                if r == 0:
                    sp.wait_ge(g.gate_stored[1], (TT + 1) * 16)

        def store(eng, r, t):
            eng.wait_ge(out_ready, r * RT + t + 1)
            eng.dma_start(g.out[(r * RT + t) * P:(r * RT + t + 1) * P, :], y[:, t, :]).then_inc(out_stored, 16)

        @block.gpsimd
        def _(pool):
            pool.wait_ge(x1_in, 16)
            for r in range(ROUNDS):
                for t in range(RT):
                    pool.wait_ge(y_scaled, r * RT + t + 1)
                    pool.tensor_tensor(y[:, t, :], y[:, t, :], x1[:, r * RT + t, :], ALU.add).then_inc(out_ready, 1)
                    store(pool, r, t)
            pool.wait_ge(out_stored, TT * 16)

        @block.scalar
        def _(act):
            def prepare(m, s, turn, free=True):
                act.wait_ge(v_in[s % RING], turn * 16)
                if free:
                    act.wait_ge(used, m - 1)
                split_hi(act, v_hi[s % 2][:], v_raw[s % RING][:]).then_inc(vhi_r, 1)
                act.wait_ge(cf_r, m + 1)
                split_hi(act, c_hi[s % 2][:], cf[s % 2][:]).then_inc(chi_r, 1)

            def finish(r, t):
                n = r * RT + t
                act.wait_ge(tile_summed, n + 1)
                if t == 0:
                    act.wait_ge(out_stored, r * RT * 16) if r else act.wait_ge(g.gate_stored[1], (TT + 1) * 16)
                act.activation(y[:, t, :], yps[t][:], ACT.Copy).then_inc(y_out, 1)
                if n:
                    act.wait_ge(y_ssq, n)
                act.activation(junk[:], yps[t][:], ACT.Square, accum_out=g.ssq[:, n:n + 1]).then_inc(y_ssq, 1)
                act.wait_ge(y_ssq, n + 1)
                act.activation(g.rstd[:, n:n + 1], g.ssq[:, n:n + 1], ACT.Sqrt, scale=1.0 / D, bias=g.eps[:]).then_inc(y_root, 1)

            for r in range(ROUNDS):
                base = r * N
                for n in range(UNROLL):
                    prepare(base + n, n, base // RING + n // RING + 1, base + n >= 2)
                    if r and n == 0:
                        for t in range(RT):
                            finish(r - 1, t)
                with act.Fori(1, N // UNROLL) as q:
                    for s in range(UNROLL):
                        prepare(base + UNROLL * q + s, s, base // RING + q * (UNROLL // RING) + s // RING + 1)
            for t in range(RT):
                finish(ROUNDS - 1, t)

        @block.vector
        def _(dve):
            def prepare(m, s, turn, gate_turn):
                if s % GROUP == 0:
                    dve.wait_ge(gt_in[s // GROUP], gate_turn * 16)
                dve.wait_ge(at_in[s % RING], turn * 16)
                gates = gt[s // GROUP][:, :, s % GROUP, :]
                dve.tensor_tensor(cf[s % 2][:].rearrange("p (j t) -> p j t", t=GTOK), gates,
                                  at[s % RING][:].rearrange("p (j t) -> p j t", t=GTOK), ALU.mult).then_inc(cf_r, 1)
                dve.wait_ge(vhi_r, m + 1)
                split_lo(dve, v_lo[s % 2][:], v_raw[s % RING][:], v_hi[s % 2][:]).then_inc(vlo_r, 1)
                dve.wait_ge(chi_r, m + 1)
                split_lo(dve, c_lo[s % 2][:], cf[s % 2][:], c_hi[s % 2][:]).then_inc(clo_r, 1)

            def finish(r, t):
                n = r * RT + t
                dve.wait_ge(y_root, n + 1)
                dve.reciprocal(g.rstd[:, n:n + 1], g.rstd[:, n:n + 1])
                dve.drain()
                dve.scalar_tensor_tensor(y[:, t, :], y[:, t, :], g.rstd[:, n:n + 1], g.gate_rows[:, 1, :],
                                         ALU.mult, ALU.mult).then_inc(y_scaled, 1)

            for r in range(ROUNDS):
                base = r * N
                for n in range(UNROLL):
                    prepare(base + n, n, base // RING + n // RING + 1, base // UNROLL + 1)
                    if r and n >= 2 and n - 2 < RT:
                        finish(r - 1, n - 2)
                with dve.Fori(1, N // UNROLL) as q:
                    for s in range(UNROLL):
                        prepare(base + UNROLL * q + s, s, base // RING + q * (UNROLL // RING) + s // RING + 1,
                                base // UNROLL + q + 1)
            for t in range(RT):
                finish(ROUNDS - 1, t)

        @block.tensor
        def _(pe):
            def product(r, n, s, first=False, last=False):
                m = r * N + n
                pe.wait_ge(vlo_r, m + 1)
                pe.wait_ge(clo_r, m + 1)
                for t in range(RT):
                    if first and r:
                        pe.wait_ge(y_ssq, (r - 1) * RT + t + 1)
                    ch, cl = c_hi[s][:, t * P:(t + 1) * P], c_lo[s][:, t * P:(t + 1) * P]
                    for k, (c, v) in enumerate(((ch, v_hi), (ch, v_lo), (cl, v_hi))):
                        for half in range(2):
                            cols = slice(half * HALF, (half + 1) * HALF)
                            done = pe.matmul(yps[t][:, cols], c, v[s][:, cols], start=first and k == 0, stop=last and k == 2)
                    if last:
                        done.then_inc(tile_summed, 1)
                if last:
                    pe.wait_ge(tile_summed, (r + 1) * RT)
                    pe.sem_inc(used, 1)
                else:
                    done.then_inc(used, 1)

            for r in range(ROUNDS):
                for n in range(UNROLL):
                    product(r, n, n % 2, first=n == 0)
                with pe.Fori(1, N // UNROLL - 1) as q:
                    for s in range(UNROLL):
                        product(r, UNROLL * q + s, s % 2)
                for s in range(UNROLL):
                    product(r, N - UNROLL + s, s % 2, last=s == UNROLL - 1)


def lay_out(a):
    f = np.ascontiguousarray
    one = {k: np.asarray(v)[0] for k, v in a.items() if k not in ("x", "c")}
    cols = lambda v: np.asarray(v).reshape(-1, P).T
    tiles = lambda w, n: f(w.reshape(KC, P, n, P).transpose(2, 1, 0, 3).reshape(n, P, KC * P))
    rows = lambda w: f(w.reshape(-1, P, w.shape[1]).transpose(1, 0, 2))
    w_in = one["w_in"]
    kw, vw = GLA_HEADS * GLA_DK, GLA_HEADS * GLA_DV
    at = np.cumsum([0, kw, kw, vw, vw, RANK, RANK, D - vw])
    q, k, v, r, af, ab, p = (w_in[:, at[n]:at[n + 1]] for n in range(7))
    rank = np.zeros((D, P), np.float32)
    rank[:, 0:RANK], rank[:, 64:64 + RANK] = af, ab
    w_alpha = np.zeros((P, kw), np.float32)
    w_alpha[0:RANK], w_alpha[64:64 + RANK] = one["w_alpha_f"], one["w_alpha_b"]
    j, t = np.meshgrid(np.arange(P), np.arange(P), indexing="ij")
    same = j // CHUNK == t // CHUNK
    consts = np.concatenate([np.eye(P), np.broadcast_to(np.arange(P), (P, P)), same & (j <= t), same & (j > t)], 1)
    reset = np.broadcast_to((np.arange(S) % CHUNK != 0), (P, S))
    pos = np.r_[0:PAD, S - PAD:S]
    edges = np.stack([1.0 / (np.clip(pos + w // 2, 0, S) - np.clip(pos - w // 2, 0, S)) for w in WINDOWS])
    return {
        "x": f(np.asarray(a["x"])[0]),
        "vecs": f(np.concatenate([cols(one[n]) for n, _ in VECS], 1)),
        "consts": f(consts.astype(np.float32)),
        "reset": f(reset.astype(np.float32)),
        "edges": f(np.broadcast_to(edges.astype(np.float32), (P, len(WINDOWS), 2 * PAD))),
        "c": f(np.asarray(a["c"])),
        "w_mod": f(one["w_mod"].T.reshape(MOD_TILES, P, D)),
        "w_qkrp": tiles(np.concatenate([q, k, r, p], 1), QKRP),
        "w_rank": tiles(rank, 1)[0],
        "w_v": f(v.reshape(4, 2, P, vw).transpose(0, 2, 1, 3).reshape(4, P, 2 * vw)),
        "w_alpha": w_alpha,
        "w_pool": f(one["w_pool"].transpose(1, 0, 2)),
        "w_out": rows(one["w_out"]),
        "w_q": tiles(one["w_peer_q"], QTILES),
        "keys": f(one["peer_sub_keys"].reshape(QTILES, NKEYS, P).transpose(2, 0, 1)),
        "u": f(one["peer_u"].reshape(NKEYS, NKEYS, KC, P).transpose(1, 3, 2, 0).reshape(NKEYS, P, KC * P)),
        "v": f(one["peer_v"].reshape(NKEYS, NKEYS, D).transpose(1, 0, 2)),
    }


def kernel(**inputs):
    import concourse.bacc as bacc
    from concourse.bass_utils import run_bass_kernel_spmd

    nc = bacc.Bacc("TRN2", target_bir_lowering=False, num_devices=1)
    arrays = {f"in_{n}": a for n, a in lay_out(inputs).items()}
    t_in = {n[3:]: nc.dram_tensor(n, a.shape, F32, kind="ExternalInput").ap() for n, a in arrays.items()}
    out = nc.dram_tensor("out", (S, D), F32, kind="ExternalOutput").ap()
    layer(nc, t_in, out)
    r = run_bass_kernel_spmd(nc, [arrays], core_ids=[0])
    return r.results[0]["out"].reshape(1, S, D)
```

```python
from contextlib import ExitStack

import numpy as np

import concourse.bass as bass
from concourse import mybir

F32 = mybir.dt.float32
F32R = mybir.dt.float32r
U32 = mybir.dt.uint32
ALU = mybir.AluOpType
ACT = mybir.ActivationFunctionType
AX = mybir.AxisListType.X

P = 128
D = 1024
S = 1024
KC = D // P
TT = S // P
HALF = 512
N_MOD = 6
EPS = 1e-6

GLA_HEADS, GLA_DK, GLA_DV = 4, 64, 128
PAIRS = GLA_HEADS // 2
CHUNK = 64
NCHUNK = S // CHUNK
TAU = 16.0
RANK = 16
WINDOWS = (2, 4, 8, 16)
PAD = WINDOWS[-1] // 2

HEADS, NKEYS, TOPK = 8, 128, 16
QTILES = 2 * HEADS
TOK = 16
GTOK = P // 2
BLOCK_STEPS = GTOK // TOK
STEPS = TT * HEADS
LOWEST = -3.0e38

VECS = [("b_mod", N_MOD * KC), ("g_pre_mix", KC), ("g_post_mix", KC), ("b_alpha_f", PAIRS),
        ("b_alpha_b", PAIRS), ("g_gla_head", GLA_HEADS), ("pool_scale", 4), ("g_pre_ffn", KC), ("g_post_ffn", KC)]
VCOL = {}
for _name, _n in VECS:
    VCOL[_name] = (sum(n for _, n in VCOL.values()), _n)
NVEC = sum(n for _, n in VECS)

MOD_TILES = N_MOD * KC
MOD_FIRST = 2 * KC
MOD_LOAD = 2
MOD_PER_PAIR = 5
QKRP = 12


def split_hi(act, hi, raw):
    return act.activation(hi, raw, ACT.Copy)


def split_lo(dve, lo, raw, hi):
    return dve.tensor_tensor(lo, raw, hi.bitcast(F32), ALU.subtract)


def tile_product(pe, acc, w_hi, w_lo, a_hi, a_lo, halves=(0, 1)):
    for k in range(KC):
        wh, wl = w_hi[:, k * P:(k + 1) * P], w_lo[:, k * P:(k + 1) * P]
        for w, a, first, last in ((wh, a_hi, k == 0, False), (wh, a_lo, False, False), (wl, a_hi, False, k == KC - 1)):
            for half in halves:
                cols = slice(half * HALF, (half + 1) * HALF)
                done = pe.matmul(acc[:, cols], w, a[:, k, cols], start=first, stop=last)
    return done


class Layer:

    def __init__(self, nc, t_in, out):
        self.nc, self.i, self.out = nc, t_in, out


def layer(nc, t_in, out):
    g = Layer(nc, t_in, out)
    with ExitStack() as ctx:
        def sem(name):
            return ctx.enter_context(nc.semaphore(name))

        def small(name, shape, dt=F32):
            return ctx.enter_context(nc.sbuf_tensor(name, shape, dt))

        g.sem = sem
        g.x1_d = nc.dram_tensor("x1_d", (TT, P, D), F32, kind="Internal").ap()
        g.s_d = nc.dram_tensor("s_d", (TT * HEADS, P, 2, NKEYS), F32, kind="Internal").ap()
        g.act_d = nc.dram_tensor("act_d", (NKEYS, P, S), F32, kind="Internal").ap()
        g.gate_d = nc.dram_tensor("gate_d", (S // GTOK, P, NKEYS, GTOK), F32, kind="Internal").ap()
        g.consts = small("consts", [P, 4 * P])
        g.ident, g.iota = g.consts[:, 0:P], g.consts[:, P:2 * P]
        g.mask_f, g.mask_b = g.consts[:, 2 * P:3 * P], g.consts[:, 3 * P:4 * P]
        g.vecs = small("vecs", [P, NVEC])
        g.vec = lambda name: g.vecs[:, VCOL[name][0]:VCOL[name][0] + VCOL[name][1]]
        g.mod = small("mod", [P, N_MOD * KC])
        g.scale1 = small("scale1", [P, KC])
        g.scale2 = small("scale2", [P, KC])
        g.gate_cols = small("gate_cols", [P, 2 * KC])
        g.gate_rows = small("gate_rows", [P, 2, D])
        g.ssq = small("ssq", [P, 4 * TT])
        g.rstd = small("rstd", [P, 4 * TT])
        g.eps = small("eps", [P, 1])
        base = nc.sbuf_base
        base = (base() if callable(base) else base)
        base = (base + 1023) // 1024 * 1024
        g.at = lambda name, kb, shape, dt=F32: nc.alloc_sbuf_tensor_at(name, shape, dt, offset=base + int(kb * 1024))
        g.a_hi = g.at("a_hi", 128, [P, KC, S], F32R)
        g.a_lo = g.at("a_lo", 160, [P, KC, S], F32R)

        modulation(g)
        projections(g)
        decays(g)
        attention(g)
        with nc.psum_tensor("mix0", [P, D], F32) as mix0, nc.psum_tensor("mix1", [P, D], F32) as mix1:
            g.mps = [mix0, mix1]
            mix_out(g)
            retrieval_scores(g)
        expert_sweep_1(g)
        expert_sweep_2(g)


def modulate_transposed(g, tag, xn, hf, tp, scale, shift, sems, act, dve, pe):
    s_tp, s_hf, s_hi, s_lo = sems
    if pe is not None:
        for k in range(KC):
            if k >= 2:
                pe.wait_ge(s_hf, k - 1)
            for t in range(TT):
                last = pe.transpose(tp[k % 2][:, t * P:(t + 1) * P], xn[:, t, k * P:(k + 1) * P], g.ident)
            last.then_inc(s_tp, 1)
    if act is not None:
        for k in range(KC):
            act.wait_ge(s_tp, k + 1)
            if k >= 2:
                act.wait_ge(s_lo, k - 1)
            act.activation(hf[k % 2][:], tp[k % 2][:], ACT.Identity, bias=shift[:, k:k + 1],
                           scale=scale[:, k:k + 1]).then_inc(s_hf, 1)
    if dve is not None:
        for k in range(KC):
            dve.wait_ge(s_hf, k + 1)
            dve.tensor_copy(g.a_hi[:, k, :], hf[k % 2][:]).then_inc(s_hi, 1)
            dve.wait_ge(s_hi, k + 1)
            split_lo(dve, g.a_lo[:, k, :], hf[k % 2][:], g.a_hi[:, k, :]).then_inc(s_lo, 1)


def mod_column(g, dve, col, w):
    return dve.scalar_tensor_tensor(w, w, 1.0, g.silu_row[:], ALU.mult, ALU.mult, accum_out=g.mod[:, bass.ds(col, 1)])


def modulation(g):
    nc, i, sem = g.nc, g.i, g.sem
    early = MOD_TILES - MOD_PER_PAIR * QKRP // 2
    x = g.at("x", 0, [P, TT, D])
    w_mod = g.at("w_mod", 32, [P, early, D])
    hf = [g.at(f"hf{s}", 104 + 4 * s, [P, S]) for s in range(2)]
    junk = g.at("junk_a", 112, [P, D])
    g.silu_row = g.at("silu_row", 124, [P, D])
    consts_in, vecs_in, c_in = sem("consts_in"), sem("vecs_in"), sem("c_in")
    x_in = [sem(f"x_in{t}") for t in range(TT)]
    w_mod_in = [sem(f"w_mod_in{s}") for s in range(early // MOD_LOAD)]
    silu_ready, eps_ready, ssq_ready, root_ready, xn_ready = (sem(n) for n in (
        "silu_ready", "eps_ready", "ssq_ready", "root_ready", "xn_ready"))
    cols_ready = sem("cols_ready")
    g.w_raw = [g.at(f"w_raw{s}", 68 + 4 * s, [P, D]) for s in range(2)]
    g.w_hi = [g.at(f"w_hi{s}", 76 + 4 * s, [P, D], F32R) for s in range(2)]
    g.w_lo = [g.at(f"w_lo{s}", 84 + 4 * s, [P, D], F32R) for s in range(2)]
    g.w_raw_in = [sem(f"w_raw_in{s}") for s in range(2)]
    g.w_hi_ready, g.w_lo_ready = sem("w_hi_ready"), sem("w_lo_ready")
    sems = tuple(sem(n) for n in ("tp_a", "hf_a", "hi_a", "lo_a"))
    with nc.psum_tensor("tp_a0", [P, S], F32) as tp0, nc.psum_tensor("tp_a1", [P, S], F32) as tp1, nc.Block() as block:
        tp = [tp0, tp1]

        @block.sync
        def _(sp):
            sp.dma_start(g.silu_row[:], i["c"].to_broadcast([P, D])).then_inc(c_in, 16)
            for t in range(TT):
                sp.dma_start(x[:, t, :], i["x"][t * P:(t + 1) * P, :]).then_inc(x_in[t], 16)
            sp.dma_start(g.vecs[:], i["vecs"]).then_inc(vecs_in, 16)
            sp.dma_start(g.consts[:], i["consts"]).then_inc(consts_in, 16)
            for s in range(early // MOD_LOAD):
                tiles = slice(s * MOD_LOAD, (s + 1) * MOD_LOAD)
                sp.dma_start(w_mod[:, tiles, :], i["w_mod"][tiles].rearrange("n p d -> p n d")).then_inc(w_mod_in[s], 16)
            sp.wait_ge(cols_ready, 1)
            for n in range(2):
                sp.dma_start(g.w_raw[n][:], i["w_qkrp"][n]).then_inc(g.w_raw_in[n], 16)

        @block.scalar
        def _(act):
            act.wait_ge(c_in, 16)
            act.activation(g.silu_row[:], g.silu_row[:], ACT.Silu).then_inc(silu_ready, 1)
            for t in range(TT):
                act.wait_ge(x_in[t], 16)
                if t:
                    act.wait_ge(ssq_ready, t)
                act.activation(junk[:], x[:, t, :], ACT.Square, accum_out=g.ssq[:, t:t + 1]).then_inc(ssq_ready, 1)
            act.wait_ge(ssq_ready, TT)
            act.wait_ge(eps_ready, 1)
            act.activation(g.rstd[:, 0:TT], g.ssq[:, 0:TT], ACT.Sqrt, scale=1.0 / D, bias=g.eps[:]).then_inc(root_ready, 1)
            act.wait_ge(cols_ready, 1)
            modulate_transposed(g, "a", x, hf, tp, g.scale1, g.mod[:, 0:KC], sems, act, None, None)
            for n in range(2):
                act.wait_ge(g.w_raw_in[n], 16)
                split_hi(act, g.w_hi[n][:], g.w_raw[n][:]).then_inc(g.w_hi_ready, 1)

        @block.vector
        def _(dve):
            dve.memset(g.eps[:], EPS).then_inc(eps_ready, 1)
            dve.wait_ge(root_ready, 1)
            dve.reciprocal(g.rstd[:, 0:TT], g.rstd[:, 0:TT])
            dve.drain()
            for t in range(TT):
                last = dve.tensor_scalar(x[:, t, :], x[:, t, :], g.rstd[:, t:t + 1], None, ALU.mult)
            last.then_inc(xn_ready, 1)
            dve.wait_ge(silu_ready, 1)
            for n in range(MOD_FIRST):
                dve.wait_ge(w_mod_in[n // MOD_LOAD], 16)
                mod_column(g, dve, n, w_mod[:, n, :])
            dve.wait_ge(vecs_in, 16)
            dve.drain()
            dve.tensor_tensor(g.mod[:, 0:MOD_FIRST], g.mod[:, 0:MOD_FIRST], g.vec("b_mod")[:, 0:MOD_FIRST], ALU.add)
            dve.drain()
            dve.scalar_tensor_tensor(g.scale1[:], g.mod[:, KC:2 * KC], 1.0, g.vec("g_pre_mix"), ALU.add, ALU.mult)\
               .then_inc(cols_ready, 1)
            for n in range(MOD_FIRST, early):
                dve.wait_ge(w_mod_in[n // MOD_LOAD], 16)
                mod_column(g, dve, n, w_mod[:, n, :])
            modulate_transposed(g, "a", x, hf, tp, None, None, sems, None, dve, None)
            for n in range(2):
                dve.wait_ge(g.w_hi_ready, n + 1)
                split_lo(dve, g.w_lo[n][:], g.w_raw[n][:], g.w_hi[n][:]).then_inc(g.w_lo_ready, 1)

        @block.tensor
        def _(pe):
            pe.wait_ge(consts_in, 16)
            pe.wait_ge(xn_ready, 1)
            modulate_transposed(g, "a", x, hf, tp, None, None, sems, None, None, pe)


def projections(g):
    nc, i, sem = g.nc, g.i, g.sem
    g.z = g.at("z", 0, [P, QKRP, S])
    g.za = g.at("za", 48, [P, S])
    g.v = g.at("v", 52, [P, TT, GLA_HEADS * GLA_DV])
    raw, w_hi, w_lo, raw_in, hi_ready, lo_ready = g.w_raw, g.w_hi, g.w_lo, g.w_raw_in, g.w_hi_ready, g.w_lo_ready
    wv_hi = g.at("wv_hi", 92, [P, KC, HALF], F32R)
    wv_lo = g.at("wv_lo", 108, [P, KC, HALF], F32R)
    w_mod = g.at("w_mod_b", 104, [P, MOD_PER_PAIR, D])
    spread = g.at("spread", 192, [P, KC // 2, P])
    w_mod_in = sem("w_mod_b_in")
    width = S + 2 * PAD
    win = [g.at(f"win{n}", 76 + 4.125 * n, [P, width]) for n in range(2)]
    pooled = g.at("pooled", 84.25, [P, S])
    w_pool = g.at("w_pool", 88.25, [P, 4, P])
    edges = g.at("edges", 90.25, [P, 4, 2 * PAD])
    edge_tmp = g.at("edge_tmp", 90.5, [P, 2 * PAD])
    pool_in, silu_done, pooled_ready, pool_mm, pool_out = (sem(n) for n in (
        "pool_in", "silu_r", "pooled_ready", "pool_mm", "pool_out"))
    POOL_AT = {2: 0, 4: 1, 6: 2}
    ROWS_AT = {4: 0, 6: 1, 7: 2}
    mod_done, spread_ready, rows_ps, rows_ready = (sem(n) for n in (
        "mod_b_done", "spread_ready", "rows_ps", "rows_ready"))
    early = MOD_TILES - MOD_PER_PAIR * QKRP // 2
    tile_done, tile_out = sem("z_done"), sem("z_out")
    v_done, v_out = sem("v_done"), sem("v_out")
    VP = KC * HALF // D
    with nc.psum_tensor("acc_b0", [P, S], F32) as acc0, nc.psum_tensor("acc_b1", [P, S], F32) as acc1, \
            nc.psum_tensor("rows", [P, HALF], F32) as rows, \
            nc.Block() as block:
        acc = [acc0, acc1]
        piece = lambda t, n: t[:, 2 * n:2 * n + 2, :].rearrange("p a b -> p (a b)")

        @block.sync
        def _(sp):
            late = i["w_mod"].rearrange("n p d -> p n d")
            sp.dma_start(w_mod[:], late[:, early:early + MOD_PER_PAIR, :]).then_inc(w_mod_in, 16)
            with sp.Fori(1, QKRP // 2) as r:
                for s in range(2):
                    sp.wait_ge(lo_ready, (r - 1) * 2 + s + 1)
                    sp.dma_start(raw[s][:], i["w_qkrp"][r * 2 + s]).then_inc(raw_in[s], 16)
                sp.wait_ge(mod_done, r)
                sp.dma_start(w_mod[:], late[:, bass.ds(early + r * MOD_PER_PAIR, MOD_PER_PAIR), :]).then_inc(w_mod_in, 16)
            for n in range(QKRP, QKRP + 1 + VP):
                sp.wait_ge(lo_ready, n - 1)
                src = i["w_rank"] if n == QKRP else i["w_v"][n - QKRP - 1]
                sp.dma_start(raw[n % 2][:], src).then_inc(raw_in[n % 2], 16)
            sp.wait_ge(tile_done, QKRP)
            sp.dma_start(w_pool[:], i["w_pool"]).then_inc(pool_in, 16)
            sp.dma_start(edges[:], i["edges"]).then_inc(pool_in, 16)

        @block.scalar
        def _(act):
            def split(s, count):
                act.wait_ge(raw_in[s], count)
                split_hi(act, w_hi[s][:], raw[s][:]).then_inc(hi_ready, 1)

            def evacuate(n, s, dst):
                act.wait_ge(tile_done, n + 1)
                act.activation(dst, acc[s][:], ACT.Copy).then_inc(tile_out, 1)

            with act.Fori(0, QKRP // 2 - 1) as r:
                for s in range(2):
                    evacuate(2 * r + s, s, g.z[:, bass.ds(2 * r + s, 1), :])
                    split(s, (r + 2) * 16)
            evacuate(QKRP - 2, 0, g.z[:, QKRP - 2, :])
            split(0, (QKRP // 2 + 1) * 16)
            for n in range(VP):
                m = QKRP + 1 + n
                act.wait_ge(raw_in[m % 2], (m // 2 + 1) * 16)
                split_hi(act, piece(wv_hi, n), raw[m % 2][:]).then_inc(hi_ready, 1)
            evacuate(QKRP - 1, 1, g.z[:, QKRP - 1, :])
            evacuate(QKRP, 0, g.za[:])
            act.wait_ge(tile_out, QKRP)
            act.activation(g.z[:, 4:8, :], g.z[:, 4:8, :], ACT.Silu).then_inc(silu_done, 1)

            def pool_group_out(n):
                act.wait_ge(pool_mm, n + 1)
                act.activation(g.z[:, 8 + n, :], acc[0][:], ACT.Copy, scale=g.vec("pool_scale")[:, n:n + 1])\
                   .then_inc(pool_out, 1)

            for t in range(TT):
                if t in POOL_AT:
                    pool_group_out(POOL_AT[t])
                act.wait_ge(v_done, t + 1)
                act.activation(g.v[:, t, :], acc[1][:, (t % 2) * HALF:(t % 2 + 1) * HALF], ACT.Copy).then_inc(v_out, 1)
            pool_group_out(3)

        @block.vector
        def _(dve):
            def split(n, s):
                dve.wait_ge(hi_ready, n + 1)
                split_lo(dve, w_lo[s][:], raw[s][:], w_hi[s][:]).then_inc(lo_ready, 1)

            def mod_columns(r):
                dve.wait_ge(w_mod_in, (r + 1) * 16)
                for s in range(MOD_PER_PAIR):
                    last = mod_column(g, dve, early + r * MOD_PER_PAIR + s, w_mod[:, s, :])
                last.then_inc(mod_done, 1)

            with dve.Fori(0, QKRP // 2 - 1) as r:
                mod_columns(r)
                for s in range(2):
                    split(2 * (r + 1) + s, s)
            mod_columns(QKRP // 2 - 1)
            split(QKRP, 0)
            dve.drain()
            for n in range(VP):
                m = QKRP + 1 + n
                dve.wait_ge(hi_ready, m + 1)
                split_lo(dve, piece(wv_lo, n), raw[m % 2][:], piece(wv_hi, n)).then_inc(lo_ready, 1)
            rest = slice(MOD_FIRST, MOD_TILES)
            dve.tensor_tensor(g.mod[:, rest], g.mod[:, rest], g.vec("b_mod")[:, rest], ALU.add)
            dve.drain()
            dve.scalar_tensor_tensor(g.scale2[:], g.mod[:, 4 * KC:5 * KC], 1.0, g.vec("g_pre_ffn"), ALU.add, ALU.mult)
            dve.tensor_tensor(g.gate_cols[:, 0:KC], g.mod[:, 2 * KC:3 * KC], g.vec("g_post_mix"), ALU.mult)
            dve.tensor_tensor(g.gate_cols[:, KC:], g.mod[:, 5 * KC:6 * KC], g.vec("g_post_ffn"), ALU.mult)
            dve.drain()
            half = KC // 2

            def gate_row(n):
                gate = g.gate_cols[:, n * half:(n + 1) * half]
                dve.tensor_copy(spread[:], gate.unsqueeze(2).to_broadcast([P, half, P])).then_inc(spread_ready, 1)
                dve.wait_ge(rows_ps, n + 1)
                dve.tensor_copy(g.gate_rows[:, n // 2, n % 2 * HALF:(n % 2 + 1) * HALF], rows[:]).then_inc(rows_ready, 1)

            def pool_group(n, w):
                p = g.z[:, 8 + n, :]
                dve.drain()
                dve.tensor_copy(win[0][:, PAD:PAD + S], p)
                src, dst, m, lo, hi = win[0], win[1], 1, 0, width
                while m < w:
                    left, right = (1, 0) if m == 1 else (m // 2, m // 2)
                    lo, hi = lo + left, hi - right
                    dve.drain()
                    dve.tensor_tensor(dst[:, lo:hi], src[:, lo - left:hi - left], src[:, lo + right:hi + right], ALU.add)
                    src, dst, m = dst, src, 2 * m
                if n:
                    dve.wait_ge(pool_mm, n)
                dve.drain()
                body = src[:, PAD:PAD + S]
                dve.scalar_tensor_tensor(pooled[:], body, 1.0 / w, p, ALU.mult, ALU.subtract)
                for e in range(2):
                    cols = slice(0, PAD) if e == 0 else slice(S - PAD, S)
                    dve.tensor_tensor(edge_tmp[:, e * PAD:(e + 1) * PAD], src[:, PAD + cols.start:PAD + cols.stop],
                                      edges[:, n, e * PAD:(e + 1) * PAD], ALU.mult)
                dve.drain()
                for e in range(2):
                    cols = slice(0, PAD) if e == 0 else slice(S - PAD, S)
                    last = dve.tensor_tensor(pooled[:, cols], edge_tmp[:, e * PAD:(e + 1) * PAD], p[:, cols], ALU.subtract)
                last.then_inc(pooled_ready, 1)
                if n < 3:
                    dve.drain()
                    dve.memset(win[0][:, 0:PAD], 0.0)
                    dve.memset(win[0][:, PAD + S:width], 0.0)

            dve.wait_ge(tile_done, QKRP + 1)
            dve.wait_ge(tile_out, QKRP + 1)
            dve.memset(win[0][:], 0.0)
            dve.memset(win[1][:], 0.0)
            dve.wait_ge(pool_in, 32)
            for n, w in enumerate(WINDOWS):
                pool_group(n, w)
                if n:
                    gate_row(n - 1)
            gate_row(3)

        @block.tensor
        def _(pe):
            def make_rows(n):
                pe.wait_ge(spread_ready, n + 1)
                if n:
                    pe.wait_ge(rows_ready, n)
                for k in range(KC // 2):
                    last = pe.matmul(rows[:, k * P:(k + 1) * P], spread[:, k, :], g.ident, start=True, stop=True)
                last.then_inc(rows_ps, 1)

            def pool_product(n):
                pe.wait_ge(pooled_ready, n + 1)
                if n:
                    pe.wait_ge(pool_out, n)
                else:
                    pe.wait_ge(tile_out, QKRP + 1)
                for half in range(2):
                    cols = slice(half * HALF, (half + 1) * HALF)
                    last = pe.matmul(acc[0][:, cols], w_pool[:, n, :], pooled[:, cols], start=True, stop=True)
                last.then_inc(pool_mm, 1)

            with pe.Fori(0, QKRP // 2) as r:
                for s in range(2):
                    pe.wait_ge(lo_ready, 2 * r + s + 1)
                    tile_product(pe, acc[s], w_hi[s], w_lo[s], g.a_hi, g.a_lo).then_inc(tile_done, 1)
            pe.wait_ge(lo_ready, QKRP + 1)
            tile_product(pe, acc[0], w_hi[0], w_lo[0], g.a_hi, g.a_lo).then_inc(tile_done, 1)
            pe.wait_ge(lo_ready, QKRP + 1 + VP)
            pe.wait_ge(tile_out, QKRP)
            for t in range(TT):
                if t >= 2:
                    pe.wait_ge(v_out, t - 1)
                if t in POOL_AT:
                    pool_product(POOL_AT[t])
                if t in ROWS_AT:
                    make_rows(ROWS_AT[t])
                dst = acc[1][:, (t % 2) * HALF:(t % 2 + 1) * HALF]
                for k in range(KC):
                    ah, al = g.a_hi[:, k, t * P:(t + 1) * P], g.a_lo[:, k, t * P:(t + 1) * P]
                    pe.matmul(dst, ah, wv_hi[:, k, :], start=k == 0, stop=False)
                    pe.matmul(dst, ah, wv_lo[:, k, :], start=False, stop=False)
                    last = pe.matmul(dst, al, wv_hi[:, k, :], start=False, stop=k == KC - 1)
                last.then_inc(v_done, 1)
            pool_product(3)
            make_rows(3)


def decays(g):
    nc, i, sem = g.nc, g.i, g.sem
    reset = g.at("reset", 68, [P, S])
    la = g.at("la", 72, [P, PAIRS, S])
    prefix = g.at("prefix", 80, [P, PAIRS, S])
    tail = g.at("tail", 88, [P, PAIRS, S])
    e_q = g.at("e_q", 96, [P, PAIRS, S])
    e_inv = g.at("e_inv", 104, [P, PAIRS, S])
    e_end = g.at("e_end", 112, [P, PAIRS, S])
    g.q_dec = [g.at(f"q_dec{d}", (187, 144)[d], [P, PAIRS, S]) for d in range(2)]
    g.k_inv = [g.at(f"k_inv{d}", 128 + 24 * d, [P, PAIRS, S]) for d in range(2)]
    g.k_end = [g.at(f"k_end{d}", 136 + 24 * d, [P, PAIRS, S]) for d in range(2)]
    g.gamma = g.at("gamma", 168, [P, 2, PAIRS, NCHUNK])
    soft = [g.at(f"softplus{n}", 169 + 8 * n, [P, PAIRS, S]) for n in range(2)]
    w_alpha = g.at("w_alpha", 185, [P, GLA_HEADS * GLA_DK])
    consts_in, weights_in = sem("reset_in"), sem("small_w_in")
    logits, logit_out, ln_ready, scan_ready, tail_ready, exps_ready, k_end_done = (sem(n) for n in (
        "logits", "logit_out", "ln_ready", "scan_ready", "tail_ready", "exps_ready", "k_end_done"))
    with ExitStack() as banks:
        lps = [banks.enter_context(nc.psum_tensor(f"logit{n}", [P, S], F32)) for n in range(PAIRS)]
        block = banks.enter_context(nc.Block())
        flat = lambda a: a[:].rearrange("p a b -> p (a b)")
        chunks = lambda a, pair: a[:, pair, :].rearrange("p (n c) -> p n c", c=CHUNK)
        last_of = lambda a, pair: chunks(a, pair)[:, :, CHUNK - 1:CHUNK]

        @block.sync
        def _(sp):
            sp.dma_start(w_alpha[:], i["w_alpha"]).then_inc(weights_in, 16)
            sp.dma_start(reset[:], i["reset"]).then_inc(consts_in, 16)

        @block.tensor
        def _(pe):
            pe.wait_ge(weights_in, 16)
            for d in range(2):
                if d:
                    pe.wait_ge(logit_out, 1)
                rows = slice(64 * d, 64 * d + RANK)
                for pair in range(PAIRS):
                    for half in range(2):
                        cols = slice(half * HALF, (half + 1) * HALF)
                        last = pe.matmul(lps[pair][:, cols], w_alpha[rows, pair * P:(pair + 1) * P], g.za[rows, cols],
                                         start=True, stop=True)
                last.then_inc(logits, 1)

        @block.scalar
        def _(act):
            def softplus(d):
                act.wait_ge(logit_out, d + 1)
                if d:
                    act.wait_ge(scan_ready, d)
                act.activation(flat(soft[0]), flat(la), ACT.Abs)
                act.drain()
                act.activation(flat(soft[0]), flat(soft[0]), ACT.Exp, scale=-1.0)
                act.drain()
                act.activation(flat(soft[1]), flat(soft[0]), ACT.Ln, bias=1.0).then_inc(ln_ready, 1)

            softplus(0)
            for d in range(2):
                act.wait_ge(scan_ready, d + 1)
                for pair in range(PAIRS):
                    act.activation(g.gamma[:, d, pair, :], last_of(prefix, pair).squeeze(2), ACT.Exp, scale=1.0 / TAU)
                act.wait_ge(tail_ready, d + 1)
                b = prefix if d == 0 else e_end
                act.activation(flat(e_q), flat(b), ACT.Exp, scale=1.0 / TAU).then_inc(exps_ready, 1)
                act.activation(flat(e_inv), flat(b), ACT.Exp, scale=-1.0 / TAU).then_inc(exps_ready, 1)
                act.drain()
                if d == 0:
                    softplus(1)
                act.activation(flat(e_end), flat(tail), ACT.Exp, scale=1.0 / TAU).then_inc(exps_ready, 1)

        @block.gpsimd
        def _(pool):
            pool.wait_ge(exps_ready, 3)
            keys = g.z[:, 2:4, :].rearrange("p a b -> p (a b)")
            pool.tensor_tensor(flat(g.k_end[0]), keys, flat(e_end), ALU.mult).then_inc(k_end_done, 1)

        @block.vector
        def _(dve):
            def logit(d):
                bias = g.vec("b_alpha_f" if d == 0 else "b_alpha_b")
                dve.wait_ge(logits, d + 1)
                for pair in range(PAIRS):
                    last = dve.tensor_scalar(la[:, pair, :], lps[pair][:], bias[:, pair:pair + 1], None, ALU.add)
                last.then_inc(logit_out, 1)

            logit(0)
            dve.wait_ge(consts_in, 16)
            for d in range(2):
                dve.wait_ge(logit_out, d + 1)
                dve.wait_ge(ln_ready, d + 1)
                dve.scalar_tensor_tensor(flat(la), flat(la), 0.0, flat(soft[1]), ALU.min, ALU.subtract)
                dve.drain()
                for pair in range(PAIRS):
                    last = dve.tensor_tensor_scan(prefix[:, pair, :], reset[:], la[:, pair, :], 0.0, ALU.mult, ALU.add)
                last.then_inc(scan_ready, 1)
                dve.drain()
                for pair in range(PAIRS):
                    total = last_of(prefix, pair).to_broadcast([P, NCHUNK, CHUNK])
                    if d == 0:
                        last = dve.tensor_tensor(chunks(tail, pair), total, chunks(prefix, pair), ALU.subtract)
                    else:
                        dve.wait_ge(exps_ready, 3)
                        dve.tensor_tensor(tail[:, pair, :], prefix[:, pair, :], la[:, pair, :], ALU.subtract)
                        dve.wait_ge(k_end_done, 1)
                        dve.drain()
                        last = dve.tensor_tensor(chunks(e_end, pair), total, chunks(tail, pair), ALU.subtract)
                last.then_inc(tail_ready, 1)
                if d == 0:
                    logit(1)
                q, k = g.z[:, 0:2, :].rearrange("p a b -> p (a b)"), g.z[:, 2:4, :].rearrange("p a b -> p (a b)")
                dve.wait_ge(exps_ready, 3 * d + 1)
                dve.scalar_tensor_tensor(flat(g.q_dec[d]), q, GLA_DK ** -0.5, flat(e_q), ALU.mult, ALU.mult)
                dve.wait_ge(exps_ready, 3 * d + 2)
                dve.tensor_tensor(flat(g.k_inv[d]), k, flat(e_inv), ALU.mult)
                dve.drain()
            dve.wait_ge(exps_ready, 6)
            dve.tensor_tensor(flat(g.k_end[1]), k, flat(e_end), ALU.mult)


def attention(g):
    nc, i, sem = g.nc, g.i, g.sem
    g.o = g.at("o", 0, [P, TT, GLA_HEADS * GLA_DV])
    k_tok = [g.at(f"k_tok{d}", 68 + 8 * d, [P, TT, PAIRS * P]) for d in range(2)]
    state = g.at("state", 84, [P, 2, PAIRS, NCHUNK, GLA_DV])
    scores = [g.at(f"scores{n}", 169 + 0.5 * n, [P, P]) for n in range(4)]
    kt_ps, kt_out, upd_ps, upd_done, sc_ps, sc_out, o_ps_done, o_out = (sem(n) for n in (
        "kt_ps", "kt_out", "upd_ps", "upd_done", "sc_ps", "sc_out", "o_done", "o_out"))
    o_ssq, o_root, o_rstd = sem("o_ssq"), sem("o_root"), sem("o_rstd")
    junk = g.at("junk_o", 172, [P, GLA_DV])
    g.wo_raw = [g.at(f"wo_raw{s}", kb, [P, D]) for s, kb in enumerate((48, 116, 120, 124))]
    g.wo_in = [sem(f"wo_in{s}") for s in range(WO_RING)]
    steps = NCHUNK - 1
    with ExitStack() as banks:
        bank = lambda name: banks.enter_context(nc.psum_tensor(name, [P, 4, P], F32))
        tr = [bank(f"tr{n}") for n in range(2)]
        upd = [[bank(f"upd{d}{n}") for n in range(2)] for d in range(2)]
        ops = upd
        sps = [bank(f"sps{n}") for n in range(2)]
        block = banks.enter_context(nc.Block())
        groups = [(d, pair, q) for d in range(2) for pair in range(PAIRS) for q in range(TT // 4)]
        chunk_at = lambda d, n: n if d == 0 else NCHUNK - 1 - n

        @block.sync
        def _(sp):
            for n in range(WO_RING):
                sp.dma_start(g.wo_raw[n][:], i["w_out"][:, MIX_ORDER[n], :]).then_inc(g.wo_in[n], 16)

        @block.tensor
        def _(pe):
            for n, (d, pair, q) in enumerate(groups):
                if n >= 2:
                    pe.wait_ge(kt_out, n - 1)
                for t in range(4):
                    cols = slice((4 * q + t) * P, (4 * q + t + 1) * P)
                    last = pe.transpose(tr[n % 2][:, t, :], g.k_end[d][:, pair, cols], g.ident)
                last.then_inc(kt_ps, 1)
            pe.wait_ge(kt_out, len(groups))
            for n in range(steps):
                if n >= 2:
                    pe.wait_ge(upd_done, n - 1)
                for d in range(2):
                    c = chunk_at(d, n)
                    rows = slice(CHUNK * (c % 2), CHUNK * (c % 2) + CHUNK)
                    for pair in range(PAIRS):
                        for h in range(2):
                            head = 2 * pair + h
                            last = pe.matmul(upd[d][n % 2][h * GLA_DK:(h + 1) * GLA_DK, pair, :],
                                             k_tok[d][rows, c // 2, pair * P + h * GLA_DK:pair * P + (h + 1) * GLA_DK],
                                             g.v[rows, c // 2, head * GLA_DV:(head + 1) * GLA_DV], start=True, stop=True)
                last.then_inc(upd_ps, 1)

            def score(n):
                t, head = n // GLA_HEADS, n % GLA_HEADS
                pair, keys = head // 2, slice(GLA_DK * (head % 2), GLA_DK * (head % 2 + 1))
                cols = slice(t * P, (t + 1) * P)
                if n >= 2:
                    pe.wait_ge(sc_out, n - 1)
                for d in range(2):
                    last = pe.matmul(sps[n % 2][:, d, :], g.k_inv[d][keys, pair, cols], g.q_dec[d][keys, pair, cols],
                                     start=True, stop=True)
                last.then_inc(sc_ps, 1)

            score(0)
            for n in range(TT * GLA_HEADS):
                t, head = n // GLA_HEADS, n % GLA_HEADS
                pair, keys = head // 2, slice(GLA_DK * (head % 2), GLA_DK * (head % 2 + 1))
                if n + 1 < TT * GLA_HEADS:
                    score(n + 1)
                pe.wait_ge(sc_out, n + 1)
                if head == 0 and t >= 2:
                    pe.wait_ge(o_out, t - 1)
                if n == 0:
                    pe.wait_ge(upd_done, steps)
                cols = slice(head * GLA_DV, (head + 1) * GLA_DV)
                dst = ops[t % 2][head % 2][:, pair, :]
                pe.matmul(dst, scores[n % 4][:], g.v[:, t, cols], start=True, stop=False)
                for half in range(2):
                    c = 2 * t + half
                    rows = slice(CHUNK * half, CHUNK * (half + 1))
                    for d in range(2):
                        last = pe.matmul(dst[rows, :], g.q_dec[d][keys, pair, c * CHUNK:(c + 1) * CHUNK],
                                         state[keys, d, pair, c, :], start=False, stop=d == 1)
                if head == GLA_HEADS - 1:
                    last.then_inc(o_ps_done, 1)

        @block.vector
        def _(dve):
            for n, (d, pair, q) in enumerate(groups):
                dve.wait_ge(kt_ps, n + 1)
                dve.tensor_copy(k_tok[d][:, 4 * q:4 * q + 4, pair * P:(pair + 1) * P], tr[n % 2][:]).then_inc(kt_out, 1)
            for n in range(4):
                dve.memset(scores[n][:], 0.0)
            for d in range(2):
                dve.memset(state[:, d, :, chunk_at(d, 0), :], 0.0)
            dve.drain()
            for n in range(steps):
                dve.wait_ge(upd_ps, n + 1)
                for d in range(2):
                    c, nxt = chunk_at(d, n), chunk_at(d, n + 1)
                    for pair in range(PAIRS):
                        last = dve.scalar_tensor_tensor(state[:, d, pair, nxt, :], state[:, d, pair, c, :],
                                                        g.gamma[:, d, pair, c:c + 1], upd[d][n % 2][:, pair, :],
                                                        ALU.mult, ALU.add)
                last.then_inc(upd_done, 1)
                dve.drain()
            def invert(t):
                dve.wait_ge(o_root, t + 1)
                cols = slice(t * GLA_HEADS, (t + 1) * GLA_HEADS)
                dve.reciprocal(g.rstd[:, cols], g.rstd[:, cols]).then_inc(o_rstd, 1)

            for n in range(TT * GLA_HEADS):
                if n > 4 and n % 4 == 3:
                    invert(n // 4 - 1)
                dve.wait_ge(sc_ps, n + 1)
                dve.copy_predicated(scores[n % 4][:], g.mask_f.bitcast(U32), sps[n % 2][:, 0, :])
                dve.drain()
                dve.copy_predicated(scores[n % 4][:], g.mask_b.bitcast(U32), sps[n % 2][:, 1, :]).then_inc(sc_out, 1)
            invert(TT - 1)

        @block.scalar
        def _(act):
            for t in range(TT):
                act.wait_ge(o_ps_done, t + 1)
                for head in range(GLA_HEADS):
                    n = t * GLA_HEADS + head
                    if n:
                        act.wait_ge(o_ssq, n)
                    act.activation(junk[:], ops[t % 2][head % 2][:, head // 2, :], ACT.Square,
                                   accum_out=g.ssq[:, n:n + 1]).then_inc(o_ssq, 1)
                act.wait_ge(o_ssq, (t + 1) * GLA_HEADS)
                cols = slice(t * GLA_HEADS, (t + 1) * GLA_HEADS)
                act.activation(g.rstd[:, cols], g.ssq[:, cols], ACT.Sqrt, scale=1.0 / GLA_DV, bias=g.eps[:]).then_inc(o_root, 1)
                act.wait_ge(o_rstd, t + 1)
                for head in range(GLA_HEADS):
                    n = t * GLA_HEADS + head
                    last = act.activation(g.o[:, t, head * GLA_DV:(head + 1) * GLA_DV], ops[t % 2][head % 2][:, head // 2, :],
                                          ACT.Copy, scale=g.rstd[:, n:n + 1])
                last.then_inc(o_out, 1)


MIX_ORDER = (4, 5, 6, 7, 0, 1, 2, 3)
WO_RING = 4


def mix_out(g):
    nc, i, sem = g.nc, g.i, g.sem
    m_hi, m_lo = g.a_hi, g.a_lo
    mf = [g.at(f"mf{k}", 160 + 4 * k, [P, S]) for k in range(GLA_HEADS)]
    wo_hi = g.at("wo_hi", 52, [P, KC, D], F32R)
    wo_lo = g.at("wo_lo", 84, [P, KC, D], F32R)
    raw, wo_in = g.wo_raw, g.wo_in
    xn = [g.at(f"xn{s}", 4 * s, [P, D]) for s in range(2)]
    xt = [g.at(f"xt{s}", 8 + 4 * s, [P, D]) for s in range(2)]
    junk = g.at("junk_e", 16, [P, D])
    junk_v = g.at("junk_v", 20, [P, D])
    hf = [g.at(f"hf_e{s}", 24 + 4 * s, [P, KC, P]) for s in range(2)]
    retrieval_weights(g)
    xt_in = [sem(f"xt_in{s}") for s in range(2)]
    x1_stored = [sem(f"x1_stored{s}") for s in range(2)]
    wo_hi_ready, wo_lo_ready, ot_ps, mf_ready, m_hi_ready, pooled_lo, heads_lo, mixed = (
        sem(n) for n in ("wo_hi_r", "wo_lo_r", "ot_ps", "mf_ready", "m_hi_r", "pooled_lo", "heads_lo", "mixed"))
    mix_root, x1_ready, x1_root, xn_done, xt_ps, hf_ready, a_hi_ready, a_ready = (sem(n) for n in (
        "mix_root", "x1_ready", "x1_root", "xn_done", "xt_ps", "hf_ready", "a_hi_ready", "a_ready"))
    act_self = sem("act_self_e")
    with ExitStack() as banks:
        otp = [banks.enter_context(nc.psum_tensor(f"otp{n}", [P, KC, P], F32)) for n in range(2)]
        mps = g.mps
        block = banks.enter_context(nc.Block())
        flat = lambda a: a[:].rearrange("p a b -> p (a b)")

        @block.sync
        def _(sp):
            for n in range(WO_RING, KC):
                sp.wait_ge(wo_lo_ready, n - WO_RING + 1)
                sp.dma_start(raw[n % WO_RING][:], i["w_out"][:, MIX_ORDER[n], :]).then_inc(wo_in[n % WO_RING], 16)
            sp.wait_ge(ot_ps, GLA_HEADS)
            for t in range(TT):
                if t >= 2:
                    sp.wait_ge(xn_done, t - 1)
                    sp.wait_ge(x1_stored[t % 2], 16 * (t // 2))
                sp.dma_start(xt[t % 2][:], i["x"][t * P:(t + 1) * P, :]).then_inc(xt_in[t % 2], 16)
                if t == 2:
                    sp.wait_ge(wo_lo_ready, KC)
                    for s in range(2):
                        sp.dma_start(g.wq_raw[s][:], i["w_q"][s]).then_inc(g.wq_in[s], 16)
                if t >= 1:
                    sp.wait_ge(x1_ready, t)
                    sp.dma_start(g.x1_d[t - 1], xt[(t - 1) % 2][:]).then_inc(x1_stored[(t - 1) % 2], 16)
            sp.wait_ge(x1_ready, TT)
            sp.dma_start(g.x1_d[TT - 1], xt[(TT - 1) % 2][:]).then_inc(x1_stored[(TT - 1) % 2], 16)
            for s in range(2):
                sp.wait_ge(x1_stored[s], 16 * TT // 2)

        @block.gpsimd
        def _(pool):
            for n in range(KC - GLA_HEADS):
                k = MIX_ORDER[n]
                pool.wait_ge(m_hi_ready, n + 1)
                split_lo(pool, m_lo[:, k, :], g.z[:, 4 + k, :], m_hi[:, k, :]).then_inc(pooled_lo, 1)

        @block.scalar
        def _(act):
            for n, k in enumerate(MIX_ORDER):
                act.wait_ge(wo_in[n % WO_RING], 16 * (n // WO_RING + 1))
                split_hi(act, wo_hi[:, k, :], raw[n % WO_RING][:]).then_inc(wo_hi_ready, 1)
                if k < GLA_HEADS:
                    act.wait_ge(mf_ready, k + 1)
                split_hi(act, m_hi[:, k, :], mf[k][:] if k < GLA_HEADS else g.z[:, 4 + k, :]).then_inc(m_hi_ready, 1)

            def modulate(t):
                act.wait_ge(xt_ps, t + 1)
                if t >= 2:
                    act.wait_ge(a_ready, t - 1)
                for k in range(KC):
                    last = act.activation(hf[t % 2][:, k, :], otp[t % 2][:, k, :], ACT.Identity,
                                          bias=g.mod[:, 3 * KC + k:3 * KC + k + 1], scale=g.scale2[:, k:k + 1])
                last.then_inc(hf_ready, 1)
                act.wait_ge(hf_ready, t + 1)
                split_hi(act, g.a_hi[:, :, t * P:(t + 1) * P], hf[t % 2][:]).then_inc(a_hi_ready, 1)

            for t in range(TT):
                act.wait_ge(mixed, t + 1)
                act.activation(junk[:], mps[t % 2][:], ACT.Square, accum_out=g.ssq[:, 2 * t:2 * t + 1]).then_inc(act_self, 1)
                act.wait_ge(act_self, 2 * t + 1)
                act.activation(g.rstd[:, 2 * t:2 * t + 1], g.ssq[:, 2 * t:2 * t + 1], ACT.Sqrt, scale=1.0 / D,
                               bias=g.eps[:]).then_inc(mix_root, 1)
                act.wait_ge(x1_ready, t + 1)
                act.activation(junk[:], xt[t % 2][:], ACT.Square, accum_out=g.ssq[:, 2 * t + 1:2 * t + 2]).then_inc(act_self, 1)
                act.wait_ge(act_self, 2 * t + 2)
                act.activation(g.rstd[:, 2 * t + 1:2 * t + 2], g.ssq[:, 2 * t + 1:2 * t + 2], ACT.Sqrt, scale=1.0 / D,
                               bias=g.eps[:]).then_inc(x1_root, 1)
                if t:
                    modulate(t - 1)
                if t in (3, 4):
                    split_query(g, act, t - 3)
            modulate(TT - 1)

        @block.vector
        def _(dve):
            def split_wo(n, k):
                dve.wait_ge(wo_hi_ready, n + 1)
                split_lo(dve, wo_lo[:, k, :], raw[n % WO_RING][:], wo_hi[:, k, :]).then_inc(wo_lo_ready, 1)

            for k in range(GLA_HEADS):
                split_wo(k, MIX_ORDER[k])
                dve.wait_ge(ot_ps, k + 1)
                dve.scalar_tensor_tensor(mf[k][:], flat(otp[k % 2]), g.vec("g_gla_head")[:, k:k + 1], g.z[:, 4 + k, :],
                                         ALU.mult, ALU.mult).then_inc(mf_ready, 1)
            for k in range(GLA_HEADS):
                n = MIX_ORDER.index(k)
                split_wo(n, k)
                dve.wait_ge(m_hi_ready, n + 1)
                split_lo(dve, m_lo[:, k, :], mf[k][:], m_hi[:, k, :]).then_inc(heads_lo, 1)

            def modulated(t):
                dve.wait_ge(a_hi_ready, t + 1)
                cols = slice(t * P, (t + 1) * P)
                split_lo(dve, g.a_lo[:, :, cols], hf[t % 2][:], g.a_hi[:, :, cols]).then_inc(a_ready, 1)

            for t in range(TT):
                dve.wait_ge(mix_root, t + 1)
                dve.reciprocal(g.rstd[:, 2 * t:2 * t + 1], g.rstd[:, 2 * t:2 * t + 1])
                dve.drain()
                dve.scalar_tensor_tensor(junk_v[:], mps[t % 2][:], g.rstd[:, 2 * t:2 * t + 1], g.gate_rows[:, 0, :],
                                         ALU.mult, ALU.mult)
                dve.drain()
                dve.wait_ge(xt_in[t % 2], 16 * (t // 2 + 1))
                dve.tensor_tensor(xt[t % 2][:], xt[t % 2][:], junk_v[:], ALU.add).then_inc(x1_ready, 1)
                dve.wait_ge(x1_root, t + 1)
                dve.reciprocal(g.rstd[:, 2 * t + 1:2 * t + 2], g.rstd[:, 2 * t + 1:2 * t + 2])
                dve.drain()
                if t >= 2:
                    dve.wait_ge(xt_ps, t - 1)
                dve.tensor_scalar(xn[t % 2][:], xt[t % 2][:], g.rstd[:, 2 * t + 1:2 * t + 2], None, ALU.mult)\
                   .then_inc(xn_done, 1)
                if t:
                    modulated(t - 1)
                if t in (3, 4):
                    split_query_lo(g, dve, t - 3)
            modulated(TT - 1)

        @block.tensor
        def _(pe):
            for h in range(GLA_HEADS):
                if h >= 2:
                    pe.wait_ge(mf_ready, h - 1)
                for t in range(TT):
                    last = pe.transpose(otp[h % 2][:, t, :], g.o[:, t, h * GLA_DV:(h + 1) * GLA_DV], g.ident)
                last.then_inc(ot_ps, 1)

            def part(t, k, first, final):
                cols = slice(t * P, (t + 1) * P)
                for m, w, start, stop in ((m_hi, wo_hi, first, False), (m_hi, wo_lo, False, False), (m_lo, wo_hi, False, final)):
                    for half in range(2):
                        out = slice(half * HALF, (half + 1) * HALF)
                        last = pe.matmul(mps[t % 2][:, out], m[:, k, cols], w[:, k, out], start=start, stop=stop)
                return last

            def transpose_xn(t):
                pe.wait_ge(xn_done, t + 1)
                if t >= 2:
                    pe.wait_ge(hf_ready, t - 1)
                else:
                    pe.wait_ge(mf_ready, GLA_HEADS)
                for k in range(KC):
                    last = pe.transpose(otp[t % 2][:, k, :], xn[t % 2][:, k * P:(k + 1) * P], g.ident)
                last.then_inc(xt_ps, 1)

            order = [(n, t) for n in range(KC - 2) for t in range(2)] + [(n, t) for t in range(2) for n in (KC - 2, KC - 1)]
            for n, t in order:
                k = MIX_ORDER[n]
                if t == 0:
                    pe.wait_ge(wo_lo_ready, n + 1)
                    if k < GLA_HEADS:
                        pe.wait_ge(heads_lo, k + 1)
                    else:
                        pe.wait_ge(pooled_lo, n + 1)
                last = part(t, k, n == 0, n == KC - 1)
                if n == KC - 1:
                    last.then_inc(mixed, 1)
            for t in range(2, TT):
                pe.wait_ge(x1_ready, t - 1)
                for n, k in enumerate(MIX_ORDER):
                    last = part(t, k, n == 0, n == KC - 1)
                last.then_inc(mixed, 1)
                transpose_xn(t - 2)
            for n in range(2):
                transpose_xn(TT - 2 + n)
                pe.wait_ge(g.wq_lo_ready, n + 1)
                pe.wait_ge(a_ready, TT // 2)
                pe.wait_ge(x1_ready, TT - 1 + n)
                tile_product(pe, mps[n], g.wq_hi[n], g.wq_lo[n], g.a_hi, g.a_lo, halves=(0,))


def retrieval_weights(g):
    g.wq_raw = [g.at(f"wq_raw{s}", 116 + 4 * s, [P, D]) for s in range(2)]
    g.wq_hi = [g.at(f"wq_hi{s}", 32 + 4 * s, [P, D], F32R) for s in range(2)]
    g.wq_lo = [g.at(f"wq_lo{s}", 40 + 4 * s, [P, D], F32R) for s in range(2)]
    g.wq_in = [g.sem(f"wq_in{s}") for s in range(2)]
    g.wq_hi_ready, g.wq_lo_ready = g.sem("wq_hi_r"), g.sem("wq_lo_r")


def split_query(g, act, s):
    act.wait_ge(g.wq_in[s], 16)
    split_hi(act, g.wq_hi[s][:], g.wq_raw[s][:]).then_inc(g.wq_hi_ready, 1)


def split_query_lo(g, dve, s):
    dve.wait_ge(g.wq_hi_ready, s + 1)
    split_lo(dve, g.wq_lo[s][:], g.wq_raw[s][:], g.wq_hi[s][:]).then_inc(g.wq_lo_ready, 1)


def topk_buffers(g):
    g.s_work = g.at("s_work", 96, [P, 2, NKEYS])
    g.s_rest = g.at("s_rest", 97, [P, 2, NKEYS])
    g.cand = g.at("cand", 98, [P, TOPK, TOPK])
    g.cand_rest = g.at("cand_rest", 99, [P, TOPK, TOPK])
    g.match = g.at("match", 100, [P, 2, TOPK, TOPK])
    g.chosen = g.at("chosen", 102, [P, 2, HEADS, TOPK])
    g.top_all = g.at("top_all", 103, [P, HEADS, TOPK])
    g.vals = g.at("vals", 103.5, [P, 2, TOPK])
    g.tops = g.at("tops", 103.625, [P, TOPK])
    g.idx = g.at("idx", 103.6875, [P, 2, TOPK], U32)
    g.pos = g.at("pos", 103.8125, [P, TOPK], U32)
    g.hilo = g.at("hilo", 103.875, [P, 2, TOPK], U32)
    g.gates = g.at("gates", 192, [P, HEADS, TOPK])
    g.norm = g.at("norm", 192.5, [P, HEADS])
    g.gate_hi = g.at("gate_hi", 194.75, [P, P], F32R)
    g.slots = g.at("slots", 192.75, [P, 4, P])


def topk_head(g, dve, h, topk_done):
    flat = lambda a: a.rearrange("p a b -> p (a b)")
    for p in range(2):
        dve.max(g.vals[:, p, 0:8], g.s_work[:, p, :])
    dve.drain()
    for p in range(2):
        dve.max_index(g.idx[:, p, 0:8], g.vals[:, p, 0:8], g.s_work[:, p, :])
        dve.match_replace(g.s_rest[:, p, :], g.vals[:, p, 0:8], g.s_work[:, p, :], LOWEST)
    dve.drain()
    for p in range(2):
        dve.max(g.vals[:, p, 8:16], g.s_rest[:, p, :])
    dve.drain()
    for p in range(2):
        dve.max_index(g.idx[:, p, 8:16], g.vals[:, p, 8:16], g.s_rest[:, p, :])
    dve.tensor_tensor(g.cand[:], g.vals[:, 0, :].unsqueeze(2).to_broadcast([P, TOPK, TOPK]),
                      g.vals[:, 1, :].unsqueeze(1).to_broadcast([P, TOPK, TOPK]), ALU.add)
    dve.drain()
    cand, rest = flat(g.cand[:]), flat(g.cand_rest[:])
    dve.max(g.tops[:, 0:8], cand)
    dve.drain()
    dve.max_index(g.pos[:, 0:8], g.tops[:, 0:8], cand)
    dve.match_replace(rest, g.tops[:, 0:8], cand, LOWEST)
    dve.drain()
    dve.max(g.tops[:, 8:16], rest)
    dve.drain()
    dve.max_index(g.pos[:, 8:16], g.tops[:, 8:16], rest)
    dve.tensor_copy(g.top_all[:, bass.ds(h, 1), :], g.tops[:].unsqueeze(1))
    dve.drain()
    dve.tensor_scalar(g.hilo[:, 0, :], g.pos[:], 4, None, ALU.logical_shift_right)
    dve.tensor_scalar(g.hilo[:, 1, :], g.pos[:], TOPK - 1, None, ALU.bitwise_and)
    dve.drain()
    full = [P, 2, TOPK, TOPK]
    dve.tensor_tensor(g.match[:], g.hilo[:].unsqueeze(3).to_broadcast(full),
                      g.iota[:, 0:TOPK].unsqueeze(1).unsqueeze(1).to_broadcast(full), ALU.is_equal)
    dve.drain()
    dve.tensor_tensor(g.match[:], g.match[:], g.idx[:].unsqueeze(2).to_broadcast(full), ALU.mult)
    dve.drain()
    dve.tensor_reduce(g.chosen[:, :, bass.ds(h, 1), :].rearrange("p a b c -> p a (b c)") if isinstance(h, int) else
                      g.chosen[:, :, bass.ds(h, 1), :], g.match[:], AX, ALU.add).then_inc(topk_done, 1)


def finish_topk(g, dve, n, shifted, exps, slots_ready):
    dve.drain()
    dve.tensor_tensor(g.gates[:], g.top_all[:], g.top_all[:, :, 0:1].to_broadcast([P, HEADS, TOPK]), ALU.subtract)\
       .then_inc(shifted, 1)
    dve.wait_ge(exps, n + 1)
    dve.tensor_reduce(g.norm[:], g.gates[:], AX, ALU.add)
    dve.drain()
    dve.reciprocal(g.norm[:], g.norm[:])
    dve.drain()
    dve.tensor_tensor(g.gates[:], g.gates[:], g.norm[:].unsqueeze(2).to_broadcast([P, HEADS, TOPK]), ALU.mult)\
       .then_inc(slots_ready, 1)


def retrieval_scores(g):
    nc, i, sem = g.nc, g.i, g.sem
    raw, w_hi, w_lo, raw_in, hi_ready, lo_ready = g.wq_raw, g.wq_hi, g.wq_lo, g.wq_in, g.wq_hi_ready, g.wq_lo_ready
    q = [g.at(f"q{s}", 4 * s, [P, S]) for s in range(2)]
    keys = g.at("keys", 8, [P, QTILES, NKEYS])
    stage = [g.at(f"stage{s}", 16 + 4 * s, [P, TT, NKEYS]) for s in range(2)]
    topk_buffers(g)
    keys_in = sem("keys_in")
    s_stored = g.s_stored = [sem(f"s_stored{s}") for s in range(2)]
    q_done, q_out, s_done, s_out, stage_free = (sem(n) for n in (
        "q_done", "q_out", "s_done", "s_out", "stage_free"))
    topk_done = g.topk_first = sem("topk_first")
    g.u_raw = [g.at(f"u_raw{s}", 24 + 4 * s, [P, D]) for s in range(2)]
    g.u_hi = [g.at(f"u_hi{s}", 104 + 4 * s, [P, D], F32R) for s in range(2)]
    g.u_lo = [g.at(f"u_lo{s}", 112 + 4 * s, [P, D], F32R) for s in range(2)]
    g.u_in = [sem(f"u_in{s}") for s in range(2)]
    g.u_hi_ready, g.u_lo_ready = sem("u_hi_r"), sem("u_lo_r")
    g.shifted, g.exps, g.slots_ready = sem("shifted"), sem("exps"), sem("slots_ready")
    s_view = g.s_d.rearrange("(t h) p m n -> p t h m n", h=HEADS)
    with ExitStack() as banks:
        acc = g.mps
        sps = [banks.enter_context(nc.psum_tensor(f"s_ps{n}", [P, TT, NKEYS], F32)) for n in range(2)]
        block = banks.enter_context(nc.Block())

        @block.sync
        def _(sp):
            sp.dma_start(keys[:], i["keys"]).then_inc(keys_in, 16)
            for s in range(2):
                sp.dma_start(g.u_raw[s][:], i["u"][s]).then_inc(g.u_in[s], 16)
            sp.sem_inc(stage_free, 2)

            def store(r):
                for s in range(2):
                    sp.wait_ge(s_out, 2 * r + s + 1)
                    sp.dma_start(s_view[:, :, bass.ds(r, 1), s, :], stage[s][:].unsqueeze(2)).then_inc(s_stored[s], 16)
                if not isinstance(r, int):
                    for s in range(2):
                        sp.wait_ge(s_stored[s], (r + 1) * 16)
                        sp.sem_inc(stage_free, 1)

            with sp.Fori(0, HEADS - 1) as r:
                for s in range(2):
                    sp.wait_ge(lo_ready, 2 * r + s + 1)
                    sp.dma_start(raw[s][:], i["w_q"][2 * (r + 1) + s]).then_inc(raw_in[s], 16)
                store(r)
            store(HEADS - 1)

        @block.scalar
        def _(act):
            def split(s, count):
                act.wait_ge(raw_in[s], count)
                split_hi(act, w_hi[s][:], raw[s][:]).then_inc(hi_ready, 1)

            def evacuate(n, s):
                act.wait_ge(q_done, n + 1)
                act.activation(q[s][:], acc[s][:], ACT.Copy).then_inc(q_out, 1)

            with act.Fori(0, HEADS - 1) as r:
                for s in range(2):
                    evacuate(2 * r + s, s)
                    split(s, (r + 2) * 16)
            evacuate(QTILES - 2, 0)
            for s in range(2):
                act.wait_ge(g.u_in[s], 16)
                split_hi(act, g.u_hi[s][:], g.u_raw[s][:]).then_inc(g.u_hi_ready, 1)
            evacuate(QTILES - 1, 1)

        @block.vector
        def _(dve):
            def split(n, s):
                dve.wait_ge(hi_ready, n + 1)
                split_lo(dve, w_lo[s][:], raw[s][:], w_hi[s][:]).then_inc(lo_ready, 1)

            def scores_out(n, s):
                dve.wait_ge(s_done, n + 1)
                dve.wait_ge(stage_free, n + 1)
                dve.tensor_copy(g.s_work[:, s, :], sps[s][:, 0, :])
                dve.tensor_copy(stage[s][:], sps[s][:]).then_inc(s_out, 1)

            with dve.Fori(0, HEADS - 1) as r:
                for s in range(2):
                    split(2 * (r + 1) + s, s)
                    scores_out(2 * r + s, s)
                dve.drain()
                topk_head(g, dve, r, topk_done)
            for s in range(2):
                dve.wait_ge(g.u_hi_ready, s + 1)
                split_lo(dve, g.u_lo[s][:], g.u_raw[s][:], g.u_hi[s][:]).then_inc(g.u_lo_ready, 1)
            for s in range(2):
                scores_out(QTILES - 2 + s, s)

        @block.tensor
        def _(pe):
            def product(n, s, halves=(0, 1)):
                pe.wait_ge(lo_ready, n + 1)
                tile_product(pe, acc[s], w_hi[s], w_lo[s], g.a_hi, g.a_lo, halves).then_inc(q_done, 1)

            def score(n, s):
                pe.wait_ge(q_out, n + 1)
                for t in range(TT):
                    last = pe.matmul(sps[s][:, t, :], q[s][:, t * P:(t + 1) * P], keys[:, bass.ds(n, 1), :],
                                     start=True, stop=True)
                last.then_inc(s_done, 1)

            for s in range(2):
                product(s, s, halves=(1,))
            pe.wait_ge(keys_in, 16)
            score(0, 0)
            product(2, 0)
            score(1, 1)
            with pe.Fori(1, HEADS - 1) as r:
                for s in range(2):
                    product(2 * r + s + 1, 1 - s)
                    score(2 * r + s, s)
            product(QTILES - 1, 1)
            score(QTILES - 2, 0)
            pe.wait_ge(s_out, QTILES - 2)
            score(QTILES - 1, 1)


ROUNDS = S // HALF
RT = TT // ROUNDS
RING = 4
GROUP = 4
UNROLL = 2 * GROUP


def sweep_2_loads(g):
    g.gt = [g.at(f"gt{s}", 32 + 8 * s, [P, HALF // GTOK, GROUP, GTOK]) for s in range(2)]
    g.act_in = [g.at(f"at{s}", 48 + 2 * s, [P, HALF]) for s in range(RING)]
    g.v_raw = [g.at(f"v_raw{s}", (56, 60, 96, 100)[s], [P, D]) for s in range(RING)]
    g.v_in, g.act_in_sem = ([g.sem(f"{n}{s}") for s in range(RING)] for n in ("v_in", "at_in"))
    g.gt_in = [g.sem(f"gt_in{s}") for s in range(2)]


def load_expert(g, sp, r, n, s):
    if s % GROUP == 0:
        per = HALF // GTOK
        gates = g.gate_d[r * per:(r + 1) * per, :, bass.ds(n, GROUP), :]
        sp.dma_start(g.gt[s // GROUP][:], gates.rearrange("j p n t -> p j n t")).then_inc(g.gt_in[s // GROUP], 16)
    sp.dma_start(g.act_in[s % RING][:], g.act_d[n][:, r * HALF:(r + 1) * HALF]).then_inc(g.act_in_sem[s % RING], 16)
    sp.dma_start(g.v_raw[s % RING][:], g.i["v"][n]).then_inc(g.v_in[s % RING], 16)


def expert_sweep_1(g):
    nc, i, sem = g.nc, g.i, g.sem
    raw, w_hi, w_lo, raw_in, hi_ready, lo_ready = g.u_raw, g.u_hi, g.u_lo, g.u_in, g.u_hi_ready, g.u_lo_ready
    gelu = [g.at(f"gelu{s}", 120 + 4 * s, [P, S]) for s in range(2)]
    gate_block = [g.at(f"gate_block{s}", 32 + 32 * s, [P, NKEYS, GTOK]) for s in range(2)]
    onehot_1 = [g.at(f"onehot_1{u}", 12 * u, [P, TOK // 2, NKEYS], F32R) for u in range(2)]
    onehot_2 = [g.at(f"onehot_2{u}", 4 + 12 * u, [P, TOK // 2, 2, NKEYS], F32R) for u in range(2)]
    act_stored = [sem(f"act_stored{s}") for s in range(2)]
    g.gate_block_last = gate_block[1]
    sweep_2_loads(g)
    s_in = sem("s_in")
    gate_stored = g.gate_stored = [sem(f"gate_stored{s}") for s in range(2)]
    tile_done, gelu_done, gelu_free = (sem(n) for n in ("u_done", "gelu_done", "gelu_free"))
    high_out = sem("high_out")
    topk_done, slots_ps, slots_out, eq_ready, onehot_ready, gate_ps, gate_out = (
        sem(n) for n in ("topk_done", "slots_ps", "slots_out", "eq_ready", "onehot_ready", "gate_ps", "gate_out"))
    BANKS = 4
    PER = TOK // 2 // BANKS
    BANK_ORDER = [*range(1, BANKS), 0]
    with ExitStack() as banks:
        acc = [banks.enter_context(nc.psum_tensor(f"acc_u{n}", [P, S], F32)) for n in range(2)]
        gps_all = banks.enter_context(nc.psum_tensor("gate_ps", [P, TOK // 2, 2, NKEYS], F32))
        gps = [gps_all[:, n * PER:(n + 1) * PER] for n in range(BANKS)]
        block = banks.enter_context(nc.Block())

        def gate_columns(h, half, u):
            first = (h - half * BLOCK_STEPS) * TOK + u * TOK // 2
            return gate_block[half][:, :, bass.ds(first, TOK // 2)].rearrange("p n t -> p t n")

        def run(eng, step, after_block=lambda j, half: None, peel=1, opening=False):
            def tile(j, topk, load_last, opening=0):
                if opening:
                    step(0, 0, 0, 0, topk, True, False, True)
                for half in range(2):
                    peeled = half
                    with eng.Fori(half * BLOCK_STEPS + (0 if half else opening), (half + 1) * BLOCK_STEPS - peeled) as h:
                        step(j, h, half, j * HEADS + h, topk, True, False)
                    if peeled:
                        step(j, HEADS - 1, half, j * HEADS + HEADS - 1, topk, load_last, topk)
                    after_block(j, half)

            if opening:
                tile(0, True, True, 1)
            with eng.Fori(1 if opening else 0, TT - peel) as j:
                tile(j, True, True)
            for j in range(TT - peel, TT):
                tile(j, j < TT - 1, j < TT - 1)

        @block.sync
        def _(sp):
            sp.sem_inc(gelu_free, 2)
            for s in range(2):
                sp.sem_inc(gate_stored[s], 16)

            for s in range(2):
                sp.wait_ge(g.s_stored[s], HEADS * 16)
            sp.wait_ge(g.topk_first, HEADS)
            sp.dma_start(g.s_work[:], g.s_d[HEADS]).then_inc(s_in, 16)

            def step(j, h, half, b, topk, more, switch, opening=False):
                if more:
                    for s in range(2):
                        sp.wait_ge(lo_ready, 2 * b + s + 1)
                        sp.dma_start(raw[s][:], i["u"][2 * (b + 1) + s]).then_inc(raw_in[s], 16)
                else:
                    sp.wait_ge(gate_stored[0], (TT + 1) * 16)
                    for n in range(RING):
                        load_expert(g, sp, 0, n, n)
                for s in range(2):
                    sp.wait_ge(gelu_done, 2 * b + s + 1)
                    sp.dma_start(g.act_d[2 * b + s], gelu[s][:]).then_inc(act_stored[s], 16)
                    if topk and s == 0 and not (switch and isinstance(j, int)):
                        sp.wait_ge(topk_done, b + 1)
                        sp.dma_start(g.s_work[:], g.s_d[b + HEADS + 1]).then_inc(s_in, 16)
                for s in range(2):
                    sp.wait_ge(act_stored[s], (b + 1) * 16)
                    sp.sem_inc(gelu_free, 1)

            def after_block(j, half):
                if not (isinstance(j, int) and j == TT - 1 and half):
                    sp.wait_ge(gate_out, 2 * (j * HEADS + (half + 1) * BLOCK_STEPS) + 1)
                    sp.dma_start(g.gate_d[2 * j + half], gate_block[half][:]).then_inc(gate_stored[half], 16)

            run(sp, step, after_block, peel=2)

        @block.gpsimd
        def _(pool):
            def step(j, h, half, b, topk, more, switch, opening=False):
                for u in range(2):
                    pool.wait_ge(eq_ready, 2 * b + u + 1)
                    for part in (1, 0):
                        gate = g.slots[:, 2 + part, bass.ds(h * TOK + u * TOK // 2, TOK // 2)]
                        last = pool.tensor_tensor(onehot_2[u][:, :, part, :], onehot_2[u][:, :, 0, :].bitcast(F32),
                                                  gate.unsqueeze(2).to_broadcast([P, TOK // 2, NKEYS]), ALU.mult)
                    last.then_inc(onehot_ready, 1)

            run(pool, step)

        @block.scalar
        def _(act):
            def split(s, count):
                act.wait_ge(raw_in[s], count)
                split_hi(act, w_hi[s][:], raw[s][:]).then_inc(hi_ready, 1)

            act.wait_ge(g.shifted, 1)
            act.activation(g.gates[:], g.gates[:], ACT.Exp).then_inc(g.exps, 1)

            def step(j, h, half, b, topk, more, switch, opening=False):
                for s in range(2):
                    act.wait_ge(tile_done, 2 * b + s + 1)
                    act.wait_ge(gelu_free, 2 * b + s + 1)
                    act.activation(gelu[s][:], acc[s][:], ACT.Gelu).then_inc(gelu_done, 1)
                    if s == 0:
                        act.wait_ge(gate_stored[half], (j + 1) * 16)
                    act.wait_ge(gate_ps, 2 * BANKS * (b + 1) + (s + 1) * BANKS)
                    act.activation(gate_columns(h, half, s), gps_all[:, :, 0, :], ACT.Copy).then_inc(high_out, 1)
                    if more:
                        split(s, (b + 2) * 16)
                    if switch and s == 0:
                        act.wait_ge(g.shifted, j + 2)
                        act.activation(g.gates[:], g.gates[:], ACT.Exp).then_inc(g.exps, 1)

            run(act, step)

        @block.vector
        def _(dve):
            def split(n, s):
                dve.wait_ge(hi_ready, n + 1)
                split_lo(dve, w_lo[s][:], raw[s][:], w_hi[s][:]).then_inc(lo_ready, 1)

            def take_slots(turn):
                dve.wait_ge(slots_ps, turn)
                dve.tensor_copy(g.slots[:, 0:2, :], gps[0][:, 0, :, :])
                dve.tensor_copy(g.slots[:, 3, :], gps[0][:, 1, 0, :]).then_inc(slots_out, 1)
                dve.drain()
                dve.tensor_copy(g.gate_hi[:], g.slots[:, 3, :])
                dve.drain()
                dve.tensor_tensor(g.slots[:, 3, :], g.slots[:, 3, :], g.gate_hi[:].bitcast(F32), ALU.subtract)
                dve.tensor_copy(g.slots[:, 2, :], g.gate_hi[:].bitcast(F32))
                dve.drain()

            dve.sem_inc(gate_out, 1)
            topk_head(g, dve, HEADS - 1, g.topk_first)
            finish_topk(g, dve, 0, g.shifted, g.exps, g.slots_ready)
            take_slots(1)

            def compare(b, first, u):
                dve.wait_ge(gate_ps, 2 * BANKS * b + (u + 1) * BANKS)
                for n, rows in enumerate((onehot_1[u][:], onehot_2[u][:, :, 0, :])):
                    chosen = g.slots[:, n, bass.ds(first + u * TOK // 2, TOK // 2)]
                    last = dve.tensor_tensor(rows, g.iota.unsqueeze(1).to_broadcast([P, TOK // 2, NKEYS]),
                                             chosen.unsqueeze(2).to_broadcast([P, TOK // 2, NKEYS]), ALU.is_equal)
                last.then_inc(eq_ready, 1)

            dve.wait_ge(s_in, 16)
            compare(0, 0, 0)

            def step(j, h, half, b, topk, more, switch, opening=False):
                def gates_out(u):
                    dve.wait_ge(high_out, 2 * b + u + 1)
                    dst = gate_columns(h, half, u)
                    dve.tensor_tensor(dst, dst, gps_all[:, :, 1, :], ALU.add).then_inc(gate_out, 1)

                compare(b, h * TOK, 1)
                if topk:
                    topk_head(g, dve, h, topk_done)
                if switch:
                    finish_topk(g, dve, j + 1, g.shifted, g.exps, g.slots_ready)
                gates_out(0)
                if more:
                    split(2 * (b + 1), 0)
                if switch:
                    dve.wait_ge(onehot_ready, 2 * b + 2)
                    take_slots(j + 2)
                if more:
                    if topk and not (switch and isinstance(j, int)):
                        dve.wait_ge(s_in, (b + 2) * 16)
                    compare(b + 1, 0 if switch else (h + 1) * TOK, 0)
                gates_out(1)
                if more:
                    split(2 * (b + 1) + 1, 1)

            run(dve, step, peel=2)

        @block.tensor
        def _(pe):
            flat = lambda a: a.rearrange("p a b -> p (a b)")

            def transpose_slots():
                for n, src in enumerate((flat(g.chosen[:, 0]), flat(g.chosen[:, 1]), flat(g.gates[:]))):
                    last = pe.transpose(gps[0][:, n // 2, n % 2, :], src, g.ident)
                last.then_inc(slots_ps, 1)

            pe.sem_inc(gate_ps, 2 * BANKS)
            def step(j, h, half, b, topk, more, switch, opening=False):
                def product(s):
                    pe.wait_ge(lo_ready, 2 * b + s + 1)
                    tile_product(pe, acc[s], w_hi[s], w_lo[s], g.a_hi, g.a_lo).then_inc(tile_done, 1)

                def gates(s):
                    pe.wait_ge(gate_out, 2 * b + s + 1)
                    if switch and s:
                        pe.wait_ge(g.slots_ready, j + 2)
                        transpose_slots()
                    pe.wait_ge(onehot_ready, 2 * b + s + 1)
                    for n in BANK_ORDER:
                        if n == 0:
                            pe.wait_ge(slots_out, j + (2 if switch and s else 1))
                        for t in range(n * PER, (n + 1) * PER):
                            last = pe.matmul(gps[n][:, t % PER], onehot_1[s][:, t, :], onehot_2[s][:, t], start=True, stop=True)
                        last.then_inc(gate_ps, 1)

                product(0)
                if opening:
                    pe.wait_ge(gate_out, 1)
                    pe.wait_ge(g.slots_ready, 1)
                    transpose_slots()
                    product(1)
                    gates(0)
                else:
                    gates(0)
                    product(1)
                gates(1)

            run(pe, step, opening=True)


def expert_sweep_2(g):
    nc, sem = g.nc, g.sem
    N = NKEYS
    v_raw, gt, at, v_in, gt_in, at_in = g.v_raw, g.gt, g.act_in, g.v_in, g.gt_in, g.act_in_sem
    v_hi = [g.at(f"v_hi{s}", 4 * s, [P, D], F32R) for s in range(2)]
    v_lo = [g.at(f"v_lo{s}", 8 + 4 * s, [P, D], F32R) for s in range(2)]
    c_lo = [g.at(f"c_lo{s}", 16 + 2 * s, [P, HALF], F32R) for s in range(2)]
    junk = g.at("junk_y", 20, [P, D])
    cf = [g.at(f"cf{s}", 104 + 2 * s, [P, HALF]) for s in range(2)]
    c_hi = [g.at(f"c_hi{s}", 108 + 2 * s, [P, HALF], F32R) for s in range(2)]
    gate_block = g.gate_block_last
    y = g.at("y", 64, [P, RT, D])
    x1 = g.at("x1", 128, [P, TT, D])
    vhi_r, vlo_r, cf_r, chi_r, clo_r, used, tile_summed, y_out = (sem(n) for n in (
        "vhi_r", "vlo_r", "cf_r", "chi_r", "clo_r", "used", "tile_summed", "y_out"))
    x1_in, y_ssq, y_root, y_scaled, out_ready = (sem(n) for n in ("x1_in", "y_ssq", "y_root", "y_scaled", "out_ready"))
    out_stored, out_ready_dve, out_stored_sp = sem("out_stored"), sem("out_ready_dve"), sem("out_stored_sp")
    by_pool = lambda r, t: r < ROUNDS - 1 or t % 2 == 0
    with ExitStack() as banks:
        yps = [banks.enter_context(nc.psum_tensor(f"y_ps{n}", [P, D], F32)) for n in range(RT)]
        block = banks.enter_context(nc.Block())

        @block.sync
        def _(sp):
            def refill(r, n, s):
                m = r * N + n
                sp.wait_ge(cf_r, m - RING + 1)
                sp.wait_ge(vlo_r, m - RING + 1)
                load_expert(g, sp, r, n, s)

            for n in range(RING, UNROLL):
                sp.wait_ge(vlo_r, n - RING + 1)
                load_expert(g, sp, 0, n, n)
            sp.dma_start(g.gate_d[S // GTOK - 1], gate_block[:]).then_inc(g.gate_stored[1], 16)
            for r in range(ROUNDS):
                for part in range(2):
                    with sp.Fori(part * N // UNROLL // 2 if r or part else 1, (part + 1) * N // UNROLL // 2) as q:
                        for s in range(UNROLL):
                            refill(r, UNROLL * q + s, s)
                    if r == 0 and part == 0:
                        sp.dma_start(x1[:], g.x1_d.rearrange("t p d -> p t d")).then_inc(x1_in, 16)
                if r == 0:
                    sp.wait_ge(g.gate_stored[1], (TT + 1) * 16)
            for m, t in enumerate(range(1, RT, 2)):
                sp.wait_ge(out_ready_dve, m + 1)
                n = (ROUNDS - 1) * RT + t
                sp.dma_start(g.out[n * P:(n + 1) * P, :], y[:, t, :]).then_inc(out_stored_sp, 16)
            sp.wait_ge(out_stored_sp, RT // 2 * 16)

        @block.gpsimd
        def _(pool):
            pool.wait_ge(x1_in, 16)
            done = 0
            for r in range(ROUNDS):
                for t in range(RT):
                    if by_pool(r, t):
                        n = r * RT + t
                        pool.wait_ge(y_scaled, n + 1)
                        pool.tensor_tensor(y[:, t, :], y[:, t, :], x1[:, n, :], ALU.add).then_inc(out_ready, 1)
                        done += 1
                        pool.wait_ge(out_ready, done)
                        pool.dma_start(g.out[n * P:(n + 1) * P, :], y[:, t, :]).then_inc(out_stored, 16)
            pool.wait_ge(out_stored, done * 16)

        @block.scalar
        def _(act):
            def prepare(m, s, turn, free=True):
                act.wait_ge(v_in[s % RING], turn * 16)
                if free:
                    act.wait_ge(used, m - 1)
                split_hi(act, v_hi[s % 2][:], v_raw[s % RING][:]).then_inc(vhi_r, 1)
                act.wait_ge(cf_r, m + 1)
                split_hi(act, c_hi[s % 2][:], cf[s % 2][:]).then_inc(chi_r, 1)

            def finish(r, t):
                n = r * RT + t
                act.wait_ge(tile_summed, n + 1)
                if t == 0:
                    act.wait_ge(g.gate_stored[1], (TT + 1) * 16)
                if r < ROUNDS - 1:
                    act.activation(y[:, t, :], yps[t][:], ACT.Copy).then_inc(y_out, 1)
                if n:
                    act.wait_ge(y_ssq, n)
                act.activation(junk[:], yps[t][:], ACT.Square, accum_out=g.ssq[:, n:n + 1]).then_inc(y_ssq, 1)
                act.wait_ge(y_ssq, n + 1)
                act.activation(g.rstd[:, n:n + 1], g.ssq[:, n:n + 1], ACT.Sqrt, scale=1.0 / D, bias=g.eps[:]).then_inc(y_root, 1)

            for r in range(ROUNDS):
                base = r * N
                for n in range(UNROLL):
                    prepare(base + n, n, base // RING + n // RING + 1, base + n >= 2)
                    if r and n == 0:
                        for t in range(RT):
                            finish(r - 1, t)
                with act.Fori(1, N // UNROLL) as q:
                    for s in range(UNROLL):
                        prepare(base + UNROLL * q + s, s, base // RING + q * (UNROLL // RING) + s // RING + 1)
            for t in range(RT):
                finish(ROUNDS - 1, t)

        @block.vector
        def _(dve):
            def prepare(m, s, turn, gate_turn):
                if s % GROUP == 0:
                    dve.wait_ge(gt_in[s // GROUP], gate_turn * 16)
                dve.wait_ge(at_in[s % RING], turn * 16)
                gates = gt[s // GROUP][:, :, s % GROUP, :]
                dve.tensor_tensor(cf[s % 2][:].rearrange("p (j t) -> p j t", t=GTOK), gates,
                                  at[s % RING][:].rearrange("p (j t) -> p j t", t=GTOK), ALU.mult).then_inc(cf_r, 1)
                dve.wait_ge(vhi_r, m + 1)
                split_lo(dve, v_lo[s % 2][:], v_raw[s % RING][:], v_hi[s % 2][:]).then_inc(vlo_r, 1)
                dve.wait_ge(chi_r, m + 1)
                split_lo(dve, c_lo[s % 2][:], cf[s % 2][:], c_hi[s % 2][:]).then_inc(clo_r, 1)

            def finish(r, t):
                n = r * RT + t
                dve.wait_ge(y_root, n + 1)
                dve.reciprocal(g.rstd[:, n:n + 1], g.rstd[:, n:n + 1])
                dve.drain()
                if r == ROUNDS - 1 and t == 0:
                    dve.wait_ge(out_stored, r * RT * 16)
                sums = y[:, t, :] if r < ROUNDS - 1 else yps[t][:]
                dve.scalar_tensor_tensor(y[:, t, :], sums, g.rstd[:, n:n + 1], g.gate_rows[:, 1, :],
                                         ALU.mult, ALU.mult).then_inc(y_scaled, 1)
                if not by_pool(r, t):
                    dve.wait_ge(y_scaled, n + 1)
                    dve.wait_ge(x1_in, 16)
                    dve.tensor_tensor(y[:, t, :], y[:, t, :], x1[:, n, :], ALU.add).then_inc(out_ready_dve, 1)

            for r in range(ROUNDS):
                base = r * N
                for n in range(UNROLL):
                    prepare(base + n, n, base // RING + n // RING + 1, base // UNROLL + 1)
                    if r and n >= 2 and n - 2 < RT:
                        finish(r - 1, n - 2)
                with dve.Fori(1, N // UNROLL) as q:
                    for s in range(UNROLL):
                        prepare(base + UNROLL * q + s, s, base // RING + q * (UNROLL // RING) + s // RING + 1,
                                base // UNROLL + q + 1)
            for t in range(RT):
                finish(ROUNDS - 1, t)

        @block.tensor
        def _(pe):
            def product(r, n, s, first=False, last=False):
                m = r * N + n
                pe.wait_ge(vlo_r, m + 1)
                pe.wait_ge(clo_r, m + 1)
                for t in range(RT):
                    if first and r:
                        pe.wait_ge(y_ssq, (r - 1) * RT + t + 1)
                    ch, cl = c_hi[s][:, t * P:(t + 1) * P], c_lo[s][:, t * P:(t + 1) * P]
                    for k, (c, v) in enumerate(((ch, v_hi), (ch, v_lo), (cl, v_hi))):
                        for half in range(2):
                            cols = slice(half * HALF, (half + 1) * HALF)
                            done = pe.matmul(yps[t][:, cols], c, v[s][:, cols], start=first and k == 0, stop=last and k == 2)
                    if last:
                        done.then_inc(tile_summed, 1)
                if last:
                    pe.wait_ge(tile_summed, (r + 1) * RT)
                    pe.sem_inc(used, 1)
                else:
                    done.then_inc(used, 1)

            for r in range(ROUNDS):
                for n in range(UNROLL):
                    product(r, n, n % 2, first=n == 0)
                with pe.Fori(1, N // UNROLL - 1) as q:
                    for s in range(UNROLL):
                        product(r, UNROLL * q + s, s % 2)
                for s in range(UNROLL):
                    product(r, N - UNROLL + s, s % 2, last=s == UNROLL - 1)


def lay_out(a):
    f = np.ascontiguousarray
    one = {k: np.asarray(v)[0] for k, v in a.items() if k not in ("x", "c")}
    cols = lambda v: np.asarray(v).reshape(-1, P).T
    tiles = lambda w, n: f(w.reshape(KC, P, n, P).transpose(2, 1, 0, 3).reshape(n, P, KC * P))
    rows = lambda w: f(w.reshape(-1, P, w.shape[1]).transpose(1, 0, 2))
    w_in = one["w_in"]
    kw, vw = GLA_HEADS * GLA_DK, GLA_HEADS * GLA_DV
    at = np.cumsum([0, kw, kw, vw, vw, RANK, RANK, D - vw])
    q, k, v, r, af, ab, p = (w_in[:, at[n]:at[n + 1]] for n in range(7))
    rank = np.zeros((D, P), np.float32)
    rank[:, 0:RANK], rank[:, 64:64 + RANK] = af, ab
    w_alpha = np.zeros((P, kw), np.float32)
    w_alpha[0:RANK], w_alpha[64:64 + RANK] = one["w_alpha_f"], one["w_alpha_b"]
    j, t = np.meshgrid(np.arange(P), np.arange(P), indexing="ij")
    same = j // CHUNK == t // CHUNK
    consts = np.concatenate([np.eye(P), np.broadcast_to(np.arange(P), (P, P)), same & (j <= t), same & (j > t)], 1)
    reset = np.broadcast_to((np.arange(S) % CHUNK != 0), (P, S))
    pos = np.r_[0:PAD, S - PAD:S]
    edges = np.stack([1.0 / (np.clip(pos + w // 2, 0, S) - np.clip(pos - w // 2, 0, S)) for w in WINDOWS])
    return {
        "x": f(np.asarray(a["x"])[0]),
        "vecs": f(np.concatenate([cols(one[n]) for n, _ in VECS], 1)),
        "consts": f(consts.astype(np.float32)),
        "reset": f(reset.astype(np.float32)),
        "edges": f(np.broadcast_to(edges.astype(np.float32), (P, len(WINDOWS), 2 * PAD))),
        "c": f(np.asarray(a["c"])),
        "w_mod": f(one["w_mod"].T.reshape(MOD_TILES, P, D)),
        "w_qkrp": tiles(np.concatenate([q, k, r, p], 1), QKRP),
        "w_rank": tiles(rank, 1)[0],
        "w_v": f(v.reshape(4, 2, P, vw).transpose(0, 2, 1, 3).reshape(4, P, 2 * vw)),
        "w_alpha": w_alpha,
        "w_pool": f(one["w_pool"].transpose(1, 0, 2)),
        "w_out": rows(one["w_out"]),
        "w_q": tiles(one["w_peer_q"], QTILES),
        "keys": f(one["peer_sub_keys"].reshape(QTILES, NKEYS, P).transpose(2, 0, 1)),
        "u": f(one["peer_u"].reshape(NKEYS, NKEYS, KC, P).transpose(1, 3, 2, 0).reshape(NKEYS, P, KC * P)),
        "v": f(one["peer_v"].reshape(NKEYS, NKEYS, D).transpose(1, 0, 2)),
    }


def kernel(**inputs):
    import concourse.bacc as bacc
    from concourse.bass_utils import run_bass_kernel_spmd

    nc = bacc.Bacc("TRN2", target_bir_lowering=False, num_devices=1)
    arrays = {f"in_{n}": a for n, a in lay_out(inputs).items()}
    t_in = {n[3:]: nc.dram_tensor(n, a.shape, F32, kind="ExternalInput").ap() for n, a in arrays.items()}
    out = nc.dram_tensor("out", (S, D), F32, kind="ExternalOutput").ap()
    layer(nc, t_in, out)
    r = run_bass_kernel_spmd(nc, [arrays], core_ids=[0])
    return r.results[0]["out"].reshape(1, S, D)
```
